# Optimizing a Trainium2 kernel written in Bass

```python
import math
import jax, jax.numpy as jnp
from jax import lax
import numpy as np

D_MODEL = 1024
BATCH = 1
SEQ = 512
DEPTH = 1

CHUNK = 64
Q_BLOCK = 128
D_PLE = 256
EPS = 1e-6

RET_HEADS = 4
RET_DK = 128
RET_DV = 128
RET_QK_WIDTH = RET_HEADS * RET_DK
RET_WIDTH = RET_HEADS * RET_DV
DIFF_HEADS = 4
DIFF_DH = 64
DIFF_DV = 2 * DIFF_DH
DIFF_QK_WIDTH = DIFF_HEADS * 2 * DIFF_DH
DIFF_WIDTH = DIFF_HEADS * DIFF_DV
MIX_WIDTH = RET_WIDTH + DIFF_WIDTH
IN_SPLITS = (RET_QK_WIDTH, RET_QK_WIDTH, RET_WIDTH, RET_WIDTH, DIFF_QK_WIDTH, DIFF_QK_WIDTH, DIFF_WIDTH)
IN_COLS = sum(IN_SPLITS)

N_GROUPS = 4
EXPERTS_PER_GROUP = 4
N_EXPERTS = N_GROUPS * EXPERTS_PER_GROUP
TOP_K_INNER = 2
D_EXPERT = 512

kernel_name = "hybrid_retention_diffattn_hmoe_ple"

def rmsnorm(x, g):
    xf = x.astype(jnp.float32)
    y = xf * lax.rsqrt(jnp.mean(xf * xf, axis=-1, keepdims=True) + EPS)
    return (y * g.astype(jnp.float32)).astype(x.dtype)

def retention(q, k, v, g):
    B, S, _ = q.shape
    nc = S // CHUNK
    dt = q.dtype
    f32 = jnp.float32

    def to_chunks(t, d):
        return t.astype(f32).reshape(B, nc, CHUNK, RET_HEADS, d).transpose(0, 1, 3, 2, 4)

    qc = to_chunks(q, RET_DK)
    kc = to_chunks(k, RET_DK) * (RET_DK ** -0.5)
    vc = to_chunks(v, RET_DV)
    log_g = jnp.log1p(-jnp.exp2(-5.0 - jnp.arange(RET_HEADS, dtype=f32)))
    pos = jnp.arange(CHUNK, dtype=f32)
    rel = pos[:, None] - pos[None, :]
    intra_decay = jnp.where(rel >= 0, jnp.exp(log_g[:, None, None] * jnp.maximum(rel, 0.0)), 0.0)
    q_decay = jnp.exp(log_g[:, None] * (pos + 1.0))
    k_decay = jnp.exp(log_g[:, None] * (CHUNK - 1.0 - pos))
    chunk_decay = jnp.exp(log_g * CHUNK)

    scores = jnp.einsum('bnhtd,bnhsd->bnhts', qc, kc) * intra_decay
    intra = jnp.einsum('bnhts,bnhse->bnhte', scores, vc)
    kv = jnp.einsum('bnhsd,bnhse->nbhde', kc * k_decay[:, :, None], vc)

    def step(state, kv_n):
        return chunk_decay[None, :, None, None] * state + kv_n, state

    _, prev = lax.scan(step, jnp.zeros((B, RET_HEADS, RET_DK, RET_DV), f32), kv)
    cross = jnp.einsum('bnhtd,nbhde->bnhte', qc * q_decay[:, :, None], prev)
    o = intra + cross
    o = o * lax.rsqrt(jnp.mean(o * o, axis=-1, keepdims=True) + EPS)
    o = o.transpose(0, 1, 3, 2, 4).reshape(B, S, RET_WIDTH)
    return (jax.nn.silu(g.astype(f32)) * o).astype(dt)

def diff_attention(q, k, v, lam, subln_g, lam_init):
    B, S, _ = q.shape
    nb = S // Q_BLOCK
    dt = q.dtype
    f32 = jnp.float32
    qh = q.astype(f32).reshape(B, S, DIFF_HEADS, 2, DIFF_DH) * (DIFF_DH ** -0.5)
    kh = k.astype(f32).reshape(B, S, DIFF_HEADS, 2, DIFF_DH)
    vh = v.astype(f32).reshape(B, S, DIFF_HEADS, DIFF_DV)
    qb = qh.reshape(B, nb, Q_BLOCK, DIFF_HEADS, 2, DIFF_DH).transpose(1, 0, 2, 3, 4, 5)
    slopes = jnp.exp2(-8.0 * jnp.arange(1, DIFF_HEADS + 1, dtype=f32) / DIFF_HEADS)
    key_pos = jnp.arange(S)

    def block(args):
        q_blk, start = args
        q_pos = start + jnp.arange(Q_BLOCK)
        s = jnp.einsum('bqhcd,bkhcd->bchqk', q_blk, kh)
        dist = jnp.abs(q_pos[:, None] - key_pos[None, :]).astype(f32)
        allowed = (key_pos[None, :] // CHUNK) <= (q_pos[:, None] // CHUNK)
        s = jnp.where(allowed, s - slopes[:, None, None] * dist, -jnp.inf)
        a = jax.nn.softmax(s, axis=-1)
        w = a[:, 0] - lam * a[:, 1]
        return jnp.einsum('bhqk,bkhe->bqhe', w, vh)

    o = lax.map(block, (qb, jnp.arange(nb) * Q_BLOCK))
    o = o.transpose(1, 0, 2, 3, 4).reshape(B, S, DIFF_HEADS, DIFF_DV)
    o = o * lax.rsqrt(jnp.mean(o * o, axis=-1, keepdims=True) + EPS) * subln_g.astype(f32)
    o = o * (1.0 - lam_init)
    return o.reshape(B, S, DIFF_WIDTH).astype(dt)

def hierarchical_moe(h, w_rg, b_rg, w_re, b_re, w_gate, w_up, w_down):
    B, S, D = h.shape
    f32 = jnp.float32
    t = h.reshape(B * S, D)
    lg = (t @ w_rg).astype(f32) + b_rg.astype(f32)
    g_idx = jnp.argmax(lg, axis=-1)
    g_w = jnp.take_along_axis(jax.nn.softmax(lg, axis=-1), g_idx[:, None], axis=-1)
    le = ((t @ w_re).astype(f32) + b_re.astype(f32)).reshape(-1, N_GROUPS, EXPERTS_PER_GROUP)
    le_sel = jnp.take_along_axis(le, g_idx[:, None, None], axis=1)[:, 0]
    top_v, top_i = lax.top_k(le_sel, TOP_K_INNER)
    top_w = jax.nn.softmax(top_v, axis=-1) * g_w
    w_in_group = jnp.sum(jax.nn.one_hot(top_i, EXPERTS_PER_GROUP, dtype=f32) * top_w[..., None], axis=1)
    combine = jax.nn.one_hot(g_idx, N_GROUPS, dtype=f32)[:, :, None] * w_in_group[:, None, :]
    combine = combine.reshape(-1, N_EXPERTS).astype(h.dtype)
    out = jnp.zeros_like(t)
    for gi in range(N_GROUPS):
        sl = slice(gi * EXPERTS_PER_GROUP, (gi + 1) * EXPERTS_PER_GROUP)
        hid = jax.nn.silu(jnp.einsum('td,edf->etf', t, w_gate[sl])) * jnp.einsum('td,edf->etf', t, w_up[sl])
        hid = hid * combine[:, sl].T[:, :, None]
        out = out + jnp.einsum('etf,efd->td', hid, w_down[sl])
    return out.reshape(B, S, D)

def setup_inputs(seed: int = 0) -> dict:
    key = jax.random.key(seed)
    ks = jax.random.split(key, 24)
    f32 = jnp.float32
    nrm = lambda k, shape, s: jax.random.normal(k, shape, f32) * s
    gain = lambda k, shape: 1.0 + 0.01 * jax.random.normal(k, shape, f32)
    return {
        "x": nrm(ks[0], (BATCH, SEQ, D_MODEL), 1.0),
        "p": nrm(ks[1], (DEPTH, BATCH, SEQ, D_PLE), 1.0),
        "norm_mix": gain(ks[2], (DEPTH, D_MODEL)),
        "w_in": nrm(ks[3], (DEPTH, D_MODEL, IN_COLS), D_MODEL ** -0.5),
        "lam_q1": nrm(ks[4], (DEPTH, DIFF_DH), 0.1),
        "lam_k1": nrm(ks[5], (DEPTH, DIFF_DH), 0.1),
        "lam_q2": nrm(ks[6], (DEPTH, DIFF_DH), 0.1),
        "lam_k2": nrm(ks[7], (DEPTH, DIFF_DH), 0.1),
        "diff_subln": gain(ks[8], (DEPTH, DIFF_DV)),
        "w_out": nrm(ks[9], (DEPTH, MIX_WIDTH, D_MODEL), MIX_WIDTH ** -0.5),
        "norm_ffn": gain(ks[10], (DEPTH, D_MODEL)),
        "w_router_group": nrm(ks[11], (DEPTH, D_MODEL, N_GROUPS), D_MODEL ** -0.5),
        "b_router_group": nrm(ks[12], (DEPTH, N_GROUPS), 0.01),
        "w_router_expert": nrm(ks[13], (DEPTH, D_MODEL, N_EXPERTS), D_MODEL ** -0.5),
        "b_router_expert": nrm(ks[14], (DEPTH, N_EXPERTS), 0.01),
        "w_gate": nrm(ks[15], (DEPTH, N_EXPERTS, D_MODEL, D_EXPERT), D_MODEL ** -0.5),
        "w_up": nrm(ks[16], (DEPTH, N_EXPERTS, D_MODEL, D_EXPERT), D_MODEL ** -0.5),
        "w_down": nrm(ks[17], (DEPTH, N_EXPERTS, D_EXPERT, D_MODEL), D_EXPERT ** -0.5),
        "norm_ple": gain(ks[18], (DEPTH, D_MODEL)),
        "w_ple_gate": nrm(ks[19], (DEPTH, D_MODEL, D_MODEL), D_MODEL ** -0.5),
        "w_ple_proj": nrm(ks[20], (DEPTH, D_PLE, D_MODEL), D_PLE ** -0.5),
        "norm_final": gain(ks[21], (D_MODEL,)),
    }

def reference(x, p, norm_mix, w_in, lam_q1, lam_k1, lam_q2, lam_k2, diff_subln, w_out,
              norm_ffn, w_router_group, b_router_group, w_router_expert, b_router_expert,
              w_gate, w_up, w_down, norm_ple, w_ple_gate, w_ple_proj, norm_final):
    f32 = jnp.float32
    for i in range(DEPTH):
        h = rmsnorm(x, norm_mix[i])
        proj = h @ w_in[i]
        rq, rk, rv, rg, dq, dk, dv = jnp.split(proj, np.cumsum(IN_SPLITS)[:-1].tolist(), axis=-1)
        lam_init = 0.8 - 0.6 * math.exp(-0.3 * i)
        lam = (jnp.exp(jnp.sum(lam_q1[i].astype(f32) * lam_k1[i].astype(f32)))
               - jnp.exp(jnp.sum(lam_q2[i].astype(f32) * lam_k2[i].astype(f32))) + lam_init)
        mix = jnp.concatenate([retention(rq, rk, rv, rg),
                               diff_attention(dq, dk, dv, lam, diff_subln[i], lam_init)], axis=-1)
        x = x + mix @ w_out[i]
        h = rmsnorm(x, norm_ffn[i])
        x = x + hierarchical_moe(h, w_router_group[i], b_router_group[i], w_router_expert[i],
                                 b_router_expert[i], w_gate[i], w_up[i], w_down[i])
        gate = jax.nn.sigmoid(rmsnorm(x, norm_ple[i]) @ w_ple_gate[i])
        x = x + gate * (p[i] @ w_ple_proj[i])
    return rmsnorm(x, norm_final)


_drawn_inputs = setup_inputs


def setup_inputs(seed=0):
    import zlib

    import numpy as np

    out = dict(_drawn_inputs(seed))
    spreads = {}
    factors = {'norm_mix': 3.078,
     'lam_k1': 3.126,
     'lam_q2': 3.169,
     'diff_subln': 8.0,
     'norm_ffn': 5.287,
     'b_router_group': 7.957,
     'b_router_expert': 5.427,
     'norm_ple': 8.0,
     'norm_final': 5.483}
    for name, (base, spread) in spreads.items():
        noise = np.random.default_rng([zlib.crc32(name.encode()), seed]).standard_normal(out[name].shape)
        drawn = base * np.exp(spread * noise) if base else spread * noise
        out[name] = __import__('jax').numpy.asarray(drawn.astype(out[name].dtype))
    for name, factor in factors.items():
        out[name] = (out[name] * factor).astype(out[name].dtype)
    return out
```

```python
from contextlib import ExitStack

import numpy as np

import concourse.bass as bass
from concourse import mybir

F32 = mybir.dt.float32
F32R = mybir.dt.float32r
I32 = mybir.dt.int32
U32 = mybir.dt.uint32
ALU = mybir.AluOpType
ACT = mybir.ActivationFunctionType
X = mybir.AxisListType.X

P = 128
SEQ, D = 512, 1024
NT = SEQ // P
KD = D // P
CHUNK = 64
HEADS = 4
DK = 128
EPS = 1e-6
LAM_INIT = 0.2
D_PLE = 256
N_GROUPS, PER_GROUP, N_EXPERTS, D_EXPERT = 4, 4, 16, 512
TOP_K = 2
NR = N_GROUPS + N_EXPERTS
BLK = 64
BPE = SEQ // BLK
MAX_BLOCKS = (TOP_K * SEQ - N_EXPERTS) // BLK + N_EXPERTS
ROWS = 34 * BLK
UC = 256
QKV = 512
PARTS = [2048, 2560, 3072, 0, 512, 1024, 1536]
DQ, DKEY, DV, RQ, RK, RV, RG = range(7)
IN_UNITS = 2 * len(PARTS)
OUT_UNITS = D // UC
UNITS = IN_UNITS + OUT_UNITS
NATURAL = (DV, RV)
MASKED = -1e30


def unit_outs(u):
    return NT if u >= IN_UNITS or u // 2 in NATURAL else 2


def outs_before(u):
    return sum(unit_outs(v) for v in range(u))


def shape_constants():
    s = np.arange(P)[:, None]
    t = np.arange(SEQ)[None, :]
    decay = np.zeros((P, HEADS, SEQ), np.float32)
    bias = np.zeros((P, HEADS, SEQ), np.float32)
    for h in range(HEADS):
        log_g = np.log1p(-np.exp2(-5.0 - h))
        decay[:, h] = np.where(t >= s, np.exp(log_g * np.maximum(t - s, 0)), 0.0) * DK ** -0.5
        key = t - (SEQ - P)
        slope = 2.0 ** (-8.0 * (h + 1) / HEADS)
        allowed = (key // CHUNK) <= (s // CHUNK)
        bias[:, h] = np.where(allowed, -slope * np.abs(s - key), MASKED)
    small = np.concatenate([
        np.eye(P),
        (s < np.arange(P)[None, :]).astype(float),
        np.tile(np.arange(PER_GROUP), (P, 1)),
        np.tile(np.arange(BPE) * BLK, (P, 1)),
        np.tile(np.arange(32), (P, 1)),
    ], 1).astype(np.float32)
    return decay.reshape(P, -1), bias.reshape(P, -1), small


def trunk(nc, x, p, norm_mix, w_in, lam_q1, lam_k1, lam_q2, lam_k2, diff_subln, w_out, norm_ffn,
          w_rg, b_rg, w_re, b_re, w_gate, w_up, w_down, norm_ple, w_ple_gate, w_ple_proj,
          norm_final, decay_tab, bias_tab, small_tab, out):
    ctx = ExitStack()
    with ctx:
        K = 1024
        base = -(-nc.sbuf_base // 32) * 32

        def at(name, kb, shape, dt=F32):
            return nc.alloc_sbuf_tensor_at(name, shape, dt, offset=base + int(kb * K))

        w_raw = [at(f"w_raw{i}", 8 * i, [P, KD, UC]) for i in range(2)]
        w_hi = [at(f"w_hi{i}", 16 + 8 * i, [P, KD, UC], F32R) for i in range(2)]
        w_lo = [at(f"w_lo{i}", 32 + 8 * i, [P, KD, UC], F32R) for i in range(2)]
        h2T = at("h2T", 0, [P, KD, SEQ])
        ple_gate_raw = at("ple_gate_raw", 0, [P, KD, D])
        ple_proj = at("ple_proj", 16, [P, D_PLE // P, D])
        pT = at("pT", 24, [P, D_PLE // P, SEQ])
        p_sb = at("p_sb", 32, [P, NT, D_PLE])
        h3T_hi = [at(f"h3T_hi{i}", 32 + 8 * i, [P, KD, P], F32R) for i in range(2)]
        h3T_lo = [at(f"h3T_lo{i}", 36 + 8 * i, [P, KD, P], F32R) for i in range(2)]
        hT_hi = at("hT_hi", 48, [P, KD, SEQ], F32R)
        hT_lo = at("hT_lo", 64, [P, KD, SEQ], F32R)
        mixT_hi = at("mixT_hi", 48, [P, KD, SEQ], F32R)
        mixT_lo = at("mixT_lo", 64, [P, KD, SEQ], F32R)
        ple = at("ple", 48, [P, NT, D])
        rows = at("rows", 64, [P, D // 2])
        rowsT = at("rowsT", 68, [P, 4, 2, BLK])
        silu_g = at("silu_g", 70, [P, UC])
        hid = at("hid", 71, [P, UC])
        hidT = at("hidT", 72, [P, 2, 2, BLK])
        y_blk = at("y_blk", 73, [P, D // 2])
        h3 = at("h3", 64, [P, D])
        h3g = at("h3g", 68, [P, D])
        out_sb = at("out_sb", 72, [P, D])
        gfin = at("gfin", 76, [P, D])
        xr = at("xr", 80, [P, NT, D])
        small = at("small", 96, [P, 300])
        ident = small[:, 0:P]
        tri = small[:, P:2 * P]
        iota4 = small[:, 256:260]
        iota64 = small[:, 260:268]
        iota_blk = small[0:1, 268:300]
        mean_w = at("mean_w", 97.25, [P, P])
        ones = at("ones", 97.75, [P, P])
        gffn = at("gffn", 98.25, [P, D])
        zeros = at("zeros", 102.25, [P, UC])
        w_r = at("w_r", 103.25, [P, KD, NR])
        cur = [104.0]

        def tiny(name, shape, dt=F32):
            n = int(np.prod(shape[1:])) * 4
            t = at(name, cur[0], shape, dt)
            cur[0] += -(-n // 32) * 32 / K
            assert cur[0] <= 108
            return t

        gmix = tiny("gmix", [P, KD])
        gple = tiny("gple", [P, KD])
        b_r = tiny("b_r", [NR, 1])
        subln = tiny("subln", [P, 1])
        subln8 = tiny("subln8", [P, 1])
        eps = tiny("eps", [P, 1])
        lam_dot = tiny("lam_dot", [P, 2])
        lam_exp = tiny("lam_exp", [P, 2])
        neg_lam = tiny("neg_lam", [P, 1])
        ssq = tiny("ssq", [P, NT])
        rms = tiny("rms", [P, NT])
        rstd = tiny("rstd", [P, NT])
        row_max = [tiny(f"row_max{i}", [P, 2]) for i in range(2)]
        neg_max = [tiny(f"neg_max{i}", [P, 2]) for i in range(2)]
        z = [tiny(f"z{i}", [P, 2]) for i in range(2)]
        rz = [tiny(f"rz{i}", [P, 2]) for i in range(2)]
        rl = [tiny(f"rl{i}", [P, 1]) for i in range(2)]
        ssq2 = tiny("ssq2", [P, NT, OUT_UNITS])
        sum2 = tiny("sum2", [P, NT])
        rms2 = tiny("rms2", [P, NT])
        rstd2 = tiny("rstd2", [P, NT])
        ssq3 = tiny("ssq3", [P, NT])
        rms3 = tiny("rms3", [P, NT])
        rstd3 = tiny("rstd3", [P, NT])
        ssq4 = tiny("ssq4", [P, NT])
        rms4 = tiny("rms4", [P, NT])
        rstd4 = tiny("rstd4", [P, NT])
        w_top = [tiny(f"w_top{k}", [P, NT]) for k in range(2)]
        slot_i = [tiny(f"slot_i{k}", [P, NT], I32) for k in range(2)]
        cum_i = tiny("cum_i", [1, N_EXPERTS], I32)
        blk_slot = tiny("blk_slot", [1, 32], I32)
        blk_loads = tiny("blk_loads", [1, 32], I32)
        dqT = at("dqT", 108, [P, HEADS, SEQ])
        dkT = at("dkT", 116, [P, HEADS, SEQ])
        dv = at("dv", 124, [P, NT, QKV])
        rqT = at("rqT", 132, [P, HEADS, SEQ])
        rkT = at("rkT", 140, [P, HEADS, SEQ])
        rv = at("rv", 148, [P, NT, QKV])
        rgT = at("rgT", 156, [P, HEADS, SEQ])
        dest = {DQ: dqT, DKEY: dkT, DV: dv, RQ: rqT, RK: rkT, RV: rv, RG: rgT}
        decay = at("decay", 164, [P, HEADS, SEQ])
        bias = at("bias", 172, [P, HEADS, SEQ])
        xn = [at(f"xn{i}", 180 + 4 * i, [P, D]) for i in range(2)]
        hg = at("hg", 188, [P, D])
        junk = at("junk", 193, [P, D])
        lamv = at("lamv", 198, [P, 4, 64])
        lam_junk = at("lam_junk", 199, [P, 2, 64])
        A = [at(f"A{i}", 180 + 4 * i, [P, 2, SEQ]) for i in range(2)]
        W = [at(f"W{i}", 188 + 0.5 * (i * (i + 1) // 2), [P, P * (i + 1)]) for i in range(NT)]
        pT_off = [0, 512, 896, 1152]
        probsT = [at(f"probsT{i}", 193 + 5 * i, [P, 1280]) for i in range(2)]
        osq = [at(f"osq{i}", 180 + 2 * i, [P, SEQ]) for i in range(2)]
        orms = [at(f"orms{i}", 184 + 2 * i, [P, SEQ]) for i in range(2)]
        onorm = [at(f"onorm{i}", 188 + 2 * i, [P, SEQ]) for i in range(2)]
        ring_gu = [at(f"ring_gu{i}", 108 + 48 * i, [P, KD, 2, D_EXPERT]) for i in range(2)]
        ring_dn = [at(f"ring_dn{i}", 140 + 48 * i, [P, D_EXPERT // P, D]) for i in range(2)]
        h2 = at("h2", 188, [P, NT, D])
        r0 = [32.0]

        def routing(name, shape, dt=F32):
            t = at(name, 36 + r0[0] - 32.0, shape, dt)
            r0[0] += -(-int(np.prod(shape[1:])) * 4 // 32) * 32 / K
            assert r0[0] <= 40
            return t

        ple_hi = [at(f"ple_hi{i}", 108 + 16 * i, [P, KD, D // 2], F32R) for i in range(2)]
        ple_lo = [at(f"ple_lo{i}", 140 + 16 * i, [P, KD, D // 2], F32R) for i in range(2)]
        yg = [[at(f"yg{i}_{k}", 172 + 8 * i + 4 * k, [P, D]) for k in range(2)] for i in range(NT)]

        lgT = at("lgT", 40, [NR, SEQ])
        lg = routing("lg", [P, NT, NR])
        gmax = routing("gmax", [P, NT])
        eq = routing("eq", [P, NT, 4])
        cand = routing("cand", [P, NT, 4])
        cmin = routing("cmin", [P, NT])
        oh_g = routing("oh_g", [P, NT, 4])
        gsub = routing("gsub", [P, NT, 4])
        gexp = routing("gexp", [P, NT, 4])
        gsum = routing("gsum", [P, NT])
        g_w = routing("g_w", [P, NT])
        picked = routing("picked", [P, NT, 4, 4])
        les = routing("les", [P, NT, 4])
        les2 = routing("les2", [P, NT, 4])
        v_top = [routing(f"v_top{k}", [P, NT]) for k in range(2)]
        oh = [routing(f"oh{k}", [P, NT, 4]) for k in range(2)]
        vd = routing("vd", [P, NT])
        ve = routing("ve", [P, NT])
        vs = routing("vs", [P, NT])
        vr = routing("vr", [P, NT])
        E = at("E", 42, [P, 2, NT, 4, 4])
        member = at("member", 42.5, [P, NT, 16])
        prefix = at("prefix", 42.75, [P, 5, 16])
        counts = at("counts", 43.25, [P, 16])
        nb_gt = at("nb_gt", 43.5, [P, 16, BPE])
        nb = at("nb", 44, [P, 16])
        nb1 = at("nb1", 44.125, [P, 16])
        one16 = at("one16", 44.25, [P, 16])
        cum = at("cum", 44.375, [P, 16])
        first = at("first", 44.5, [P, 16])
        first64 = at("first64", 44.625, [P, 16])
        slots = at("slots", 44.75, [P, NT, 16])
        slot_e = at("slot_e", 45, [P, 2, NT, 16])
        slot_f = at("slot_f", 45.5, [P, 2, NT])
        blk_ge = at("blk_ge", 46, [1, 32, 16])
        blk_e = at("blk_e", 45.75, [1, 32])
        blk_ei = at("blk_ei", 45.875, [1, 32], I32)
        blk_t = at("blk_t", 43.5, [1, 32], I32)

        xs = nc.dram_tensor("slot_rows", [ROWS, D], F32, kind="Internal").ap()
        ys = nc.dram_tensor("slot_out", [32 * BLK, D], F32, kind="Internal").ap()

        bank = [ctx.enter_context(nc.psum_tensor(f"bank{i}", [P, 512], F32)) for i in range(8)]
        b_proj = bank[0:2]
        b_score = bank[2:6]
        b_o, b_mean = bank[6], bank[7]
        b_gu, b_dn, b_xT, b_hT = bank[0], bank[1], bank[2], bank[3]
        b_gate = [bank[0:2], bank[6:8]]

        def sem(name):
            return ctx.enter_context(nc.semaphore(name))

        s_x = [sem(f"x_loaded{i}") for i in range(NT)]
        s_const = sem("constants_loaded")
        s_tab = sem("tables_loaded")
        s_lam = sem("lambda_vectors_loaded")
        s_raw = [sem(f"unit_loaded{i}") for i in range(2)]
        s_zero = sem("slot_rows_zeroed")
        s_gu = [sem(f"gate_up_loaded{i}") for i in range(2)]
        s_dn = [sem(f"down_loaded{i}") for i in range(2)]
        s_pple = sem("ple_inputs_loaded")
        s_plegate = sem("ple_gate_loaded")
        s_scatter = sem("rows_scattered")
        s_rows = sem("block_rows_loaded")
        s_ystored = sem("block_out_stored")
        s_gather = [sem(f"expert_rows_gathered{i}") for i in range(NT)]
        s_out = sem("out_stored")

        dve_chain = sem("dve_chain")
        act_chain = sem("act_chain")
        memsets = sem("memsets_done")
        x_ssq = sem("x_rms_ready")
        xn_ready = sem("xn_ready")
        xn_T = sem("xn_transposed")
        hg_ready = sem("hg_ready")
        h_hi = sem("h_hi_ready")
        h_lo = sem("h_lo_ready")
        hi_done = sem("unit_hi_ready")
        lo_done = sem("unit_lo_ready")
        proj_done = sem("proj_done")
        proj_evac = sem("proj_evacuated")
        lam_ready = sem("lam_dots_ready")
        lam_exped = sem("lam_exp_ready")
        score_done = sem("scores_ready")
        score_evac = sem("scores_evacuated")
        max_ready = sem("row_max_ready")
        exp_done = sem("exp_ready")
        w_ready = sem("probs_ready")
        wT_done = sem("probs_transposed")
        wT_ready = sem("probsT_ready")
        ret_done = sem("ret_scores_ready")
        ret_ready = sem("ret_scoresT_ready")
        o_done = sem("head_out_ready")
        o_evac = sem("head_out_evacuated")
        osq_ready = sem("head_squares_ready")
        mean_done = sem("head_mean_ready")
        orms_ready = sem("head_rms_ready")
        onorm_ready = sem("head_normed")
        mix_hi = sem("mix_hi_ready")
        mix_lo = sem("mix_lo_ready")
        x1_add = sem("x1_added")
        x1_sq = sem("x1_squares_ready")
        sum2_ready = sem("x1_sum_ready")
        rms2_ready = sem("x1_rms_ready")
        h2_ready = sem("h2_ready")
        h2_T = sem("h2_transposed")
        h2T_act = sem("h2T_low_half_ready")
        h2T_dve = sem("h2T_high_half_ready")
        lgT_done = sem("logits_transposed_done")
        lgT_ready = sem("logits_biased")
        lg_done = sem("logits_done")
        gsub_ready = sem("group_logits_shifted")
        gexp_ready = sem("group_exp_ready")
        vd_ready = sem("expert_logit_gap_ready")
        ve_ready = sem("expert_exp_ready")
        member_ready = sem("members_ready")
        rank_done = sem("ranks_ready")
        slot_ready = sem("slots_ready")
        table_ready = sem("block_tables_ready")
        p_T = sem("p_transposed")
        pT_ready = sem("pT_ready")
        ple_done = sem("ple_product_ready")
        ple_ready = sem("ple_evacuated")
        xT_done = sem("rows_transposed")
        xT_ready = sem("rowsT_ready")
        gu_done = sem("gate_up_done")
        sg_ready = sem("silu_ready")
        hid_ready = sem("hidden_ready")
        hT_done = sem("hidden_transposed")
        hidT_ready = sem("hiddenT_ready")
        dn_done = sem("down_done")
        dn_bank_free = sem("down_bank_free")
        y_ready = sem("block_out_ready")
        y_free = sem("block_out_buffer_free")
        pg_hi = sem("ple_gate_hi_ready")
        pg_lo = sem("ple_gate_lo_ready")
        x2_ready = sem("x2_ready")
        rms3_ready = sem("x2_rms_ready")
        h3_ready = sem("h3_ready")
        h3_T = sem("h3_transposed")
        h3g_ready = sem("h3g_ready")
        h3_hi = sem("h3_hi_ready")
        h3_lo = sem("h3_lo_ready")
        gate_done = sem("ple_gate_logits_ready")
        gate_ready = sem("ple_gate_ready")
        x3_ready = sem("x3_ready")
        rms4_ready = sem("x3_rms_ready")
        res_ready = sem("result_ready")

        MIX_K = [4, 5, 6, 7, 0, 1, 2, 3]
        P1_OUTS = outs_before(IN_UNITS)
        block = ctx.enter_context(nc.Block())

        @block.sync
        def _(sp):
            w_in_v = w_in.rearrange("(k p) n -> p k n", p=P)
            w_out_v = w_out.rearrange("(k p) n -> p k n", p=P)

            def load_unit(u):
                if u >= 2:
                    sp.wait_ge(hi_done, u - 1)
                    sp.wait_ge(lo_done, u - 1)
                if u < IN_UNITS:
                    c = PARTS[u // 2] + UC * (u % 2)
                    src = w_in_v[:, :, c:c + UC]
                else:
                    c = UC * (u - IN_UNITS)
                    src = w_out_v[:, :, c:c + UC]
                sp.dma_start(w_raw[u % 2][:], src).then_inc(s_raw[u % 2], 16)

            load_unit(0)
            load_unit(1)
            sp.dma_start(bias[:], bias_tab.rearrange("p (h t) -> p h t", h=HEADS)).then_inc(s_tab, 16)
            sp.dma_start(decay[:], decay_tab.rearrange("p (h t) -> p h t", h=HEADS)).then_inc(s_tab, 16)
            for u in range(2, 8):
                load_unit(u)
            sp.wait_ge(memsets, 1)
            for t, n_rows in ((xs, ROWS), (ys, 32 * BLK)):
                sp.dma_start(t.rearrange("(p n) (m c) -> p (n m) c", p=P, c=UC),
                             zeros[:].unsqueeze(1).to_broadcast([P, n_rows * D // P // UC, UC])).then_inc(s_zero, 16)
            for u in range(8, UNITS):
                load_unit(u)
            sp.wait_ge(mix_lo, 2 * HEADS)
            sp.wait_ge(mix_hi, 2 * HEADS)

            def load_gu(e, slot):
                sp.dma_start(ring_gu[slot][:, :, 0, :],
                             w_gate[bass.ds(e, 1)].rearrange("o (k p) f -> p (o k) f", p=P)).then_inc(s_gu[slot], 16)
                sp.dma_start(ring_gu[slot][:, :, 1, :],
                             w_up[bass.ds(e, 1)].rearrange("o (k p) f -> p (o k) f", p=P)).then_inc(s_gu[slot], 16)

            def load_dn(e, slot):
                sp.dma_start(ring_dn[slot][:],
                             w_down[bass.ds(e, 1)].rearrange("o (k p) f -> p (o k) f", p=P)).then_inc(s_dn[slot], 16)

            load_gu(0, 0)
            load_dn(0, 0)
            sp.wait_ge(x1_add, NT * (OUT_UNITS - 1))
            sp.dma_start(ple_proj[:], w_ple_proj.rearrange("(k p) n -> p k n", p=P)).then_inc(s_pple, 16)
            sp.dma_start(p_sb[:], p.rearrange("(t p) c -> p t c", p=P)).then_inc(s_pple, 16)
            load_gu(1, 1)
            sp.wait_ge(s_scatter, 16 * NT * TOP_K)
            load_dn(1, 1)
            sp.wait_ge(ple_done, 2 * NT)
            sp.dma_start(ple_gate_raw[:], w_ple_gate.rearrange("(k p) n -> p k n", p=P)).then_inc(s_plegate, 16)
            sp.wait_ge(ple_ready, 2 * NT)
            sp.dma_start(gfin[:], norm_final.rearrange("(o n) -> o n", o=1).to_broadcast([P, D])).then_inc(s_plegate, 16)
            sp.wait_ge(table_ready, 1)
            with sp.Fori(0, N_EXPERTS // 2 - 1) as pair:
                for slot in range(2):
                    used = sp.value_load(cum_i[0:1, bass.ds(2 * pair + slot, 1)], min_val=1, max_val=MAX_BLOCKS)
                    sp.wait_ge(gu_done, used)
                    load_gu(2 * pair + (slot + 2), slot)
                    sp.wait_ge(dn_done, used)
                    load_dn(2 * pair + (slot + 2), slot)
            for i in range(NT):
                sp.wait_ge(res_ready, i + 1)
                sp.dma_start(out[i * P:(i + 1) * P, :], out_sb[:]).then_inc(s_out, 16)
            sp.wait_ge(s_out, 16 * NT)

        @block.gpsimd
        def _(pool):
            pool.memset(zeros[:], 0.0).then_inc(memsets, 1)
            pool.memset(mean_w[:], 1.0 / P).then_inc(memsets, 1)
            pool.memset(ones[:], 1.0).then_inc(memsets, 1)
            pool.memset(eps[:], EPS).then_inc(memsets, 1)
            pool.wait_ge(memsets, 4)
            pool.sem_inc(y_free, 1)
            pool.wait_ge(s_zero, 32)
            pool.wait_ge(slot_ready, 1)
            for i in range(NT):
                for k in range(TOP_K):
                    pool.indirect_dma_start(
                        out=xs, out_offset=bass.IndirectOffsetOnAxis(ap=slot_i[k][:, i:i + 1].bitcast(U32), axis=0),
                        in_=h2[:, i, :], in_offset=None).then_inc(s_scatter, 16)
            pool.wait_ge(table_ready, 1)
            total = pool.value_load(cum_i[0:1, N_EXPERTS - 1:N_EXPERTS], min_val=N_EXPERTS, max_val=MAX_BLOCKS)

            def store(b):
                pool.wait_ge(y_ready, b + 2)
                for q in range(2):
                    pool.dma_start(ys[bass.ds(b * BLK, BLK), q * (D // 2):(q + 1) * (D // 2)],
                                   y_blk[q * BLK:(q + 1) * BLK, :]).then_inc(s_ystored, 16)
                pool.wait_ge(s_ystored, 32 * (b + 1))
                pool.sem_inc(y_free, 1)

            with pool.Fori(1, MAX_BLOCKS) as b:
                with pool.If(b < total):
                    store(b - 1)
            store(total - 1)
            for i in range(NT):
                for k in range(TOP_K):
                    pool.indirect_dma_start(
                        out=yg[i][k][:], out_offset=None, in_=ys,
                        in_offset=bass.IndirectOffsetOnAxis(ap=slot_i[k][:, i:i + 1].bitcast(U32), axis=0),
                    ).then_inc(s_gather[i], 16)

        @block.scalar
        def _(act):
            chain = [0]

            def link(ins):
                chain[0] += 1
                ins.then_inc(act_chain, 1)
                act.wait_ge(act_chain, chain[0])

            for i in range(NT):
                act.dma_start(xr[:, i, :], x[i * P:(i + 1) * P, :]).then_inc(s_x[i], 16)
                if i == 0:
                    act.dma_start(small[:], small_tab).then_inc(s_const, 16)
                    act.dma_start(gmix[:], norm_mix.rearrange("(k p) -> p k", p=P),
                                  allow_slow_non_contiguous=True).then_inc(s_const, 16)
            for n, v in enumerate((lam_q1, lam_k1, lam_q2, lam_k2)):
                act.dma_start(lamv[:, n, :], v.rearrange("(o n) -> o n", o=1).to_broadcast([P, 64])).then_inc(s_lam, 16)
            act.dma_start(gple[:], norm_ple.rearrange("(k p) -> p k", p=P),
                          allow_slow_non_contiguous=True).then_inc(s_const, 16)
            act.dma_start(subln[:], diff_subln.rearrange("(p o) -> p o", o=1)).then_inc(s_const, 16)
            act.dma_start(gffn[:], norm_ffn.rearrange("(o n) -> o n", o=1).to_broadcast([P, D])).then_inc(s_const, 16)
            act.dma_start(w_r[:, :, 0:N_GROUPS], w_rg.rearrange("(k p) n -> p k n", p=P)).then_inc(s_const, 16)
            act.dma_start(w_r[:, :, N_GROUPS:NR], w_re.rearrange("(k p) n -> p k n", p=P)).then_inc(s_const, 16)
            act.dma_start(b_r[0:N_GROUPS, :], b_rg.rearrange("(p o) -> p o", o=1)).then_inc(s_const, 16)
            act.dma_start(b_r[N_GROUPS:NR, :], b_re.rearrange("(p o) -> p o", o=1)).then_inc(s_const, 16)

            act.wait_ge(memsets, 4)
            for i in range(NT):
                act.wait_ge(s_x[i], 16)
                link(nc.scalar.activation(junk[:], xr[:, i, :], ACT.Square, accum_out=ssq[:, i:i + 1]))
                nc.scalar.activation(rms[:, i:i + 1], ssq[:, i:i + 1], ACT.Sqrt, bias=eps[:], scale=1.0 / D).then_inc(x_ssq, 1)

            def split_hi(u):
                if u >= 2:
                    act.wait_ge(proj_done, outs_before(u - 1))
                act.wait_ge(s_raw[u % 2], 16 * (u // 2 + 1))
                nc.scalar.activation(w_hi[u % 2][:], w_raw[u % 2][:], ACT.Copy).then_inc(hi_done, 1)

            split_hi(0)
            for i in range(NT):
                act.wait_ge(hg_ready, i + 1)
                nc.scalar.activation(hT_hi[:, :, i * P:(i + 1) * P], hg[:].rearrange("p (k t) -> p k t", k=KD),
                                     ACT.Copy).then_inc(h_hi, 1)
            split_hi(1)

            def evacuate(u):
                part, half = u // 2, u % 2
                for j in range(unit_outs(u)):
                    n = outs_before(u) + j
                    act.wait_ge(proj_done, n + 1)
                    b = b_proj[n % 2]
                    if part in NATURAL:
                        o, i_ = dest[part][:, j, half * UC:(half + 1) * UC], b[:, 0:UC]
                        nc.scalar.activation(o, i_, ACT.Copy).then_inc(proj_evac, 1)
                    else:
                        o = dest[part][:, 2 * half + j, :]
                        if part == RG:
                            nc.scalar.activation(o, b[:], ACT.Silu).then_inc(proj_evac, 1)
                        else:
                            nc.scalar.activation(o, b[:], ACT.Copy, scale=0.125 if part == DQ else 1.0).then_inc(proj_evac, 1)

            def exps(h):
                for i in range(NT):
                    s, L = NT * h + i, P * (i + 1)
                    act.wait_ge(max_ready, s + 1)
                    for c in range(2):
                        last = nc.scalar.activation(A[s % 2][:, c, 0:L], A[s % 2][:, c, 0:L], ACT.Exp,
                                                    bias=neg_max[s % 2][:, c:c + 1], accum_out=z[s % 2][:, c:c + 1])
                    last.then_inc(exp_done, 1)

            def probsT_evac(h):
                for j in range(NT):
                    act.wait_ge(wT_done, h + 1)
                    if h >= 2 and j == 0:
                        act.wait_ge(o_done, h - 1)
                    o = pT_off[j]
                    nc.scalar.activation(probsT[h % 2][:, o:o + SEQ - P * j], b_score[j][:, P * j:SEQ],
                                         ACT.Copy).then_inc(wT_ready, 1)

            def head_evac(n):
                act.wait_ge(o_done, n + 1)
                o = dqT if n < HEADS else rqT
                nc.scalar.activation(o[:, n % HEADS, :], b_o[:], ACT.Copy).then_inc(o_evac, 1)

            def head_squares(n):
                act.wait_ge(o_evac, n + 1)
                if n >= 2:
                    act.wait_ge(mean_done, n - 1)
                o = dqT if n < HEADS else rqT
                nc.scalar.activation(osq[n % 2][:], o[:, n % HEADS, :], ACT.Square).then_inc(osq_ready, 1)

            def head_rms(n):
                act.wait_ge(mean_done, n + 1)
                if n >= 2:
                    act.wait_ge(onorm_ready, n - 1)
                nc.scalar.activation(orms[n % 2][:], b_mean[:], ACT.Sqrt, bias=eps[:]).then_inc(orms_ready, 1)

            def head_hi(n):
                act.wait_ge(onorm_ready, n + 1)
                nc.scalar.activation(mixT_hi[:, MIX_K[n], :], onorm[n % 2][:], ACT.Copy).then_inc(mix_hi, 1)

            def unit(u):
                evacuate(u)
                split_hi(u + 2)

            act.wait_ge(lam_ready, 1)
            nc.scalar.activation(lam_exp[:], lam_dot[:], ACT.Exp).then_inc(lam_exped, 1)
            for u in range(7):
                unit(u)
            for h in range(HEADS):
                exps(h)
                unit(7 + 2 * h)
                probsT_evac(h)
                if h < HEADS - 1:
                    unit(8 + 2 * h)
                    head_evac(h)
            head_evac(3)
            head_squares(0)
            for n in range(2 * HEADS):
                if n < HEADS:
                    head_evac(HEADS + n)
                if n + 1 < 2 * HEADS:
                    head_squares(n + 1)
                head_rms(n)
                head_hi(n)

            for u in range(OUT_UNITS):
                for i in range(NT):
                    m = NT * u + i
                    act.wait_ge(x1_add, m + 1)
                    if m:
                        act.wait_ge(x1_sq, m)
                    nc.scalar.activation(b_mean[:, 0:UC], xr[:, i, u * UC:(u + 1) * UC], ACT.Square,
                                         accum_out=ssq2[:, i, u:u + 1]).then_inc(x1_sq, 1)
                    if u == OUT_UNITS - 1:
                        act.wait_ge(sum2_ready, i + 1)
                        nc.scalar.activation(rms2[:, i:i + 1], sum2[:, i:i + 1], ACT.Sqrt, bias=eps[:],
                                             scale=1.0 / D).then_inc(rms2_ready, 1)
                if u < 2:
                    split_hi(IN_UNITS + 2 + u)
            for i in range(NT):
                act.wait_ge(h2_T, i + 1)
                nc.scalar.activation(h2T[:, 0:4, i * P:(i + 1) * P],
                                     b_score[2 * (i % 2)][:].rearrange("p (k t) -> p k t", k=4),
                                     ACT.Copy).then_inc(h2T_act, 1)
            act.wait_ge(lgT_done, NT)
            nc.scalar.activation(lgT[:], b_o[0:NR, :], ACT.Identity, bias=b_r[:]).then_inc(lgT_ready, 1)
            for c in range(D_PLE // P):
                act.wait_ge(p_T, c + 1)
                nc.scalar.activation(pT[:, c, :], b_score[c][:], ACT.Copy).then_inc(pT_ready, 1)
            act.wait_ge(gsub_ready, 1)
            nc.scalar.activation(gexp[:], gsub[:], ACT.Exp).then_inc(gexp_ready, 1)
            act.wait_ge(vd_ready, 1)
            nc.scalar.activation(ve[:], vd[:], ACT.Exp).then_inc(ve_ready, 1)
            for n in range(2 * NT):
                act.wait_ge(ple_done, n + 1)
                nc.scalar.activation(ple[:, n // 2, (n % 2) * 512:(n % 2) * 512 + 512], b_proj[n % 2][:],
                                     ACT.Copy).then_inc(ple_ready, 1)

            act.wait_ge(table_ready, 1)
            total = act.value_load(cum_i[0:1, N_EXPERTS - 1:N_EXPERTS], min_val=N_EXPERTS, max_val=MAX_BLOCKS)

            def load_rows(b):
                for q in range(2):
                    act.dma_start(rows[q * BLK:(q + 1) * BLK, :],
                                  xs[bass.ds(b * BLK, BLK), q * (D // 2):(q + 1) * (D // 2)]).then_inc(s_rows, 16)

            def rowsT_evac(b):
                act.wait_ge(xT_done, b + 1)
                nc.scalar.activation(rowsT[:], b_xT[:].rearrange("p (j q t) -> p j q t", j=4, q=2),
                                     ACT.Copy).then_inc(xT_ready, 1)
                load_rows(b + 1)

            def silu(b):
                act.wait_ge(gu_done, b + 1)
                nc.scalar.activation(silu_g[:], b_gu[:, 0:UC], ACT.Silu).then_inc(sg_ready, 1)

            act.wait_ge(s_scatter, 16 * NT * TOP_K)
            load_rows(0)
            rowsT_evac(0)
            silu(0)
            rowsT_evac(1)
            with act.Fori(1, MAX_BLOCKS) as b:
                with act.If(b < total):
                    act.wait_ge(hid_ready, b)
                    silu(b)
                    rowsT_evac(b + 1)

            act.wait_ge(s_plegate, 32)
            act.wait_ge(dn_done, total)
            for q in range(2):
                nc.scalar.activation(ple_hi[q][:], ple_gate_raw[:, :, q * 512:(q + 1) * 512], ACT.Copy).then_inc(pg_hi, 1)

            def rms_of(i, ready, n, ssq_t, rms_t, done, scratch):
                act.wait_ge(ready, n)
                link(nc.scalar.activation(scratch, xr[:, i, :], ACT.Square, accum_out=ssq_t[:, i:i + 1]))
                nc.scalar.activation(rms_t[:, i:i + 1], ssq_t[:, i:i + 1], ACT.Sqrt, bias=eps[:], scale=1.0 / D).then_inc(done, 1)

            def stage6_a(i):
                rms_of(i, x2_ready, i + 1, ssq3, rms3, rms3_ready, yg[i][1][:])
                act.wait_ge(h3g_ready, i + 1)
                if i >= 2:
                    act.wait_ge(gate_done, 2 * (i - 1))
                nc.scalar.activation(h3T_hi[i % 2][:], h3g[:].rearrange("p (k t) -> p k t", k=KD), ACT.Copy).then_inc(h3_hi, 1)

            def stage6_b(i):
                for q in range(2):
                    act.wait_ge(gate_done, 2 * i + q + 1)
                    nc.scalar.activation(yg[i][0][:, q * 512:(q + 1) * 512], b_gate[i % 2][q][:], ACT.Sigmoid).then_inc(gate_ready, 1)
                rms_of(i, x3_ready, i + 1, ssq4, rms4, rms4_ready, yg[i][1][:])

            stage6_a(0)
            for i in range(NT):
                if i + 1 < NT:
                    stage6_a(i + 1)
                stage6_b(i)

        @block.vector
        def _(dve):
            chain = [0]
            V = nc.vector

            def link(ins):
                chain[0] += 1
                ins.then_inc(dve_chain, 1)
                dve.wait_ge(dve_chain, chain[0])

            def h2T_high(i):
                dve.wait_ge(h2_T, i + 1)
                V.tensor_copy(h2T[:, 4:8, i * P:(i + 1) * P],
                              b_score[2 * (i % 2) + 1][:].rearrange("p (k t) -> p k t", k=4)).then_inc(h2T_dve, 1)

            def route():
                def wide(t, n):
                    return t.unsqueeze(len(t.shape)).to_broadcast(list(t.shape) + [n])

                def all_tiles(t):
                    return t.unsqueeze(1).to_broadcast([P, NT, t.shape[-1]])

                def first_max(values, best, one_hot):
                    link(V.tensor_reduce(best[:], values, X, ALU.max))
                    link(V.tensor_tensor(eq[:], values, wide(best[:], 4), ALU.is_equal))
                    link(V.scalar_tensor_tensor(cand[:], eq[:], -64.0, all_tiles(iota4), ALU.mult, ALU.add))
                    link(V.tensor_reduce(cmin[:], cand[:], X, ALU.min))
                    link(V.tensor_tensor(one_hot[:], cand[:], wide(cmin[:], 4), ALU.is_equal))

                dve.wait_ge(lg_done, 1)
                link(V.tensor_copy(lg[:], b_mean[:, 0:NT * NR].rearrange("p (t c) -> p t c", t=NT)))
                first_max(lg[:, :, 0:N_GROUPS], gmax, oh_g)
                V.tensor_tensor(gsub[:], lg[:, :, 0:N_GROUPS], wide(gmax[:], 4), ALU.subtract).then_inc(gsub_ready, 1)
                link(V.tensor_tensor(picked[:], lg[:, :, N_GROUPS:NR].rearrange("p t (g j) -> p t g j", g=4),
                                     wide(oh_g[:], 4), ALU.mult))
                link(V.tensor_reduce(les[:], picked[:].rearrange("p t g j -> p t j g"), X, ALU.add))
                first_max(les[:], v_top[0], oh[0])
                link(V.scalar_tensor_tensor(les2[:], oh[0][:], MASKED, les[:], ALU.mult, ALU.add))
                first_max(les2[:], v_top[1], oh[1])
                V.tensor_tensor(vd[:], v_top[1][:], v_top[0][:], ALU.subtract).then_inc(vd_ready, 1)
                for k in range(TOP_K):
                    for g in range(N_GROUPS):
                        last = V.tensor_tensor(E[:, k, :, g, :], oh[k][:],
                                               oh_g[:, :, g:g + 1].to_broadcast([P, NT, 4]), ALU.mult)
                    link(last)
                Ef = E[:].rearrange("p k t g j -> p k t (g j)")
                link(V.tensor_tensor(member[:], Ef[:, 0], Ef[:, 1], ALU.add))
                link(V.memset(prefix[:, 0, :], 0.0))
                for i in range(NT):
                    link(V.tensor_tensor(prefix[:, i + 1, :], prefix[:, i, :], member[:, i, :], ALU.add))
                V.memset(one16[:], 1.0).then_inc(member_ready, 1)
                dve.wait_ge(gexp_ready, 1)
                link(V.tensor_reduce(gsum[:], gexp[:], X, ALU.add))
                link(V.reciprocal(g_w[:], gsum[:]))
                dve.wait_ge(ve_ready, 1)
                link(V.tensor_scalar(vs[:], ve[:], 1.0, None, ALU.add))
                link(V.reciprocal(vr[:], vs[:]))
                link(V.tensor_tensor(w_top[0][:], vr[:], g_w[:], ALU.mult))
                link(V.tensor_tensor(w_top[1][:], w_top[0][:], ve[:], ALU.mult))
                dve.wait_ge(rank_done, 1)
                link(V.tensor_copy(counts[:], b_o[:, NT * 16:NT * 16 + 16]))
                link(V.tensor_tensor(nb_gt[:], wide(counts[:], BPE),
                                     iota64.unsqueeze(1).to_broadcast([P, 16, BPE]), ALU.is_gt))
                link(V.tensor_reduce(nb[:], nb_gt[:], X, ALU.add))
                link(V.tensor_scalar(nb1[:], nb[:], 1.0, None, ALU.max))
                link(V.tensor_tensor_scan(cum[:], one16[:], nb1[:], 0.0, ALU.mult, ALU.add))
                link(V.tensor_tensor(first[:], cum[:], nb1[:], ALU.subtract))
                link(V.tensor_scalar(first64[:], first[:], float(BLK), None, ALU.mult))
                link(V.tensor_tensor(slots[:], b_o[:, 0:NT * 16].rearrange("p (t e) -> p t e", t=NT),
                                     first64[:].unsqueeze(1).to_broadcast([P, NT, 16]), ALU.add))
                for k in range(TOP_K):
                    link(V.tensor_tensor(slot_e[:, k], Ef[:, k], slots[:], ALU.mult))
                link(V.tensor_reduce(slot_f[:], slot_e[:], X, ALU.add))
                V.tensor_copy(slot_i[0][:], slot_f[:, 0, :])
                V.tensor_copy(slot_i[1][:], slot_f[:, 1, :]).then_inc(slot_ready, 1)
                link(V.tensor_copy(cum_i[:], cum[0:1, :]))
                link(V.tensor_tensor(blk_ge[:], iota_blk.unsqueeze(2).to_broadcast([1, 32, 16]),
                                     cum[0:1, :].unsqueeze(1).to_broadcast([1, 32, 16]), ALU.is_ge))
                link(V.tensor_reduce(blk_e[:], blk_ge[:], X, ALU.add))
                link(V.tensor_copy(blk_ei[:], blk_e[:]))
                link(V.tensor_scalar(blk_slot[:], blk_ei[:], 1, None, ALU.bitwise_and))
                link(V.tensor_scalar(blk_t[:], blk_ei[:], 1, None, ALU.logical_shift_right))
                link(V.tensor_scalar(blk_loads[:], blk_t[:], 1.0, None, ALU.add))
                V.sem_inc(table_ready, 1)

            def split_lo(u):
                if u >= 2:
                    dve.wait_ge(proj_done, outs_before(u - 1))
                dve.wait_ge(hi_done, u + 1)
                V.tensor_tensor(w_lo[u % 2][:], w_raw[u % 2][:], w_hi[u % 2][:].bitcast(F32),
                                ALU.subtract).then_inc(lo_done, 1)

            for i in range(NT):
                dve.wait_ge(x_ssq, i + 1)
                link(V.reciprocal(rstd[:, i:i + 1], rms[:, i:i + 1]))
                if i >= 2:
                    dve.wait_ge(xn_T, i - 1)
                V.tensor_scalar(xn[i % 2][:], xr[:, i, :], rstd[:, i:i + 1], None, ALU.mult).then_inc(xn_ready, 1)
                if i == 0:
                    dve.wait_ge(s_const, 16 * 9)
                    split_lo(0)
                dve.wait_ge(xn_T, i + 1)
                if i >= 1:
                    dve.wait_ge(h_hi, i)
                    dve.wait_ge(h_lo, i)
                for q in range(2):
                    last = V.tensor_tensor(hg[:, q * 512:(q + 1) * 512].rearrange("p (k t) -> p k t", k=4),
                                           b_score[2 * (i % 2) + q][:].rearrange("p (k t) -> p k t", k=4),
                                           gmix[:, 4 * q:4 * q + 4].unsqueeze(2).to_broadcast([P, 4, P]), ALU.mult)
                last.then_inc(hg_ready, 1)
                dve.wait_ge(h_hi, i + 1)
                V.tensor_tensor(hT_lo[:, :, i * P:(i + 1) * P], hg[:].rearrange("p (k t) -> p k t", k=KD),
                                hT_hi[:, :, i * P:(i + 1) * P].bitcast(F32), ALU.subtract).then_inc(h_lo, 1)
            split_lo(1)
            dve.wait_ge(s_lam, 64)
            for c in range(2):
                last = V.tensor_tensor_reduce(out=lam_junk[:, c, :], in0=lamv[:, 2 * c, :], in1=lamv[:, 2 * c + 1, :],
                                              scale=1.0, scalar=0.0, op0=ALU.mult, op1=ALU.add,
                                              accum_out=lam_dot[:, c:c + 1])
            last.then_inc(lam_ready, 1)
            dve.wait_ge(lam_exped, 1)
            link(V.tensor_tensor(neg_lam[:], lam_exp[:, 1:2], lam_exp[:, 0:1], ALU.subtract))
            link(V.tensor_scalar(neg_lam[:], neg_lam[:], LAM_INIT, None, ALU.subtract))
            V.tensor_scalar(subln8[:], subln[:], 1.0 - LAM_INIT, None, ALU.mult).then_inc(dve_chain, 1)
            chain[0] += 1
            dve.wait_ge(s_tab, 32)

            def scores(h, i):
                s, L = NT * h + i, P * (i + 1)
                dve.wait_ge(score_done, s + 1)
                for c in range(2):
                    last = V.tensor_tensor_reduce(
                        out=A[s % 2][:, c, 0:L], in0=b_score[2 * (i % 2) + c][:, 0:L],
                        in1=bias[:, h, SEQ - L:SEQ], scale=1.0, scalar=MASKED, op0=ALU.add, op1=ALU.max,
                        accum_out=row_max[s % 2][:, c:c + 1])
                last.then_inc(score_evac, 1)
                dve.wait_ge(score_evac, s + 1)
                V.tensor_scalar(neg_max[s % 2][:], row_max[s % 2][:], -1.0, None, ALU.mult).then_inc(max_ready, 1)

            def probs(h, i):
                s, L = NT * h + i, P * (i + 1)
                dve.wait_ge(exp_done, s + 1)
                link(V.reciprocal(rz[s % 2][:], z[s % 2][:]))
                link(V.tensor_tensor(rl[s % 2][:], rz[s % 2][:, 1:2], neg_lam[:], ALU.mult))
                link(V.tensor_scalar(A[s % 2][:, 1, 0:L], A[s % 2][:, 1, 0:L], rl[s % 2][:], None, ALU.mult))
                if h and i == 0:
                    dve.wait_ge(wT_done, h)
                V.scalar_tensor_tensor(W[i][:], A[s % 2][:, 0, 0:L], rz[s % 2][:, 0:1], A[s % 2][:, 1, 0:L],
                                       ALU.mult, ALU.add).then_inc(w_ready, 1)
                dve.wait_ge(w_ready, s + 1)

            def softmax(h):
                scores(h, 0)
                for i in range(1, NT):
                    scores(h, i)
                    probs(h, i - 1)
                probs(h, NT - 1)

            def decayed(r):
                for j in range(NT):
                    dve.wait_ge(ret_done, NT * r + j + 1)
                    if j == 0:
                        dve.wait_ge(o_done, HEADS + r - 1)
                    o, L = pT_off[j], SEQ - P * j
                    V.tensor_tensor(probsT[r % 2][:, o:o + L], b_score[j][:, 0:L], decay[:, r, 0:L],
                                    ALU.mult).then_inc(ret_ready, 1)

            def head_norm(n):
                dve.wait_ge(orms_ready, n + 1)
                if n >= 2:
                    dve.wait_ge(mix_hi, n - 1)
                h = n % HEADS
                link(V.reciprocal(orms[n % 2][:], orms[n % 2][:]))
                if n < HEADS:
                    V.scalar_tensor_tensor(onorm[n % 2][:], dqT[:, h, :], subln8[:], orms[n % 2][:], ALU.mult,
                                           ALU.mult).then_inc(onorm_ready, 1)
                else:
                    link(V.tensor_tensor(orms[n % 2][:], orms[n % 2][:], rgT[:, h, :], ALU.mult))
                    V.tensor_tensor(onorm[n % 2][:], rqT[:, h, :], orms[n % 2][:], ALU.mult).then_inc(onorm_ready, 1)
                dve.wait_ge(mix_hi, n + 1)
                V.tensor_tensor(mixT_lo[:, MIX_K[n], :], onorm[n % 2][:], mixT_hi[:, MIX_K[n], :].bitcast(F32),
                                ALU.subtract).then_inc(mix_lo, 1)
                dve.wait_ge(mix_lo, n + 1)

            for u in range(2, 9):
                split_lo(u)
            for h in range(HEADS):
                softmax(h)
                split_lo(9 + 2 * h)
                if h < HEADS - 1:
                    split_lo(10 + 2 * h)
            for r in range(HEADS):
                decayed(r)
                head_norm(r)
            for n in range(HEADS, 2 * HEADS):
                head_norm(n)

            for u in range(OUT_UNITS):
                for i in range(NT):
                    m = NT * u + i
                    dve.wait_ge(proj_done, P1_OUTS + m + 1)
                    part = xr[:, i, u * UC:(u + 1) * UC]
                    V.tensor_tensor(part, b_proj[(P1_OUTS + m) % 2][:, 0:UC], part, ALU.add).then_inc(x1_add, 1)
                    if u == OUT_UNITS - 1:
                        dve.wait_ge(x1_sq, m + 1)
                        V.tensor_reduce(sum2[:, i:i + 1], ssq2[:, i, :], X, ALU.add).then_inc(sum2_ready, 1)
                        dve.wait_ge(rms2_ready, i + 1)
                        link(V.reciprocal(rstd2[:, i:i + 1], rms2[:, i:i + 1]))
                        V.scalar_tensor_tensor(h2[:, i, :], xr[:, i, :], rstd2[:, i:i + 1], gffn[:], ALU.mult,
                                               ALU.mult).then_inc(h2_ready, 1)
                        if i:
                            h2T_high(i - 1)
                if u < 2:
                    split_lo(IN_UNITS + 2 + u)
            h2T_high(NT - 1)
            route()

            total = dve.value_load(cum_i[0:1, N_EXPERTS - 1:N_EXPERTS], min_val=N_EXPERTS, max_val=MAX_BLOCKS)
            dve.sem_inc(y_ready, 1)

            def hidden(b):
                dve.wait_ge(sg_ready, b + 1)
                V.tensor_tensor(hid[:], silu_g[:], b_gu[:, UC:2 * UC], ALU.mult).then_inc(hid_ready, 1)

            def hiddenT(b):
                dve.wait_ge(hT_done, b + 1)
                V.tensor_copy(hidT[:], b_hT[:, 0:256].rearrange("p (j q t) -> p j q t", j=2, q=2)).then_inc(hidT_ready, 1)

            def evacuate_y(b):
                dve.wait_ge(dn_done, b + 1)
                dve.wait_ge(y_free, b + 1)
                V.tensor_copy(y_blk[:], b_dn[:]).then_inc(y_ready, 1)

            hidden(0)
            with dve.Fori(1, MAX_BLOCKS) as b:
                with dve.If(b < total):
                    hiddenT(b - 1)
                    hidden(b)
                    evacuate_y(b - 1)
            hiddenT(total - 1)
            evacuate_y(total - 1)
            dve.wait_ge(s_rows, 32 * (total + 2))

            def stage6_a(i):
                dve.wait_ge(s_gather[i], 16 * TOP_K)
                link(V.scalar_tensor_tensor(xr[:, i, :], yg[i][0][:], w_top[0][:, i:i + 1], xr[:, i, :], ALU.mult, ALU.add))
                V.scalar_tensor_tensor(xr[:, i, :], yg[i][1][:], w_top[1][:, i:i + 1], xr[:, i, :], ALU.mult,
                                       ALU.add).then_inc(x2_ready, 1)
                dve.wait_ge(rms3_ready, i + 1)
                link(V.reciprocal(rstd3[:, i:i + 1], rms3[:, i:i + 1]))
                if i:
                    dve.wait_ge(h3_T, i)
                V.tensor_scalar(h3[:], xr[:, i, :], rstd3[:, i:i + 1], None, ALU.mult).then_inc(h3_ready, 1)
                dve.wait_ge(h3_T, i + 1)
                for q in range(2):
                    last = V.tensor_tensor(h3g[:, q * 512:(q + 1) * 512].rearrange("p (k t) -> p k t", k=4),
                                           b_score[2 * (i % 2) + q][:].rearrange("p (k t) -> p k t", k=4),
                                           gple[:, 4 * q:4 * q + 4].unsqueeze(2).to_broadcast([P, 4, P]), ALU.mult)
                last.then_inc(h3g_ready, 1)
                dve.wait_ge(h3_hi, i + 1)
                if i >= 2:
                    dve.wait_ge(gate_done, 2 * (i - 1))
                V.tensor_tensor(h3T_lo[i % 2][:], h3g[:].rearrange("p (k t) -> p k t", k=KD),
                                h3T_hi[i % 2][:].bitcast(F32), ALU.subtract).then_inc(h3_lo, 1)
                dve.wait_ge(h3_lo, i + 1)

            def stage6_b(i):
                dve.wait_ge(gate_ready, 2 * i + 2)
                link(V.tensor_tensor(yg[i][0][:], yg[i][0][:], ple[:, i, :], ALU.mult))
                V.tensor_tensor(xr[:, i, :], xr[:, i, :], yg[i][0][:], ALU.add).then_inc(x3_ready, 1)
                dve.wait_ge(rms4_ready, i + 1)
                link(V.reciprocal(rstd4[:, i:i + 1], rms4[:, i:i + 1]))
                if i:
                    dve.wait_ge(s_out, 16 * i)
                V.scalar_tensor_tensor(out_sb[:], xr[:, i, :], rstd4[:, i:i + 1], gfin[:], ALU.mult,
                                       ALU.mult).then_inc(res_ready, 1)

            for q in range(2):
                dve.wait_ge(pg_hi, q + 1)
                V.tensor_tensor(ple_lo[q][:], ple_gate_raw[:, :, q * 512:(q + 1) * 512], ple_hi[q][:].bitcast(F32),
                                ALU.subtract).then_inc(pg_lo, 1)
            stage6_a(0)
            for i in range(NT):
                if i + 1 < NT:
                    stage6_a(i + 1)
                stage6_b(i)

        @block.tensor
        def _(pe):
            T = nc.tensor

            def three_pass(o, w, m, chunks, w_of, m_of):
                for n, k in enumerate(chunks):
                    T.matmul(o, w_of(w[0], k), m_of(m[0], k), start=(n == 0), stop=False)
                    T.matmul(o, w_of(w[0], k), m_of(m[1], k), start=False, stop=False)
                    last = T.matmul(o, w_of(w[1], k), m_of(m[0], k), start=False, stop=(n == len(chunks) - 1))
                return last

            pe.wait_ge(s_const, 16 * 9)
            for i in range(NT):
                pe.wait_ge(xn_ready, i + 1)
                if i >= 2:
                    pe.wait_ge(hg_ready, i - 1)
                for k in range(KD):
                    last = T.transpose(b_score[2 * (i % 2) + k // 4][:, (k % 4) * P:(k % 4 + 1) * P],
                                       xn[i % 2][:, k * P:(k + 1) * P], ident)
                last.then_inc(xn_T, 1)
            pe.wait_ge(h_hi, NT)
            pe.wait_ge(h_lo, NT)

            def unit_part(u, j):
                n = outs_before(u) + j
                pe.wait_ge(hi_done, u + 1)
                pe.wait_ge(lo_done, u + 1)
                if n >= 2:
                    pe.wait_ge(proj_evac, n - 1)
                b = b_proj[n % 2]
                whl, hhl = (w_hi[u % 2], w_lo[u % 2]), (hT_hi, hT_lo)
                if u // 2 in NATURAL:
                    last = three_pass(b[:, 0:UC], hhl, whl, range(KD),
                                      lambda w, k: w[:, k, j * P:(j + 1) * P], lambda m, k: m[:, k, :])
                else:
                    last = three_pass(b[:], whl, hhl, range(KD),
                                      lambda w, k: w[:, k, j * P:(j + 1) * P], lambda m, k: m[:, k, :])
                last.then_inc(proj_done, 1)

            def unit(u):
                for j in range(unit_outs(u)):
                    unit_part(u, j)

            def scores(h):
                pe.wait_ge(proj_evac, outs_before(2 * DKEY + 2))
                for i in range(NT):
                    s, L = NT * h + i, P * (i + 1)
                    if h and i == 0:
                        pe.wait_ge(wT_ready, NT * h)
                    if s >= 2:
                        pe.wait_ge(score_evac, s - 1)
                    for c in range(2):
                        last = T.matmul(b_score[2 * (i % 2) + c][:, 0:L], dqT[64 * c:64 * c + 64, h, i * P:(i + 1) * P],
                                        dkT[64 * c:64 * c + 64, h, 0:L], start=True, stop=True)
                    last.then_inc(score_done, 1)

            def probs_transpose(h):
                pe.wait_ge(score_evac, NT * (h + 1))
                for i in range(NT):
                    pe.wait_ge(w_ready, NT * h + i + 1)
                    for j in range(i + 1):
                        last = T.transpose(b_score[j][:, i * P:(i + 1) * P], W[i][:, j * P:(j + 1) * P], ident)
                last.then_inc(wT_done, 1)

            def head_product(n):
                if n:
                    pe.wait_ge(o_evac, n)
                h, v = n % HEADS, dv if n < HEADS else rv
                for j in range(NT):
                    if n < HEADS:
                        pe.wait_ge(wT_ready, NT * h + j + 1)
                    else:
                        pe.wait_ge(ret_ready, NT * h + j + 1)
                    o = pT_off[j]
                    last = T.matmul(b_o[:, j * P:SEQ], v[:, j, h * P:(h + 1) * P],
                                    probsT[n % 2][:, o:o + SEQ - j * P], start=(j == 0), stop=(j == NT - 1))
                last.then_inc(o_done, 1)

            def ret_scores(r):
                if r == 0:
                    pe.wait_ge(proj_evac, P1_OUTS)
                    pe.wait_ge(wT_ready, NT * HEADS)
                for j in range(NT):
                    if r:
                        pe.wait_ge(ret_ready, NT * (r - 1) + j + 1)
                    T.matmul(b_score[j][:, 0:SEQ - j * P], rkT[:, r, j * P:(j + 1) * P],
                             rqT[:, r, j * P:SEQ], start=True, stop=True).then_inc(ret_done, 1)

            def head_mean(n):
                pe.wait_ge(osq_ready, n + 1)
                if n:
                    pe.wait_ge(orms_ready, n)
                T.matmul(b_mean[:], mean_w[:], osq[n % 2][:], start=True, stop=True).then_inc(mean_done, 1)

            pe.wait_ge(memsets, 4)
            for u in range(7):
                unit(u)
            for h in range(HEADS):
                scores(h)
                unit(7 + 2 * h)
                probs_transpose(h)
                if h < HEADS - 1:
                    unit_part(8 + 2 * h, 0)
                    head_product(h)
                    for j in range(1, unit_outs(8 + 2 * h)):
                        unit_part(8 + 2 * h, j)
            ret_scores(0)
            head_product(HEADS - 1)
            for r in range(HEADS):
                head_mean(r)
                if r < HEADS - 1:
                    ret_scores(r + 1)
                head_product(HEADS + r)
            for n in range(HEADS, 2 * HEADS):
                head_mean(n)

            for u in range(IN_UNITS, UNITS):
                pe.wait_ge(hi_done, u + 1)
                pe.wait_ge(lo_done, u + 1)
                for i in range(NT):
                    m = NT * (u - IN_UNITS) + i
                    if m == 0:
                        pe.wait_ge(proj_evac, P1_OUTS)
                        pe.wait_ge(mix_lo, 2 * HEADS)
                    if m >= 2:
                        pe.wait_ge(x1_add, m - 1)
                    three_pass(b_proj[(P1_OUTS + m) % 2][:, 0:UC], (mixT_hi, mixT_lo), (w_hi[u % 2], w_lo[u % 2]), MIX_K,
                               lambda w, k: w[:, k, i * P:(i + 1) * P], lambda t, k: t[:, k, :]).then_inc(proj_done, 1)

            def logits(i):
                pe.wait_ge(h2T_act, i + 1)
                pe.wait_ge(h2T_dve, i + 1)
                for k in range(KD):
                    last = T.matmul(b_o[0:NR, i * P:(i + 1) * P], w_r[:, k, :], h2T[:, k, i * P:(i + 1) * P],
                                    start=(k == 0), stop=(k == KD - 1))
                last.then_inc(lgT_done, 1)

            for i in range(NT):
                pe.wait_ge(h2_ready, i + 1)
                for k in range(KD):
                    last = T.transpose(b_score[2 * (i % 2) + k // 4][:, (k % 4) * P:(k % 4 + 1) * P],
                                       h2[:, i, k * P:(k + 1) * P], ident)
                last.then_inc(h2_T, 1)
                if i:
                    logits(i - 1)
            logits(NT - 1)
            pe.wait_ge(s_pple, 32)
            for c in range(D_PLE // P):
                for t in range(NT):
                    last = T.transpose(b_score[c][:, t * P:(t + 1) * P], p_sb[:, t, c * P:(c + 1) * P], ident)
                last.then_inc(p_T, 1)
            pe.wait_ge(lgT_ready, 1)
            for i in range(NT):
                last = T.transpose(b_mean[:, i * NR:(i + 1) * NR], lgT[:, i * P:(i + 1) * P], ident[0:NR, 0:NR])
            last.then_inc(lg_done, 1)

            def ple_product(n):
                t, q = n // 2, n % 2
                if n >= 2:
                    pe.wait_ge(ple_ready, n - 1)
                else:
                    pe.wait_ge(x1_add, NT * OUT_UNITS)
                for c in range(D_PLE // P):
                    last = T.matmul(b_proj[n % 2][:], pT[:, c, t * P:(t + 1) * P], ple_proj[:, c, q * 512:(q + 1) * 512],
                                    start=(c == 0), stop=(c == D_PLE // P - 1))
                last.then_inc(ple_done, 1)

            pe.wait_ge(pT_ready, 2)
            ple_product(0)
            ple_product(1)
            pe.wait_ge(member_ready, 1)
            T.matmul(b_o[:, 0:80], ones[:], prefix[:].rearrange("p i e -> p (i e)"), start=True, stop=False)
            T.matmul(b_o[:, 0:64], tri, member[:].rearrange("p i e -> p (i e)"), start=False, stop=True).then_inc(rank_done, 1)
            for n in range(2, 2 * NT):
                ple_product(n)

            pe.wait_ge(table_ready, 1)
            total = pe.value_load(cum_i[0:1, N_EXPERTS - 1:N_EXPERTS], min_val=N_EXPERTS, max_val=MAX_BLOCKS)

            def in_slot(b, products):
                loads = pe.value_load(blk_loads[0:1, bass.ds(b, 1)], min_val=1, max_val=N_EXPERTS // 2)
                slot = pe.value_load(blk_slot[0:1, bass.ds(b, 1)], min_val=0, max_val=1)
                with pe.If(slot < 1):
                    products(0, loads)
                with pe.Else():
                    products(1, loads)

            def rows_transpose(b):
                pe.wait_ge(s_rows, 32 * (b + 1))
                for j in range(4):
                    last = T.transpose(b_xT[:, j * P:(j + 1) * P], rows[:, j * P:(j + 1) * P], ident)
                last.then_inc(xT_done, 1)

            def gate_up(b):
                pe.wait_ge(xT_ready, b + 1)

                def products(s, loads):
                    pe.wait_ge(s_gu[s], 32 * loads)
                    for k in range(KD):
                        for q in range(2):
                            last = T.matmul(b_gu[q * BLK:(q + 1) * BLK, :], rowsT[:, k % 4, k // 4, :],
                                            ring_gu[s][:, k, :, q * UC:(q + 1) * UC],
                                            start=(k == 0), stop=(k == KD - 1))
                    last.then_inc(gu_done, 1)

                in_slot(b, products)

            def hidden_transpose(b):
                pe.wait_ge(hid_ready, b + 1)
                for j in range(2):
                    last = T.transpose(b_hT[:, j * P:(j + 1) * P], hid[:, j * P:(j + 1) * P], ident)
                last.then_inc(hT_done, 1)

            def down(b):
                pe.wait_ge(hidT_ready, b + 1)
                pe.wait_ge(y_ready, b + 1)

                def products(s, loads):
                    pe.wait_ge(s_dn[s], 16 * loads)
                    for kf in range(D_EXPERT // P):
                        for q in range(2):
                            last = T.matmul(b_dn[q * BLK:(q + 1) * BLK, :], hidT[:, kf % 2, kf // 2, :],
                                            ring_dn[s][:, kf, q * (D // 2):(q + 1) * (D // 2)],
                                            start=(kf == 0), stop=(kf == D_EXPERT // P - 1))
                    last.then_inc(dn_done, 1)

                in_slot(b, products)

            pe.wait_ge(ple_ready, 2 * NT)
            rows_transpose(0)
            gate_up(0)
            rows_transpose(1)
            with pe.Fori(1, MAX_BLOCKS) as b:
                with pe.If(b < total):
                    hidden_transpose(b - 1)
                    gate_up(b)
                    rows_transpose(b + 1)
                    down(b - 1)
            hidden_transpose(total - 1)
            down(total - 1)

            for i in range(NT):
                pe.wait_ge(h3_ready, i + 1)
                if i >= 2:
                    pe.wait_ge(h3g_ready, i - 1)
                for k in range(KD):
                    last = T.transpose(b_score[2 * (i % 2) + k // 4][:, (k % 4) * P:(k % 4 + 1) * P],
                                       h3[:, k * P:(k + 1) * P], ident)
                last.then_inc(h3_T, 1)
                pe.wait_ge(h3_hi, i + 1)
                pe.wait_ge(h3_lo, i + 1)
                for q in range(2):
                    pe.wait_ge(pg_lo, q + 1)
                    if i >= 2:
                        pe.wait_ge(gate_ready, 2 * (i - 2) + q + 1)
                    three_pass(b_gate[i % 2][q][:], (h3T_hi[i % 2], h3T_lo[i % 2]), (ple_hi[q], ple_lo[q]), range(KD),
                               lambda w, k: w[:, k, :], lambda m, k: m[:, k, :]).then_inc(gate_done, 1)


_INS = ["x", "p", "norm_mix", "w_in", "lam_q1", "lam_k1", "lam_q2", "lam_k2", "diff_subln", "w_out", "norm_ffn",
        "w_router_group", "b_router_group", "w_router_expert", "b_router_expert", "w_gate", "w_up", "w_down",
        "norm_ple", "w_ple_gate", "w_ple_proj", "norm_final"]
_LEADING = {"x": 1, "p": 2, "norm_final": 0}


def kernel(**inputs):
    import concourse.bacc as bacc
    from concourse.bass_utils import run_bass_kernel_spmd

    nc = bacc.Bacc("TRN2", target_bir_lowering=False, num_devices=1)
    arrays, args = {}, []
    for name in _INS:
        a = np.ascontiguousarray(inputs[name])
        a = a.reshape(a.shape[_LEADING.get(name, 1):])
        arrays[f"in_{name}"] = a
        args.append(nc.dram_tensor(f"in_{name}", a.shape, mybir.dt.from_np(a.dtype), kind="ExternalInput").ap())
    for name, a in zip(("decay", "bias", "small"), shape_constants()):
        arrays[f"const_{name}"] = a
        args.append(nc.dram_tensor(f"const_{name}", a.shape, F32, kind="ExternalInput").ap())
    args.append(nc.dram_tensor("out", (SEQ, D), F32, kind="ExternalOutput").ap())
    trunk(nc, *args)
    r = run_bass_kernel_spmd(nc, [arrays], core_ids=[0])
    return r.results[0]["out"].reshape(1, SEQ, D)
```

```python
from contextlib import ExitStack

import numpy as np

import concourse.bass as bass
from concourse import mybir

F32 = mybir.dt.float32
F32R = mybir.dt.float32r
I32 = mybir.dt.int32
U32 = mybir.dt.uint32
ALU = mybir.AluOpType
ACT = mybir.ActivationFunctionType
X = mybir.AxisListType.X

P = 128
SEQ, D = 512, 1024
NT = SEQ // P
KD = D // P
CHUNK = 64
HEADS = 4
DK = 128
EPS = 1e-6
LAM_INIT = 0.2
D_PLE = 256
N_GROUPS, PER_GROUP, N_EXPERTS, D_EXPERT = 4, 4, 16, 512
TOP_K = 2
NR = N_GROUPS + N_EXPERTS
BLK = 64
BPE = SEQ // BLK
MAX_BLOCKS = (TOP_K * SEQ - N_EXPERTS) // BLK + N_EXPERTS
TABLE = 34
HALF = D // 2
N_PAIRS = TOP_K * SEQ
UC = 256
QKV = 512
PARTS = [3072, 2048, 2560, 0, 512, 1024, 1536]
DV, DQ, DKEY, RQ, RK, RV, RG = range(7)
IN_UNITS = 2 * len(PARTS)
OUT_UNITS = D // UC
UNITS = IN_UNITS + OUT_UNITS
NATURAL = (DV, RV, RG)
MASKED = -1e30
RING = 3
PROJ_BANKS = 3


def unit_outs(u):
    return NT if u >= IN_UNITS or u // 2 in NATURAL else 2


def outs_before(u):
    return sum(unit_outs(v) for v in range(u))


def schedule():
    steps = []

    def outs(u, *js):
        steps.extend(("out", u, j) for j in js)

    for u in range(5):
        outs(u, *range(unit_outs(u)))
    outs(5, 0)
    steps.append(("scores", 0))
    outs(5, 1)
    outs(6, 0)
    steps.append(("weights", 0))
    outs(6, 1)
    steps.extend([("product", 0), ("scores", 1)])
    outs(7, 0, 1)
    steps.append(("weights", 1))
    outs(8, 0)
    steps.extend([("product", 1), ("scores", 2)])
    outs(8, 1)
    outs(9, 0)
    steps.append(("weights", 2))
    outs(9, 1)
    steps.extend([("product", 2), ("scores", 3)])
    outs(10, 0, 1, 2, 3)
    steps.append(("weights", 3))
    outs(11, 0, 1)
    steps.extend([("product", 3), ("scores", 4)])
    outs(11, 2, 3)
    outs(12, 0)
    steps.extend([("scores", 5), ("product", 4)])
    outs(12, 1, 2)
    steps.extend([("scores", 6), ("product", 5)])
    outs(12, 3)
    outs(13, 0)
    steps.extend([("scores", 7), ("product", 6), ("norm", -1)])
    outs(13, 1)
    steps.extend([("product", 7), ("mixT", 0)])
    outs(13, 2)
    steps.extend([("norm", 4), ("mixT", 1)])
    outs(13, 3)
    steps.extend([("norm", 5), ("mixT", 2), ("norm", 6), ("mixT", 3), ("norm", 7)])
    steps.extend(("mixT", q) for q in range(4, 8))
    return steps


MIX_ROWS = [4, 5, 6, 7, 0, 1, 2, 3]


def shape_constants():
    s = np.arange(P)[:, None]
    t = np.arange(SEQ)[None, :]
    decay = np.zeros((P, HEADS, SEQ), np.float32)
    bias = np.zeros((P, HEADS, SEQ), np.float32)
    for h in range(HEADS):
        log_g = np.log1p(-np.exp2(-5.0 - h))
        decay[:, h] = np.where(t >= s, np.exp(log_g * np.maximum(t - s, 0)), 0.0) * DK ** -0.5
        key = t - (SEQ - P)
        slope = 2.0 ** (-8.0 * (h + 1) / HEADS)
        allowed = (key // CHUNK) <= (s // CHUNK)
        bias[:, h] = np.where(allowed, -slope * np.abs(s - key), MASKED)
    k, i, tok = np.arange(TOP_K)[None, :, None], np.arange(NT)[None, None, :], s[:, :, None]
    src = np.broadcast_to(2 * (P * i + tok), (P, TOP_K, NT))
    dst = np.broadcast_to(2 * (SEQ * k + P * i + tok - N_PAIRS), (P, TOP_K, NT))
    half = np.broadcast_to(s // BLK, (P, TABLE))
    small = np.concatenate([
        np.eye(P),
        (s < np.arange(P)[None, :]).astype(float),
        np.tile(np.arange(PER_GROUP), (P, 1)),
        np.tile(np.arange(BPE) * BLK, (P, 1)),
        np.tile(np.arange(TABLE), (P, 1)),
        np.tile((np.arange(TABLE) + 1) * BLK, (P, 1)),
        np.tile(np.arange(RING, N_EXPERTS, RING), (P, 1)),
        np.tile(np.arange(P) % BLK, (P, 1)),
        np.stack([src, dst], 3).reshape(P, -1),
        np.concatenate([half, half + 2 * N_PAIRS], 1),
    ], 1).astype(np.float32)
    return decay.reshape(P, -1), bias.reshape(P, -1), small


def trunk(nc, x, p, norm_mix, w_in, lam_q1, lam_k1, lam_q2, lam_k2, diff_subln, w_out, norm_ffn,
          w_rg, b_rg, w_re, b_re, w_gate, w_up, w_down, norm_ple, w_ple_gate, w_ple_proj,
          norm_final, decay_tab, bias_tab, small_tab, out):
    ctx = ExitStack()
    with ctx:
        K = 1024
        base = -(-nc.sbuf_base // 32) * 32

        def at(name, kb, shape, dt=F32):
            return nc.alloc_sbuf_tensor_at(name, shape, dt, offset=base + int(kb * K))

        w_raw = [at(f"w_raw{i}", 8 * i, [P, KD, UC]) for i in range(2)]
        w_hi = [at(f"w_hi{i}", 16 + 8 * i, [P, KD, UC], F32R) for i in range(2)]
        w_lo = [at(f"w_lo{i}", 32 + 8 * i, [P, KD, UC], F32R) for i in range(2)]
        ple_proj = at("ple_proj", 16, [P, D_PLE // P, D])
        pT = at("pT", 24, [P, D_PLE // P, SEQ])
        p_sb = at("p_sb", 32, [P, NT, D_PLE])
        hT_hi = at("hT_hi", 48, [P, KD, SEQ], F32R)
        hT_lo = at("hT_lo", 108, [P, KD, SEQ], F32R)
        dkT = at("dkT", 64, [P, HEADS, SEQ])
        dv = at("dv", 72, [P, NT, QKV])
        mix_r = [at(f"mix_r{i}", 48 + 8 * i, [P, HEADS, SEQ], F32R) for i in range(2)]
        mix_d = [at(f"mix_d{i}", 64 + 8 * i, [P, HEADS, SEQ], F32R) for i in range(2)]
        ple = at("ple", 48, [P, NT, D])
        rows = [at(f"rows{i}", 64 + 2 * i, [P, D // 2]) for i in range(2)]
        rowsT = at("rowsT", 68, [P, 4, 2, BLK])
        silu_g = at("silu_g", 70, [P, UC])
        hid = at("hid", 71, [P, UC])
        hidT = at("hidT", 72, [P, 2, 2, BLK])
        y_blk = at("y_blk", 73, [P, D // 2])
        out_sb = at("out_sb", 76, [P, D])
        xr = at("xr", 80, [P, NT, D])
        small = at("small", 96, [P, 553])
        widths = [P, P, PER_GROUP, BPE, TABLE, TABLE, (N_EXPERTS - 1) // RING, P, 4 * NT, 2 * TABLE]
        starts = [sum(widths[:n]) for n in range(len(widths))]
        assert sum(widths) == 553
        (ident, tri, iota4, iota64, iota_blk, edges, iota_ring, slot_of_row, pair_rows,
         row_offset) = [small[:, a:a + w] for a, w in zip(starts, widths)]
        subln_b = at("subln_b", 98.25, [P, P])
        ones = at("ones", 98.75, [P, P])
        gffn = at("gffn", 99.25, [P, D])
        w_r = at("w_r", 103.25, [P, KD, NR])
        cur = [104.0]

        def tiny(name, shape, dt=F32):
            n = int(np.prod(shape[1:])) * 4
            t = at(name, cur[0], shape, dt)
            cur[0] += -(-n // 32) * 32 / K
            assert cur[0] <= 107.75
            return t

        gffn_k = tiny("gffn_k", [P, KD])
        gple = tiny("gple", [P, KD])
        b_r = tiny("b_r", [P, NR])
        warm = tiny("warm", [P, 1])
        ssqh = tiny("ssqh", [P, 2 * HEADS, NT])
        rmsh = tiny("rmsh", [P, 2 * HEADS, NT])
        rstdh = tiny("rstdh", [P, 2 * HEADS, NT])
        eps = tiny("eps", [P, 1])
        lam_dot = tiny("lam_dot", [P, 2])
        lam_exp = tiny("lam_exp", [P, 2])
        neg_lam = tiny("neg_lam", [P, 1])
        ssq = tiny("ssq", [P, NT])
        rms = tiny("rms", [P, NT])
        rstd = tiny("rstd", [P, NT])
        row_max = [tiny(f"row_max{i}", [P, 2]) for i in range(2)]
        neg_max = [tiny(f"neg_max{i}", [P, 2]) for i in range(2)]
        z = [tiny(f"z{i}", [P, 2]) for i in range(2)]
        rz = [tiny(f"rz{i}", [P, 2]) for i in range(2)]
        rl = [tiny(f"rl{i}", [P, 1]) for i in range(2)]
        ssq2 = tiny("ssq2", [P, NT, OUT_UNITS])
        sum2 = tiny("sum2", [P, NT])
        rms2 = tiny("rms2", [P, NT])
        rstd2 = tiny("rstd2", [P, NT])
        ssq3 = tiny("ssq3", [P, NT])
        rms3 = tiny("rms3", [P, NT])
        rstd3 = tiny("rstd3", [P, NT])
        ssq4 = tiny("ssq4", [P, NT, 2])
        sum4 = tiny("sum4", [P, NT])
        rms4 = tiny("rms4", [P, NT])
        rstd4 = tiny("rstd4", [P, NT])
        w_top = [tiny(f"w_top{k}", [P, NT]) for k in range(2)]
        src_row = tiny("src_row", [P, TABLE], I32)
        dst_row = tiny("dst_row", [P, TABLE], I32)
        src_now = [tiny(f"src_now{i}", [P, 1], I32) for i in range(2)]
        dst_now = [tiny(f"dst_now{i}", [P, 1], I32) for i in range(3)]
        cum_i = tiny("cum_i", [1, N_EXPERTS + 1], I32)
        blk_slot = tiny("blk_slot", [1, 32], I32)
        blk_loads = tiny("blk_loads", [1, 32], I32)
        dqT = at("dqT", 124, [P, HEADS, SEQ])
        rqT = at("rqT", 132, [P, HEADS, SEQ])
        rkT = at("rkT", 140, [P, HEADS, SEQ])
        rv = at("rv", 148, [P, NT, QKV])
        rg = at("rg", 156, [P, NT, QKV])
        dest = {DQ: dqT, DKEY: dkT, DV: dv, RQ: rqT, RK: rkT, RV: rv, RG: rg}
        decay = at("decay", 164, [P, HEADS, SEQ])
        bias = at("bias", 172, [P, HEADS, SEQ])
        xn = [at(f"xn{i}", 180 + 4 * i, [P, D]) for i in range(2)]
        gmix = at("gmix", 188, [P, D])
        junk = at("junk", 196, [P, D])
        A = [at(f"A{i}", 180 + 4 * i, [P, 2, SEQ]) for i in range(2)]
        W = [at(f"W{i}", 188 + 0.5 * (i * (i + 1) // 2), [P, P * (i + 1)]) for i in range(NT)]
        pT_off = [0, 512, 896, 1152]
        probsT = [at(f"probsT{i}", 193 + 5 * i, [P, 1280]) for i in range(2)]
        sq_head = at("sq_head", 203.75, [P, NT, P])
        sq_x1 = at("sq_x1", 205.75, [P, UC])
        lamv = at("lamv", 205.75, [P, 4, 64])
        lam_junk = at("lam_junk", 206.75, [P, 2, 64])
        gfin = at("gfin", 203.75, [P, D])
        RING_AT = [107.75, 155.75, 0]
        ring_gu = [at(f"ring_gu{i}", RING_AT[i], [P, KD, 2, D_EXPERT]) for i in range(RING)]
        ring_dn = [at(f"ring_dn{i}", RING_AT[i] + 32, [P, D_EXPERT // P, D]) for i in range(RING)]
        h2 = at("h2", 187.75, [P, NT, D])
        x1T = at("x1T", 155.75, [P, KD, SEQ])
        r0 = [32.0]

        def routing(name, shape, dt=F32):
            t = at(name, 36 + r0[0] - 32.0, shape, dt)
            r0[0] += -(-int(np.prod(shape[1:])) * 4 // 32) * 32 / K
            assert r0[0] <= 40
            return t

        ple_gate_raw = at("ple_gate_raw", 155.75, [P, KD, D])
        ple_hi = [at(f"ple_hi{i}", 16 * i, [P, KD, D // 2], F32R) for i in range(2)]
        ple_lo = [at("ple_lo0", 32, [P, KD, D // 2], F32R), at("ple_lo1", 187.75, [P, KD, D // 2], F32R)]
        yg = [[at(f"yg{i}_{k}", 108 + 8 * i + 4 * k, [P, D]) for k in range(2)] for i in range(NT)]
        x2T_hi = [at(f"x2T_hi{i}", 140 + 8 * i, [P, KD, P], F32R) for i in range(2)]
        x2T_lo = [at(f"x2T_lo{i}", 144 + 8 * i, [P, KD, P], F32R) for i in range(2)]

        lg = routing("lg", [P, NT, NR])
        gmax = routing("gmax", [P, NT])
        eq = routing("eq", [P, NT, 4])
        cand = routing("cand", [P, NT, 4])
        cmin = routing("cmin", [P, NT])
        oh_g = routing("oh_g", [P, NT, 4])
        gsub = routing("gsub", [P, NT, 4])
        gexp = routing("gexp", [P, NT, 4])
        gsum = routing("gsum", [P, NT])
        g_w = routing("g_w", [P, NT])
        picked = routing("picked", [P, NT, 4, 4])
        les = routing("les", [P, NT, 4])
        les2 = routing("les2", [P, NT, 4])
        v_top = [routing(f"v_top{k}", [P, NT]) for k in range(2)]
        oh = [routing(f"oh{k}", [P, NT, 4]) for k in range(2)]
        vd = routing("vd", [P, NT])
        ve = routing("ve", [P, NT])
        vs = routing("vs", [P, NT])
        vr = routing("vr", [P, NT])
        E = at("E", 42, [P, 2, NT, 4, 4])
        member = at("member", 42.5, [P, NT, 16])
        prefix = at("prefix", 42.75, [P, 5, 16])
        counts = at("counts", 43.25, [P, 16])
        nb_gt = at("nb_gt", 43.5, [P, 16, BPE])
        nb = at("nb", 44, [P, 16])
        nb1 = at("nb1", 44.125, [P, 16])
        one16 = at("one16", 44.25, [P, 16])
        cum = at("cum", 44.375, [P, 16])
        first = at("first", 44.5, [P, 16])
        first64 = at("first64", 44.625, [P, 16])
        slots = at("slots", 44.75, [P, NT, 16])
        slot_e = at("slot_e", 45, [P, 2, NT, 16])
        slot_f = at("slot_f", 45.5, [P, 2, NT])
        past_edge = at("past_edge", 0, [P, 2 * NT, TABLE])
        blk_f = at("blk_f", 1.25, [P, 2 * NT])
        in_blk = at("in_blk", 1.5, [P, 2 * NT])
        blk_oh = at("blk_oh", 2, [P, 2 * NT, TABLE])
        blk_rows = at("blk_rows", 4, [P, 2 * NT, 2, TABLE])
        slot_oh = at("slot_oh", 8, [P, 2 * NT, P])
        rows_f = at("rows_f", 12, [P, 2 * TABLE])
        blk_ge = at("blk_ge", 46, [1, 32, 16])
        blk_e = at("blk_e", 45.75, [1, 32])
        blk_rge = at("blk_rge", 43.25, [1, 32, 5])
        blk_q = at("blk_q", 45.875, [1, 32])

        h2_rows = nc.dram_tensor("h2_rows", [2 * SEQ, HALF], F32, kind="Internal").ap()
        y_rows = nc.dram_tensor("y_rows", [2 * N_PAIRS + 2, HALF], F32, kind="Internal").ap()

        bank = [ctx.enter_context(nc.psum_tensor(f"bank{i}", [P, 512], F32)) for i in range(8)]
        b_proj = [bank[0], bank[1], bank[7]]
        b_score = bank[2:6]
        b_o = bank[6]
        b_rank = bank[5]
        b_gu, b_dn, b_xT, b_hT = bank[0], bank[1], bank[2], bank[3]
        b_gate = [bank[0:2], bank[6:8]]

        def sem(name):
            return ctx.enter_context(nc.semaphore(name))

        s_x = [sem(f"x_loaded{i}") for i in range(NT)]
        s_const = sem("constants_loaded")
        s_late = sem("late_constants_loaded")
        s_tab = sem("tables_loaded")
        s_lam = sem("lambda_vectors_loaded")
        s_raw = [sem(f"unit_loaded{i}") for i in range(2)]
        s_h2 = sem("h2_stored")
        s_gu = [sem(f"gate_up_loaded{i}") for i in range(RING)]
        s_dn = [sem(f"down_loaded{i}") for i in range(RING)]
        s_pple = sem("ple_inputs_loaded")
        s_plegate = sem("ple_gate_loaded")
        s_rows = [sem(f"block_rows_loaded{i}") for i in range(2)]
        s_ystored = sem("block_out_stored")
        s_gather = [sem(f"expert_rows_gathered{i}") for i in range(NT)]
        s_out = sem("out_stored")

        dve_chain = sem("dve_chain")
        act_chain = sem("act_chain")
        memsets = sem("memsets_done")
        column_ready = sem("table_column_ready")
        gathers_begun = sem("gathers_begun")
        scatters_begun = sem("scatters_begun")
        x_ssq = sem("x_rms_ready")
        xn_ready = sem("xn_ready")
        xn_T = sem("xn_transposed")
        h_hi = sem("h_hi_ready")
        h_lo = sem("h_lo_ready")
        hi_done = sem("unit_hi_ready")
        lo_done = sem("unit_lo_ready")
        proj_done = sem("proj_done")
        proj_evac = sem("proj_evacuated")
        lam_ready = sem("lam_dots_ready")
        lam_exped = sem("lam_exp_ready")
        score_done = sem("scores_ready")
        score_evac = sem("scores_evacuated")
        max_ready = sem("row_max_ready")
        exp_done = sem("exp_ready")
        w_ready = sem("probs_ready")
        wT_done = sem("probs_transposed")
        wT_ready = sem("probsT_ready")
        ret_done = sem("ret_scores_ready")
        ret_ready = sem("ret_scoresT_ready")
        o_done = sem("head_out_ready")
        o_evac = sem("head_out_evacuated")
        o_sq = sem("head_squares_ready")
        orms_ready = sem("head_rms_ready")
        onorm_ready = sem("head_normed")
        mixT_done = sem("mix_transposed")
        mix_hi = sem("mix_hi_ready")
        mix_lo = sem("mix_lo_ready")
        x1_add = sem("x1_added")
        x1_sq = sem("x1_squares_ready")
        sum2_ready = sem("x1_sum_ready")
        rms2_ready = sem("x1_rms_ready")
        h2_ready = sem("h2_ready")
        x1_T = sem("x1_transposed")
        x1T_ready = sem("x1T_ready")
        wr_ready = sem("router_weights_scaled")
        lg_done = sem("logits_done")
        gsub_ready = sem("group_logits_shifted")
        gexp_ready = sem("group_exp_ready")
        vd_ready = sem("expert_logit_gap_ready")
        ve_ready = sem("expert_exp_ready")
        member_ready = sem("members_ready")
        rank_done = sem("ranks_ready")
        slot_oh_ready = sem("slot_one_hots_ready")
        rows_done = sem("slot_rows_summed")
        table_ready = sem("block_tables_ready")
        p_T = sem("p_transposed")
        pT_ready = sem("pT_ready")
        ple_done = sem("ple_product_ready")
        ple_ready = sem("ple_evacuated")
        xT_done = sem("rows_transposed")
        xT_ready = sem("rowsT_ready")
        gu_done = sem("gate_up_done")
        sg_ready = sem("silu_ready")
        hid_ready = sem("hidden_ready")
        hT_done = sem("hidden_transposed")
        hidT_ready = sem("hiddenT_ready")
        dn_done = sem("down_done")
        dn_bank_free = sem("down_bank_free")
        y_ready = sem("block_out_ready")
        pg_hi = sem("ple_gate_hi_ready")
        pg_lo = sem("ple_gate_lo_ready")
        x2_ready = sem("x2_ready")
        rms3_ready = sem("x2_rms_ready")
        x2_T = sem("x2_transposed")
        rstd3_ready = sem("x2_rstd_ready")
        x3_sq = sem("x3_squares_ready")
        sum4_ready = sem("x3_sum_ready")
        x2_hi = sem("x2_hi_ready")
        x2_lo = sem("x2_lo_ready")
        gate_done = sem("ple_gate_logits_ready")
        gate_ready = sem("ple_gate_ready")
        x3_ready = sem("x3_ready")
        rms4_ready = sem("x3_rms_ready")
        res_ready = sem("result_ready")

        def mix_of(part, q):
            return (mix_d if q < HEADS else mix_r)[part][:, q % HEADS, :]

        def o_of(n):
            return (dqT if n < HEADS else rqT)[:, n % HEADS, :].rearrange("p (t c) -> p t c", t=NT)

        P1_OUTS = outs_before(IN_UNITS)
        block = ctx.enter_context(nc.Block())

        @block.sync
        def _(sp):
            w_in_v = w_in.rearrange("(k p) n -> p k n", p=P)
            w_out_v = w_out.rearrange("(k p) n -> p k n", p=P)

            def load_unit(u):
                if u >= 2:
                    sp.wait_ge(hi_done, u - 1)
                    sp.wait_ge(lo_done, u - 1)
                if u < IN_UNITS:
                    c = PARTS[u // 2] + UC * (u % 2)
                    src = w_in_v[:, :, c:c + UC]
                else:
                    c = UC * (u - IN_UNITS)
                    src = w_out_v[:, :, c:c + UC]
                sp.dma_start(w_raw[u % 2][:], src).then_inc(s_raw[u % 2], 16)

            for i in range(NT):
                sp.dma_start(xr[:, i, :], x[i * P:(i + 1) * P, :]).then_inc(s_x[i], 16)
            load_unit(0)
            load_unit(1)
            for n, v in enumerate((lam_q1, lam_k1, lam_q2, lam_k2)):
                sp.dma_start(lamv[:, n, :], v.rearrange("(o n) -> o n", o=1).to_broadcast([P, 64])).then_inc(s_lam, 16)
            sp.dma_start(subln_b[:], diff_subln.rearrange("(o n) -> o n", o=1).to_broadcast([P, P])).then_inc(s_late, 16)
            sp.dma_start(gple[:], norm_ple.rearrange("(k p) -> p k", p=P),
                         allow_slow_non_contiguous=True).then_inc(s_late, 16)
            sp.dma_start(gffn_k[:], norm_ffn.rearrange("(k p) -> p k", p=P),
                         allow_slow_non_contiguous=True).then_inc(s_late, 16)
            sp.dma_start(gffn[:], norm_ffn.rearrange("(o n) -> o n", o=1).to_broadcast([P, D])).then_inc(s_late, 16)
            sp.dma_start(w_r[:, :, 0:N_GROUPS], w_rg.rearrange("(k p) n -> p k n", p=P)).then_inc(s_late, 16)
            sp.dma_start(w_r[:, :, N_GROUPS:NR], w_re.rearrange("(k p) n -> p k n", p=P)).then_inc(s_late, 16)
            sp.dma_start(b_r[:, 0:N_GROUPS], b_rg.rearrange("(o n) -> o n", o=1).to_broadcast([P, N_GROUPS])).then_inc(s_late, 16)
            sp.dma_start(b_r[:, N_GROUPS:NR], b_re.rearrange("(o n) -> o n", o=1).to_broadcast([P, N_EXPERTS])).then_inc(s_late, 16)
            load_unit(2)
            load_unit(3)
            sp.dma_start(bias[:], bias_tab.rearrange("p (h t) -> p h t", h=HEADS)).then_inc(s_tab, 16)
            sp.dma_start(decay[:], decay_tab.rearrange("p (h t) -> p h t", h=HEADS)).then_inc(s_tab, 16)
            for u in range(4, UNITS):
                load_unit(u)
            sp.wait_ge(mix_lo, 2 * HEADS)
            sp.wait_ge(mix_hi, 2 * HEADS)

            def load_gu(e, slot):
                sp.dma_start(ring_gu[slot][:, :, 0, :],
                             w_gate[bass.ds(e, 1)].rearrange("o (k p) f -> p (o k) f", p=P)).then_inc(s_gu[slot], 16)
                sp.dma_start(ring_gu[slot][:, :, 1, :],
                             w_up[bass.ds(e, 1)].rearrange("o (k p) f -> p (o k) f", p=P)).then_inc(s_gu[slot], 16)

            def load_dn(e, slot):
                sp.dma_start(ring_dn[slot][:],
                             w_down[bass.ds(e, 1)].rearrange("o (k p) f -> p (o k) f", p=P)).then_inc(s_dn[slot], 16)

            load_gu(0, 0)
            load_dn(0, 0)
            sp.wait_ge(x1_add, NT * (OUT_UNITS - 1))
            sp.dma_start(ple_proj[:], w_ple_proj.rearrange("(k p) n -> p k n", p=P)).then_inc(s_pple, 16)
            sp.dma_start(p_sb[:], p.rearrange("(t p) c -> p t c", p=P)).then_inc(s_pple, 16)
            for i in range(NT):
                sp.wait_ge(h2_ready, i + 1)
                sp.dma_start(h2_rows[2 * P * i:2 * P * (i + 1)].rearrange("(p q) c -> p (q c)", q=2),
                             h2[:, i, :]).then_inc(s_h2, 16)
            sp.wait_ge(lg_done, 1)
            load_gu(1, 1)
            sp.wait_ge(s_h2, 16 * NT)
            load_dn(1, 1)
            sp.wait_ge(ple_ready, 2 * NT)
            sp.wait_ge(table_ready, 1)
            load_gu(2, 2)
            load_dn(2, 2)
            sp.dma_start(gfin[:], norm_final.rearrange("(o n) -> o n", o=1).to_broadcast([P, D])).then_inc(s_plegate, 16)

            def blocks_through(e):
                return sp.value_load(cum_i[0:1, bass.ds(e, 1)], min_val=1, max_val=MAX_BLOCKS)

            def reload(e, slot):
                used = blocks_through(e - RING)
                sp.wait_ge(gu_done, used)
                load_gu(e, slot)
                sp.wait_ge(dn_done, used)
                load_dn(e, slot)

            with sp.Fori(0, N_EXPERTS // RING - 1) as turn:
                for slot in range(RING):
                    reload(RING * turn + (RING + slot), slot)
            reload(N_EXPERTS - 1, 0)
            sp.wait_ge(dn_done, blocks_through(N_EXPERTS - 3))
            sp.dma_start(ple_gate_raw[:], w_ple_gate.rearrange("(k p) n -> p k n", p=P)).then_inc(s_plegate, 16)
            sp.wait_ge(s_ystored, 16 * blocks_through(N_EXPERTS - 1))
            for i in range(NT):
                for k in range(TOP_K):
                    r = 2 * (SEQ * k + P * i)
                    sp.dma_start(yg[i][k][:], y_rows[r:r + 2 * P].rearrange("(p q) c -> p (q c)", q=2)).then_inc(s_gather[i], 16)
            for i in range(NT):
                for q in range(2):
                    sp.wait_ge(res_ready, 2 * i + q + 1)
                    sp.dma_start(out[i * P:(i + 1) * P, q * HALF:(q + 1) * HALF],
                                 out_sb[:, q * HALF:(q + 1) * HALF]).then_inc(s_out, 16)
            sp.wait_ge(s_out, 32 * NT)

        @block.gpsimd
        def _(pool):
            pool.memset(ones[:], 1.0).then_inc(memsets, 1)
            pool.memset(eps[:], EPS).then_inc(memsets, 1)
            pool.wait_ge(table_ready, 1)
            pool.wait_ge(s_h2, 16 * NT)
            total = pool.value_load(cum_i[0:1, N_EXPERTS - 1:N_EXPERTS], min_val=N_EXPERTS, max_val=MAX_BLOCKS)

            def column(now, table, b):
                c = slice(b, b + 1) if isinstance(b, int) else bass.ds(b, 1)
                pool.tensor_copy(now[:], table[:, c]).then_inc(column_ready, 1)
                return bass.IndirectOffsetOnAxis(ap=now[:].bitcast(U32), axis=0)

            def gather(b, par, n_columns):
                rows_of = column(src_now[par], src_row, b)
                pool.wait_ge(column_ready, n_columns)
                pool.sem_inc(gathers_begun, 1)
                pool.indirect_dma_start(out=rows[par][:], out_offset=None, in_=h2_rows,
                                        in_offset=rows_of).then_inc(s_rows[par], 16)

            def scatter(b, par, n_columns):
                rows_of = column(dst_now[par], dst_row, b)
                pool.wait_ge(column_ready, n_columns)
                pool.wait_ge(y_ready, b + 2)
                pool.sem_inc(scatters_begun, 1)
                pool.indirect_dma_start(out=y_rows, out_offset=rows_of, in_=y_blk[:],
                                        in_offset=None).then_inc(s_ystored, 16)

            gather(0, 0, 1)
            gather(1, 1, 2)
            pool.wait_ge(xT_done, 1)
            gather(2, 0, 3)
            with pool.Fori(0, (MAX_BLOCKS - 1) // 2) as pair:
                for half in range(2):
                    b = 2 * pair + (1 + half)
                    with pool.If(b < total):
                        pool.wait_ge(xT_done, b + 1)
                        gather(b + 2, 1 - half, 2 * b + 2)
                        scatter(b - 1, half, 2 * b + 3)
            scatter(total - 1, 2, 2 * total + 2)

        @block.scalar
        def _(act):
            chain = [0]

            def link(ins):
                chain[0] += 1
                ins.then_inc(act_chain, 1)
                act.wait_ge(act_chain, chain[0])

            act.dma_start(small[:], small_tab).then_inc(s_const, 16)
            act.dma_start(gmix[:], norm_mix.rearrange("(o n) -> o n", o=1).to_broadcast([P, D])).then_inc(s_const, 16)
            act.wait_ge(memsets, 2)
            link(nc.scalar.activation(warm[:], eps[:], ACT.Sqrt))

            def x_rms(i):
                act.wait_ge(s_x[i], 16)
                link(nc.scalar.activation(junk[:], xr[:, i, :], ACT.Square, accum_out=ssq[:, i:i + 1]))
                nc.scalar.activation(rms[:, i:i + 1], ssq[:, i:i + 1], ACT.Sqrt, bias=eps[:], scale=1.0 / D).then_inc(x_ssq, 1)

            def h_part(i):
                act.wait_ge(xn_T, i + 1)
                for q in range(2):
                    last = nc.scalar.activation(hT_hi[:, 4 * q:4 * q + 4, i * P:(i + 1) * P],
                                                b_score[2 * (i % 2) + q][:].rearrange("p (k t) -> p k t", k=4), ACT.Copy)
                last.then_inc(h_hi, 1)

            def split_hi(u):
                if u >= 2:
                    act.wait_ge(proj_done, outs_before(u - 1))
                act.wait_ge(s_raw[u % 2], 16 * (u // 2 + 1))
                nc.scalar.activation(w_hi[u % 2][:], w_raw[u % 2][:], ACT.Copy).then_inc(hi_done, 1)

            x_rms(0)
            x_rms(1)
            h_part(0)
            x_rms(2)
            h_part(1)
            x_rms(3)
            split_hi(0)
            h_part(2)
            h_part(3)
            split_hi(1)

            def evacuate(u, j):
                part, half = u // 2, u % 2
                n = outs_before(u) + j
                act.wait_ge(proj_done, n + 1)
                b = b_proj[n % PROJ_BANKS]
                if part in NATURAL:
                    o, i_ = dest[part][:, j, half * UC:(half + 1) * UC], b[:, 0:UC]
                else:
                    o, i_ = dest[part][:, 2 * half + j, :], b[:]
                if part == RG:
                    nc.scalar.activation(o, i_, ACT.Silu).then_inc(proj_evac, 1)
                else:
                    nc.scalar.activation(o, i_, ACT.Copy, scale=0.125 if part == DQ else 1.0).then_inc(proj_evac, 1)
                if j == unit_outs(u) - 1:
                    split_hi(u + 2)

            def exps(h):
                for i in range(NT):
                    s, L = NT * h + i, P * (i + 1)
                    act.wait_ge(max_ready, s + 1)
                    for c in range(2):
                        last = nc.scalar.activation(A[s % 2][:, c, 0:L], A[s % 2][:, c, 0:L], ACT.Exp,
                                                    bias=neg_max[s % 2][:, c:c + 1], accum_out=z[s % 2][:, c:c + 1])
                    last.then_inc(exp_done, 1)

            def probsT_evac(h):
                for j in range(NT):
                    act.wait_ge(wT_done, h + 1)
                    if h >= 2 and j == 0:
                        act.wait_ge(o_done, h - 1)
                    o = pT_off[j]
                    nc.scalar.activation(probsT[h % 2][:, o:o + SEQ - P * j], b_score[j][:, P * j:SEQ],
                                         ACT.Copy).then_inc(wT_ready, 1)

            def head_evac(n):
                act.wait_ge(o_done, n + 1)
                if n:
                    act.wait_ge(o_evac, n)
                ob = b_o[:].rearrange("p (t c) -> p t c", t=NT)
                for i in range(NT):
                    nc.scalar.activation(sq_head[:, i, :], ob[:, i, :], ACT.Square, accum_out=ssqh[:, n, i:i + 1])
                nc.scalar.activation(o_of(n), ob, ACT.Copy).then_inc(o_evac, 1)

            def head_rms(n):
                heads = slice(0, HEADS) if n < 0 else slice(n, n + 1)
                act.wait_ge(o_evac, HEADS if n < 0 else n + 1)
                nc.scalar.activation(rmsh[:, heads, :], ssqh[:, heads, :], ACT.Sqrt, bias=eps[:],
                                     scale=1.0 / P).then_inc(orms_ready, 1)

            def mix_split_hi(q):
                act.wait_ge(mixT_done, q + 1)
                nc.scalar.activation(mix_of(0, q), b_score[q % 4][:], ACT.Copy).then_inc(mix_hi, 1)

            act.wait_ge(lam_ready, 1)
            nc.scalar.activation(lam_exp[:], lam_dot[:], ACT.Exp).then_inc(lam_exped, 1)
            for step, n, *j in schedule():
                if step == "out":
                    evacuate(n, *j)
                elif step == "scores" and n < HEADS:
                    exps(n)
                elif step == "weights":
                    probsT_evac(n)
                elif step == "product":
                    head_evac(n)
                elif step == "norm":
                    head_rms(n)
                elif step == "mixT":
                    mix_split_hi(n)

            def x1T_evac(m):
                u, i = m // NT, m % NT
                act.wait_ge(x1_T, m + 1)
                nc.scalar.activation(x1T[:, 2 * u:2 * u + 2, i * P:(i + 1) * P],
                                     b_score[m % 4][:, 0:UC].rearrange("p (k t) -> p k t", k=2), ACT.Copy).then_inc(x1T_ready, 1)

            for u in range(OUT_UNITS):
                for i in range(NT):
                    m = NT * u + i
                    act.wait_ge(x1_add, m + 1)
                    if m:
                        act.wait_ge(x1_sq, m)
                    nc.scalar.activation(sq_x1[:], xr[:, i, u * UC:(u + 1) * UC], ACT.Square,
                                         accum_out=ssq2[:, i, u:u + 1]).then_inc(x1_sq, 1)
                    if u == OUT_UNITS - 1:
                        act.wait_ge(sum2_ready, i + 1)
                        nc.scalar.activation(rms2[:, i:i + 1], sum2[:, i:i + 1], ACT.Sqrt, bias=eps[:],
                                             scale=1.0 / D).then_inc(rms2_ready, 1)
                    if m:
                        x1T_evac(m - 1)
                if u < 2:
                    split_hi(IN_UNITS + 2 + u)
            x1T_evac(NT * OUT_UNITS - 1)
            for c in range(D_PLE // P):
                act.wait_ge(p_T, c + 1)
                nc.scalar.activation(pT[:, c, :], b_score[c][:], ACT.Copy).then_inc(pT_ready, 1)
            act.wait_ge(gsub_ready, 1)
            nc.scalar.activation(gexp[:], gsub[:], ACT.Exp).then_inc(gexp_ready, 1)
            act.wait_ge(vd_ready, 1)
            nc.scalar.activation(ve[:], vd[:], ACT.Exp).then_inc(ve_ready, 1)
            for n in range(2 * NT):
                act.wait_ge(ple_done, n + 1)
                nc.scalar.activation(ple[:, n // 2, (n % 2) * 512:(n % 2) * 512 + 512], bank[n % 2][:],
                                     ACT.Copy).then_inc(ple_ready, 1)

            act.wait_ge(table_ready, 1)
            total = act.value_load(cum_i[0:1, N_EXPERTS - 1:N_EXPERTS], min_val=N_EXPERTS, max_val=MAX_BLOCKS)

            def rowsT_evac(b):
                act.wait_ge(xT_done, b + 1)
                nc.scalar.activation(rowsT[:], b_xT[:].rearrange("p (j q t) -> p j q t", j=4, q=2),
                                     ACT.Copy).then_inc(xT_ready, 1)

            def silu(b):
                act.wait_ge(gu_done, b + 1)
                nc.scalar.activation(silu_g[:], b_gu[:, 0:UC], ACT.Silu).then_inc(sg_ready, 1)

            rowsT_evac(0)
            silu(0)
            rowsT_evac(1)
            with act.Fori(1, MAX_BLOCKS) as b:
                with act.If(b < total):
                    act.wait_ge(hid_ready, b)
                    silu(b)
                    rowsT_evac(b + 1)

            act.wait_ge(s_plegate, 32)
            act.wait_ge(dn_done, act.value_load(cum_i[0:1, N_EXPERTS - 2:N_EXPERTS - 1], min_val=1, max_val=MAX_BLOCKS))
            for q in range(2):
                for k in range(KD):
                    last = nc.scalar.activation(ple_hi[q][:, k, :], ple_gate_raw[:, k, q * HALF:(q + 1) * HALF], ACT.Copy,
                                                scale=gple[:, k:k + 1])
                last.then_inc(pg_hi, 1)

            def stage6_a(i):
                act.wait_ge(x2_T, i + 1)
                if i >= 2:
                    act.wait_ge(gate_done, 2 * (i - 1))
                for q in range(2):
                    last = nc.scalar.activation(x2T_hi[i % 2][:, 4 * q:4 * q + 4, :],
                                                b_score[2 * (i % 2) + q][:].rearrange("p (k t) -> p k t", k=4), ACT.Copy)
                last.then_inc(x2_hi, 1)
                link(nc.scalar.activation(yg[i][1][:], xr[:, i, :], ACT.Square, accum_out=ssq3[:, i:i + 1]))
                nc.scalar.activation(rms3[:, i:i + 1], ssq3[:, i:i + 1], ACT.Sqrt, bias=eps[:], scale=1.0 / D).then_inc(rms3_ready, 1)

            def stage6_b(i):
                act.wait_ge(rstd3_ready, i + 1)
                for q in range(2):
                    act.wait_ge(gate_done, 2 * i + q + 1)
                    nc.scalar.activation(yg[i][0][:, q * HALF:(q + 1) * HALF], b_gate[i % 2][q][:], ACT.Sigmoid,
                                         scale=rstd3[:, i:i + 1]).then_inc(gate_ready, 1)
                for q in range(2):
                    act.wait_ge(x3_ready, 2 * i + q + 1)
                    nc.scalar.activation(yg[i][1][:, q * HALF:(q + 1) * HALF], xr[:, i, q * HALF:(q + 1) * HALF], ACT.Square,
                                         accum_out=ssq4[:, i, q:q + 1]).then_inc(x3_sq, 1)
                act.wait_ge(sum4_ready, i + 1)
                nc.scalar.activation(rms4[:, i:i + 1], sum4[:, i:i + 1], ACT.Sqrt, bias=eps[:], scale=1.0 / D).then_inc(rms4_ready, 1)

            stage6_a(0)
            for i in range(NT):
                if i + 1 < NT:
                    stage6_a(i + 1)
                stage6_b(i)

        @block.vector
        def _(dve):
            chain = [0]
            V = nc.vector

            def link(ins):
                chain[0] += 1
                ins.then_inc(dve_chain, 1)
                dve.wait_ge(dve_chain, chain[0])

            def route():
                def wide(t, n):
                    return t.unsqueeze(len(t.shape)).to_broadcast(list(t.shape) + [n])

                def all_tiles(t):
                    return t.unsqueeze(1).to_broadcast([P, NT, t.shape[-1]])

                def first_max(values, best, one_hot):
                    link(V.tensor_reduce(best[:], values, X, ALU.max))
                    link(V.tensor_tensor(eq[:], values, wide(best[:], 4), ALU.is_equal))
                    link(V.scalar_tensor_tensor(cand[:], eq[:], -64.0, all_tiles(iota4), ALU.mult, ALU.add))
                    link(V.tensor_reduce(cmin[:], cand[:], X, ALU.min))
                    link(V.tensor_tensor(one_hot[:], cand[:], wide(cmin[:], 4), ALU.is_equal))

                dve.wait_ge(lg_done, 1)
                link(V.tensor_tensor(lg[:], b_o[:, 0:NT * NR].rearrange("p (t c) -> p t c", t=NT), wide(rstd2[:], NR),
                                     ALU.mult))
                link(V.tensor_tensor(lg[:], lg[:], all_tiles(b_r[:]), ALU.add))
                first_max(lg[:, :, 0:N_GROUPS], gmax, oh_g)
                V.tensor_tensor(gsub[:], lg[:, :, 0:N_GROUPS], wide(gmax[:], 4), ALU.subtract).then_inc(gsub_ready, 1)
                link(V.tensor_tensor(picked[:], lg[:, :, N_GROUPS:NR].rearrange("p t (g j) -> p t g j", g=4),
                                     wide(oh_g[:], 4), ALU.mult))
                link(V.tensor_reduce(les[:], picked[:].rearrange("p t g j -> p t j g"), X, ALU.add))
                first_max(les[:], v_top[0], oh[0])
                link(V.scalar_tensor_tensor(les2[:], oh[0][:], MASKED, les[:], ALU.mult, ALU.add))
                first_max(les2[:], v_top[1], oh[1])
                V.tensor_tensor(vd[:], v_top[1][:], v_top[0][:], ALU.subtract).then_inc(vd_ready, 1)
                for k in range(TOP_K):
                    for g in range(N_GROUPS):
                        last = V.tensor_tensor(E[:, k, :, g, :], oh[k][:],
                                               oh_g[:, :, g:g + 1].to_broadcast([P, NT, 4]), ALU.mult)
                    link(last)
                Ef = E[:].rearrange("p k t g j -> p k t (g j)")
                link(V.tensor_tensor(member[:], Ef[:, 0], Ef[:, 1], ALU.add))
                link(V.memset(prefix[:, 0, :], 0.0))
                for i in range(NT):
                    link(V.tensor_tensor(prefix[:, i + 1, :], prefix[:, i, :], member[:, i, :], ALU.add))
                V.memset(one16[:], 1.0).then_inc(member_ready, 1)
                dve.wait_ge(gexp_ready, 1)
                link(V.tensor_reduce(gsum[:], gexp[:], X, ALU.add))
                link(V.reciprocal(g_w[:], gsum[:]))
                dve.wait_ge(ve_ready, 1)
                link(V.tensor_scalar(vs[:], ve[:], 1.0, None, ALU.add))
                link(V.reciprocal(vr[:], vs[:]))
                link(V.tensor_tensor(w_top[0][:], vr[:], g_w[:], ALU.mult))
                link(V.tensor_tensor(w_top[1][:], w_top[0][:], ve[:], ALU.mult))
                dve.wait_ge(rank_done, 1)
                link(V.tensor_copy(counts[:], b_rank[:, NT * 16:NT * 16 + 16]))
                link(V.tensor_tensor(nb_gt[:], wide(counts[:], BPE),
                                     iota64.unsqueeze(1).to_broadcast([P, 16, BPE]), ALU.is_gt))
                link(V.tensor_reduce(nb[:], nb_gt[:], X, ALU.add))
                link(V.tensor_scalar(nb1[:], nb[:], 1.0, None, ALU.max))
                link(V.tensor_tensor_scan(cum[:], one16[:], nb1[:], 0.0, ALU.mult, ALU.add))
                link(V.tensor_tensor(first[:], cum[:], nb1[:], ALU.subtract))
                link(V.tensor_scalar(first64[:], first[:], float(BLK), None, ALU.mult))
                link(V.tensor_tensor(slots[:], b_rank[:, 0:NT * 16].rearrange("p (t e) -> p t e", t=NT),
                                     first64[:].unsqueeze(1).to_broadcast([P, NT, 16]), ALU.add))
                for k in range(TOP_K):
                    link(V.tensor_tensor(slot_e[:, k], Ef[:, k], slots[:], ALU.mult))
                link(V.tensor_reduce(slot_f[:], slot_e[:], X, ALU.add))
                pairs = slot_f[:].rearrange("p k t -> p (k t)")

                def all_pairs(t):
                    return t.unsqueeze(1).to_broadcast([P, 2 * NT, t.shape[-1]])

                link(V.tensor_tensor(past_edge[:], wide(pairs, TABLE), all_pairs(edges), ALU.is_ge))
                link(V.tensor_reduce(blk_f[:], past_edge[:], X, ALU.add))
                V.scalar_tensor_tensor(in_blk[:], blk_f[:], -float(BLK), pairs, ALU.mult, ALU.add)
                link(V.tensor_tensor(blk_oh[:], wide(blk_f[:], TABLE), all_pairs(iota_blk), ALU.is_equal))
                V.tensor_tensor(slot_oh[:], wide(in_blk[:], P), all_pairs(slot_of_row), ALU.is_equal)
                V.tensor_tensor(blk_rows[:], blk_oh[:].unsqueeze(2).to_broadcast([P, 2 * NT, 2, TABLE]),
                                pair_rows.rearrange("p (n w) -> p n w", w=2).unsqueeze(3).to_broadcast([P, 2 * NT, 2, TABLE]),
                                ALU.mult).then_inc(slot_oh_ready, 1)
                V.tensor_copy(cum_i[:, 0:N_EXPERTS], cum[0:1, :])
                link(V.tensor_scalar(cum_i[:, N_EXPERTS:], cum[0:1, N_EXPERTS - 1:], -1.0, None, ALU.add))
                link(V.tensor_tensor(blk_ge[:], iota_blk[0:1, 0:32].unsqueeze(2).to_broadcast([1, 32, 16]),
                                     cum[0:1, :].unsqueeze(1).to_broadcast([1, 32, 16]), ALU.is_ge))
                link(V.tensor_reduce(blk_e[:], blk_ge[:], X, ALU.add))
                link(V.tensor_tensor(blk_rge[:], blk_e[:].unsqueeze(2).to_broadcast([1, 32, 5]),
                                     iota_ring[0:1].unsqueeze(1).to_broadcast([1, 32, 5]), ALU.is_ge))
                link(V.tensor_reduce(blk_q[:], blk_rge[:], X, ALU.add))
                link(V.scalar_tensor_tensor(blk_slot[:], blk_q[:], -float(RING), blk_e[:], ALU.mult, ALU.add))
                V.tensor_scalar(blk_loads[:], blk_q[:], 1.0, None, ALU.add)
                dve.wait_ge(rows_done, 1)
                link(V.tensor_tensor(rows_f[:], b_rank[:, P:P + 2 * TABLE], row_offset, ALU.add))
                V.tensor_copy(src_row[:], rows_f[:, 0:TABLE])
                link(V.tensor_copy(dst_row[:], rows_f[:, TABLE:2 * TABLE]))
                V.sem_inc(table_ready, 1)

            def split_lo(u):
                if u >= 2:
                    dve.wait_ge(proj_done, outs_before(u - 1))
                dve.wait_ge(hi_done, u + 1)
                V.tensor_tensor(w_lo[u % 2][:], w_raw[u % 2][:], w_hi[u % 2][:].bitcast(F32),
                                ALU.subtract).then_inc(lo_done, 1)

            def normed(i):
                dve.wait_ge(x_ssq, i + 1)
                link(V.reciprocal(rstd[:, i:i + 1], rms[:, i:i + 1]))
                if i >= 2:
                    dve.wait_ge(xn_T, i - 1)
                V.scalar_tensor_tensor(xn[i % 2][:], xr[:, i, :], rstd[:, i:i + 1], gmix[:], ALU.mult,
                                       ALU.mult).then_inc(xn_ready, 1)

            def h_rest(i):
                dve.wait_ge(h_hi, i + 1)
                for q in range(2):
                    part = slice(4 * q, 4 * q + 4), slice(i * P, (i + 1) * P)
                    last = V.tensor_tensor(hT_lo[:, part[0], part[1]],
                                           b_score[2 * (i % 2) + q][:].rearrange("p (k t) -> p k t", k=4),
                                           hT_hi[:, part[0], part[1]].bitcast(F32), ALU.subtract)
                last.then_inc(h_lo, 1)

            dve.wait_ge(s_const, 16 * 2)
            normed(0)
            normed(1)
            h_rest(0)
            normed(2)
            h_rest(1)
            normed(3)
            split_lo(0)
            h_rest(2)
            h_rest(3)
            split_lo(1)
            dve.wait_ge(s_lam, 64)
            for c in range(2):
                last = V.tensor_tensor_reduce(out=lam_junk[:, c, :], in0=lamv[:, 2 * c, :], in1=lamv[:, 2 * c + 1, :],
                                              scale=1.0, scalar=0.0, op0=ALU.mult, op1=ALU.add,
                                              accum_out=lam_dot[:, c:c + 1])
            last.then_inc(lam_ready, 1)
            dve.wait_ge(lam_exped, 1)
            link(V.tensor_tensor(neg_lam[:], lam_exp[:, 1:2], lam_exp[:, 0:1], ALU.subtract))
            link(V.tensor_scalar(neg_lam[:], neg_lam[:], LAM_INIT, None, ALU.subtract))
            dve.wait_ge(s_late, 16 * 8)
            link(V.tensor_scalar(subln_b[:], subln_b[:], 1.0 - LAM_INIT, None, ALU.mult))
            V.tensor_tensor(w_r[:], w_r[:], gffn_k[:].unsqueeze(2).to_broadcast([P, KD, NR]), ALU.mult).then_inc(wr_ready, 1)
            dve.wait_ge(s_tab, 32)

            def scores(h, i):
                s, L = NT * h + i, P * (i + 1)
                dve.wait_ge(score_done, s + 1)
                for c in range(2):
                    last = V.tensor_tensor_reduce(
                        out=A[s % 2][:, c, 0:L], in0=b_score[2 * (i % 2) + c][:, 0:L],
                        in1=bias[:, h, SEQ - L:SEQ], scale=1.0, scalar=MASKED, op0=ALU.add, op1=ALU.max,
                        accum_out=row_max[s % 2][:, c:c + 1])
                last.then_inc(score_evac, 1)
                dve.wait_ge(score_evac, s + 1)
                V.tensor_scalar(neg_max[s % 2][:], row_max[s % 2][:], -1.0, None, ALU.mult).then_inc(max_ready, 1)

            def probs(h, i):
                s, L = NT * h + i, P * (i + 1)
                dve.wait_ge(exp_done, s + 1)
                link(V.reciprocal(rz[s % 2][:], z[s % 2][:]))
                link(V.tensor_tensor(rl[s % 2][:], rz[s % 2][:, 1:2], neg_lam[:], ALU.mult))
                link(V.tensor_scalar(A[s % 2][:, 1, 0:L], A[s % 2][:, 1, 0:L], rl[s % 2][:], None, ALU.mult))
                if h and i == 0:
                    dve.wait_ge(wT_done, h)
                V.scalar_tensor_tensor(W[i][:], A[s % 2][:, 0, 0:L], rz[s % 2][:, 0:1], A[s % 2][:, 1, 0:L],
                                       ALU.mult, ALU.add).then_inc(w_ready, 1)
                dve.wait_ge(w_ready, s + 1)

            def softmax(h):
                scores(h, 0)
                for i in range(1, NT):
                    scores(h, i)
                    probs(h, i - 1)
                probs(h, NT - 1)

            def decayed(r):
                for j in range(NT):
                    dve.wait_ge(ret_done, NT * r + j + 1)
                    if j == 0:
                        dve.wait_ge(o_done, HEADS + r - 1)
                    o, L = pT_off[j], SEQ - P * j
                    V.tensor_tensor(probsT[r % 2][:, o:o + L], b_score[j][:, 0:L], decay[:, r, 0:L],
                                    ALU.mult).then_inc(ret_ready, 1)

            def head_norm(n):
                heads = slice(0, HEADS) if n < 0 else slice(n, n + 1)
                dve.wait_ge(orms_ready, 1 if n < 0 else n - HEADS + 2)
                link(V.reciprocal(rstdh[:, heads, :], rmsh[:, heads, :]))
                if n >= HEADS:
                    dve.wait_ge(proj_evac, outs_before(2 * RG + 1 + (n - HEADS) // 2))
                for m in range(heads.start, heads.stop):
                    h = m % HEADS
                    for i in range(NT):
                        gain = subln_b[:] if n < 0 else rg[:, i, h * P:(h + 1) * P]
                        last = V.scalar_tensor_tensor(o_of(m)[:, i, :], o_of(m)[:, i, :], rstdh[:, m, i:i + 1], gain,
                                                      ALU.mult, ALU.mult)
                    last.then_inc(onorm_ready, 1)

            def mix_split_lo(q):
                dve.wait_ge(mix_hi, q + 1)
                V.tensor_tensor(mix_of(1, q), b_score[q % 4][:], mix_of(0, q).bitcast(F32), ALU.subtract).then_inc(mix_lo, 1)

            for step, n, *j in schedule():
                if step == "out" and j[0] == unit_outs(n) - 1:
                    split_lo(n + 2)
                elif step == "scores":
                    softmax(n) if n < HEADS else decayed(n - HEADS)
                elif step == "norm":
                    head_norm(n)
                elif step == "mixT":
                    mix_split_lo(n)

            for u in range(OUT_UNITS):
                for i in range(NT):
                    m = NT * u + i
                    dve.wait_ge(proj_done, P1_OUTS + m + 1)
                    part = xr[:, i, u * UC:(u + 1) * UC]
                    V.tensor_tensor(part, b_proj[(P1_OUTS + m) % PROJ_BANKS][:, 0:UC], part, ALU.add).then_inc(x1_add, 1)
                    if u == OUT_UNITS - 1:
                        dve.wait_ge(x1_sq, m + 1)
                        V.tensor_reduce(sum2[:, i:i + 1], ssq2[:, i, :], X, ALU.add).then_inc(sum2_ready, 1)
                        dve.wait_ge(rms2_ready, i + 1)
                        link(V.reciprocal(rstd2[:, i:i + 1], rms2[:, i:i + 1]))
                        V.scalar_tensor_tensor(h2[:, i, :], xr[:, i, :], rstd2[:, i:i + 1], gffn[:], ALU.mult,
                                               ALU.mult).then_inc(h2_ready, 1)
                if u < 2:
                    split_lo(IN_UNITS + 2 + u)
            route()

            total = dve.value_load(cum_i[0:1, N_EXPERTS - 1:N_EXPERTS], min_val=N_EXPERTS, max_val=MAX_BLOCKS)
            dve.sem_inc(y_ready, 1)

            def hidden(b):
                dve.wait_ge(sg_ready, b + 1)
                V.tensor_tensor(hid[:], silu_g[:], b_gu[:, UC:2 * UC], ALU.mult).then_inc(hid_ready, 1)

            def hiddenT(b):
                dve.wait_ge(hT_done, b + 1)
                V.tensor_copy(hidT[:], b_hT[:, 0:256].rearrange("p (j q t) -> p j q t", j=2, q=2)).then_inc(hidT_ready, 1)

            last_block = dve.value_load(cum_i[0:1, N_EXPERTS:], min_val=N_EXPERTS - 1, max_val=MAX_BLOCKS - 1)

            def evacuate_y(b, first=False):
                dve.wait_ge(dn_done, b + 1)
                if not first:
                    dve.wait_ge(s_ystored, 16 * b)
                V.tensor_copy(y_blk[:], b_dn[:]).then_inc(y_ready, 1)

            hidden(0)
            hiddenT(0)
            hidden(1)
            evacuate_y(0, first=True)
            with dve.Fori(1, MAX_BLOCKS - 1) as b:
                with dve.If(b + 1 < total):
                    hiddenT(b)
                    hidden(b + 1)
                    evacuate_y(b)

            def split_gate(q):
                dve.wait_ge(pg_hi, q + 1)
                for k in range(KD):
                    last = V.scalar_tensor_tensor(ple_lo[q][:, k, :], ple_gate_raw[:, k, q * HALF:(q + 1) * HALF],
                                                  gple[:, k:k + 1], ple_hi[q][:, k, :].bitcast(F32), ALU.mult, ALU.subtract)
                last.then_inc(pg_lo, 1)

            hiddenT(last_block)
            split_gate(0)
            evacuate_y(last_block)
            split_gate(1)

            def stage6_a(i):
                dve.wait_ge(s_gather[i], 16 * TOP_K)
                link(V.scalar_tensor_tensor(xr[:, i, :], yg[i][0][:], w_top[0][:, i:i + 1], xr[:, i, :], ALU.mult, ALU.add))
                V.scalar_tensor_tensor(xr[:, i, :], yg[i][1][:], w_top[1][:, i:i + 1], xr[:, i, :], ALU.mult,
                                       ALU.add).then_inc(x2_ready, 1)

            def stage6_split(i):
                dve.wait_ge(x2_hi, i + 1)
                for q in range(2):
                    last = V.tensor_tensor(x2T_lo[i % 2][:, 4 * q:4 * q + 4, :],
                                           b_score[2 * (i % 2) + q][:].rearrange("p (k t) -> p k t", k=4),
                                           x2T_hi[i % 2][:, 4 * q:4 * q + 4, :].bitcast(F32), ALU.subtract)
                last.then_inc(x2_lo, 1)
                dve.wait_ge(rms3_ready, i + 1)
                V.reciprocal(rstd3[:, i:i + 1], rms3[:, i:i + 1]).then_inc(rstd3_ready, 1)

            def stage6_b(i):
                for q in range(2):
                    half = slice(q * HALF, (q + 1) * HALF)
                    dve.wait_ge(gate_ready, 2 * i + q + 1)
                    link(V.tensor_tensor(yg[i][0][:, half], yg[i][0][:, half], ple[:, i, half], ALU.mult))
                    V.tensor_tensor(xr[:, i, half], xr[:, i, half], yg[i][0][:, half], ALU.add).then_inc(x3_ready, 1)
                dve.wait_ge(x3_sq, 2 * i + 2)
                V.tensor_tensor(sum4[:, i:i + 1], ssq4[:, i, 0:1], ssq4[:, i, 1:2], ALU.add).then_inc(sum4_ready, 1)
                dve.wait_ge(rms4_ready, i + 1)
                link(V.reciprocal(rstd4[:, i:i + 1], rms4[:, i:i + 1]))
                if i:
                    dve.wait_ge(s_out, 32 * i)
                for q in range(2):
                    half = slice(q * HALF, (q + 1) * HALF)
                    V.scalar_tensor_tensor(out_sb[:, half], xr[:, i, half], rstd4[:, i:i + 1], gfin[:, half], ALU.mult,
                                           ALU.mult).then_inc(res_ready, 1)

            for par in range(2):
                dve.wait_ge(s_rows[par], 16 * ((total + (3 - par)) // 2))
            stage6_a(0)
            stage6_split(0)
            for i in range(NT):
                if i + 1 < NT:
                    stage6_a(i + 1)
                    stage6_split(i + 1)
                stage6_b(i)

        @block.tensor
        def _(pe):
            T = nc.tensor

            def three_pass(o, w, m, chunks, w_of, m_of):
                for n, k in enumerate(chunks):
                    T.matmul(o, w_of(w[0], k), m_of(m[0], k), start=(n == 0), stop=False)
                    T.matmul(o, w_of(w[0], k), m_of(m[1], k), start=False, stop=False)
                    last = T.matmul(o, w_of(w[1], k), m_of(m[0], k), start=False, stop=(n == len(chunks) - 1))
                return last

            pe.wait_ge(s_const, 16 * 2)
            for i in range(NT):
                pe.wait_ge(xn_ready, i + 1)
                if i >= 2:
                    pe.wait_ge(h_lo, i - 1)
                for k in range(KD):
                    last = T.transpose(b_score[2 * (i % 2) + k // 4][:, (k % 4) * P:(k % 4 + 1) * P],
                                       xn[i % 2][:, k * P:(k + 1) * P], ident)
                last.then_inc(xn_T, 1)
            def unit_part(u, j):
                n = outs_before(u) + j
                pe.wait_ge(hi_done, u + 1)
                pe.wait_ge(lo_done, u + 1)
                if n >= PROJ_BANKS:
                    pe.wait_ge(proj_evac, n - PROJ_BANKS + 1)
                if n < NT:
                    pe.wait_ge(h_hi, n + 1)
                    pe.wait_ge(h_lo, n + 1)
                b = b_proj[n % PROJ_BANKS]
                whl, hhl = (w_hi[u % 2], w_lo[u % 2]), (hT_hi, hT_lo)
                if u // 2 in NATURAL:
                    last = three_pass(b[:, 0:UC], hhl, whl, range(KD),
                                      lambda w, k: w[:, k, j * P:(j + 1) * P], lambda m, k: m[:, k, :])
                else:
                    last = three_pass(b[:], whl, hhl, range(KD),
                                      lambda w, k: w[:, k, j * P:(j + 1) * P], lambda m, k: m[:, k, :])
                last.then_inc(proj_done, 1)

            def scores(h):
                pe.wait_ge(proj_evac, outs_before(2 * DKEY + 1 + h // 2))
                for i in range(NT):
                    s, L = NT * h + i, P * (i + 1)
                    if h and i == 0:
                        pe.wait_ge(wT_ready, NT * h)
                    if s >= 2:
                        pe.wait_ge(score_evac, s - 1)
                    for c in range(2):
                        last = T.matmul(b_score[2 * (i % 2) + c][:, 0:L], dqT[64 * c:64 * c + 64, h, i * P:(i + 1) * P],
                                        dkT[64 * c:64 * c + 64, h, 0:L], start=True, stop=True)
                    last.then_inc(score_done, 1)

            def probs_transpose(h):
                pe.wait_ge(score_evac, NT * (h + 1))
                for i in range(NT):
                    pe.wait_ge(w_ready, NT * h + i + 1)
                    for j in range(i + 1):
                        last = T.transpose(b_score[j][:, i * P:(i + 1) * P], W[i][:, j * P:(j + 1) * P], ident)
                last.then_inc(wT_done, 1)

            def head_product(n):
                if n:
                    pe.wait_ge(o_evac, n)
                h, v = n % HEADS, dv if n < HEADS else rv
                if n < HEADS:
                    pe.wait_ge(wT_ready, NT * (h + 1))
                else:
                    pe.wait_ge(ret_ready, NT * (h + 1))
                    pe.wait_ge(proj_evac, outs_before(2 * RV + 2))
                for i in range(NT):
                    for j in range(i + 1):
                        o = pT_off[j] + (i - j) * P
                        last = T.matmul(b_o[:, i * P:(i + 1) * P], probsT[n % 2][:, o:o + P],
                                        v[:, j, h * P:(h + 1) * P], start=(j == 0), stop=(j == i))
                last.then_inc(o_done, 1)

            def ret_scores(r):
                if r == 0:
                    pe.wait_ge(proj_evac, outs_before(2 * RK + 2))
                    pe.wait_ge(wT_ready, NT * HEADS)
                for j in range(NT):
                    if r:
                        pe.wait_ge(ret_ready, NT * (r - 1) + j + 1)
                    T.matmul(b_score[j][:, 0:SEQ - j * P], rkT[:, r, j * P:(j + 1) * P],
                             rqT[:, r, j * P:SEQ], start=True, stop=True).then_inc(ret_done, 1)

            def mix_transpose(q):
                pe.wait_ge(onorm_ready, q + 1)
                if q < 4:
                    pe.wait_ge(ret_ready, NT * HEADS)
                else:
                    pe.wait_ge(mix_lo, q - 3)
                for i in range(NT):
                    last = T.transpose(b_score[q % 4][:, i * P:(i + 1) * P], o_of(q)[:, i, :], ident)
                last.then_inc(mixT_done, 1)

            for step, n, *j in schedule():
                if step == "out":
                    unit_part(n, *j)
                elif step == "scores":
                    scores(n) if n < HEADS else ret_scores(n - HEADS)
                elif step == "weights":
                    probs_transpose(n)
                elif step == "product":
                    head_product(n)
                elif step == "mixT":
                    mix_transpose(n)

            def x1_transpose(m):
                u, i = m // NT, m % NT
                pe.wait_ge(x1_add, m + 1)
                if m >= 4:
                    pe.wait_ge(x1T_ready, m - 3)
                for c in range(2):
                    k = 2 * u + c
                    last = T.transpose(b_score[m % 4][:, c * P:(c + 1) * P], xr[:, i, k * P:(k + 1) * P], ident)
                last.then_inc(x1_T, 1)

            for u in range(IN_UNITS, UNITS):
                pe.wait_ge(hi_done, u + 1)
                pe.wait_ge(lo_done, u + 1)
                for i in range(NT):
                    m = NT * (u - IN_UNITS) + i
                    if m == 0:
                        pe.wait_ge(proj_evac, P1_OUTS)
                        pe.wait_ge(mix_lo, 2 * HEADS)
                    if m >= PROJ_BANKS:
                        pe.wait_ge(x1_add, m - PROJ_BANKS + 1)
                    three_pass(b_proj[(P1_OUTS + m) % PROJ_BANKS][:, 0:UC], (0, 1), (w_hi[u % 2], w_lo[u % 2]), range(KD),
                               lambda part, q: mix_of(part, q)[:, i * P:(i + 1) * P],
                               lambda t, q: t[:, MIX_ROWS[q], :]).then_inc(proj_done, 1)
                    if m:
                        x1_transpose(m - 1)
            x1_transpose(NT * OUT_UNITS - 1)

            pe.wait_ge(wr_ready, 1)
            for i in range(NT):
                pe.wait_ge(x1T_ready, NT * (OUT_UNITS - 1) + i + 1)
                for k in range(KD):
                    last = T.matmul(b_o[:, i * NR:(i + 1) * NR], x1T[:, k, i * P:(i + 1) * P], w_r[:, k, :],
                                    start=(k == 0), stop=(k == KD - 1))
            last.then_inc(lg_done, 1)
            pe.wait_ge(s_pple, 32)
            for c in range(D_PLE // P):
                for t in range(NT):
                    last = T.transpose(b_score[c][:, t * P:(t + 1) * P], p_sb[:, t, c * P:(c + 1) * P], ident)
                last.then_inc(p_T, 1)

            def ple_product(n):
                t, q = n // 2, n % 2
                if n >= 2:
                    pe.wait_ge(ple_ready, n - 1)
                else:
                    pe.wait_ge(x1_add, NT * OUT_UNITS)
                for c in range(D_PLE // P):
                    last = T.matmul(bank[n % 2][:], pT[:, c, t * P:(t + 1) * P], ple_proj[:, c, q * 512:(q + 1) * 512],
                                    start=(c == 0), stop=(c == D_PLE // P - 1))
                last.then_inc(ple_done, 1)

            pe.wait_ge(pT_ready, 2)
            ple_product(0)
            ple_product(1)
            pe.wait_ge(member_ready, 1)
            T.matmul(b_rank[:, 0:80], ones[:], prefix[:].rearrange("p i e -> p (i e)"), start=True, stop=False)
            T.matmul(b_rank[:, 0:64], tri, member[:].rearrange("p i e -> p (i e)"), start=False, stop=True).then_inc(rank_done, 1)
            for n in range(2, 6):
                ple_product(n)
            pe.wait_ge(slot_oh_ready, 1)
            for n in range(2 * NT):
                last = T.matmul(b_rank[:, P:P + 2 * TABLE], slot_oh[:, n, :], blk_rows[:, n].rearrange("p w b -> p (w b)"),
                                start=(n == 0), stop=(n == 2 * NT - 1))
            last.then_inc(rows_done, 1)
            for n in range(6, 2 * NT):
                ple_product(n)

            pe.wait_ge(table_ready, 1)
            total = pe.value_load(cum_i[0:1, N_EXPERTS - 1:N_EXPERTS], min_val=N_EXPERTS, max_val=MAX_BLOCKS)

            def in_slot(b, products):
                loads = pe.value_load(blk_loads[0:1, bass.ds(b, 1)], min_val=1, max_val=6)
                slot = pe.value_load(blk_slot[0:1, bass.ds(b, 1)], min_val=0, max_val=RING - 1)
                with pe.If(slot < 1):
                    products(0, loads)
                with pe.Else():
                    with pe.If(slot < 2):
                        products(1, loads)
                    with pe.Else():
                        products(2, loads)

            def rows_transpose(b, par):
                pe.wait_ge(s_rows[par], 16 * ((b - par) // 2 + 1) if isinstance(b, int) else 8 * (b + (2 - par)))
                for j in range(4):
                    last = T.transpose(b_xT[:, j * P:(j + 1) * P], rows[par][:, j * P:(j + 1) * P], ident)
                last.then_inc(xT_done, 1)

            def gate_up(b):
                pe.wait_ge(xT_ready, b + 1)

                def products(s, loads):
                    pe.wait_ge(s_gu[s], 32 * loads)
                    for k in range(KD):
                        for q in range(2):
                            last = T.matmul(b_gu[q * BLK:(q + 1) * BLK, :], rowsT[:, k % 4, k // 4, :],
                                            ring_gu[s][:, k, :, q * UC:(q + 1) * UC],
                                            start=(k == 0), stop=(k == KD - 1))
                    last.then_inc(gu_done, 1)

                in_slot(b, products)

            def hidden_transpose(b):
                pe.wait_ge(hid_ready, b + 1)
                for j in range(2):
                    last = T.transpose(b_hT[:, j * P:(j + 1) * P], hid[:, j * P:(j + 1) * P], ident)
                last.then_inc(hT_done, 1)

            def down(b):
                pe.wait_ge(hidT_ready, b + 1)
                pe.wait_ge(y_ready, b + 1)

                def products(s, loads):
                    pe.wait_ge(s_dn[s], 16 * loads)
                    for kf in range(D_EXPERT // P):
                        for q in range(2):
                            last = T.matmul(b_dn[q * BLK:(q + 1) * BLK, :], hidT[:, kf % 2, kf // 2, :],
                                            ring_dn[s][:, kf, q * (D // 2):(q + 1) * (D // 2)],
                                            start=(kf == 0), stop=(kf == D_EXPERT // P - 1))
                    last.then_inc(dn_done, 1)

                in_slot(b, products)

            pe.wait_ge(ple_ready, 2 * NT)
            rows_transpose(0, 0)
            gate_up(0)
            rows_transpose(1, 1)
            with pe.Fori(0, (MAX_BLOCKS - 1) // 2) as pair:
                for half in range(2):
                    b = 2 * pair + (1 + half)
                    with pe.If(b < total):
                        hidden_transpose(b - 1)
                        gate_up(b)
                        rows_transpose(b + 1, half)
                        down(b - 1)
            hidden_transpose(total - 1)
            down(total - 1)

            def x2_transpose(i):
                pe.wait_ge(x2_ready, i + 1)
                if i >= 2:
                    pe.wait_ge(x2_lo, i - 1)
                for k in range(KD):
                    last = T.transpose(b_score[2 * (i % 2) + k // 4][:, (k % 4) * P:(k % 4 + 1) * P],
                                       xr[:, i, k * P:(k + 1) * P], ident)
                last.then_inc(x2_T, 1)

            x2_transpose(0)
            for i in range(NT):
                pe.wait_ge(x2_hi, i + 1)
                pe.wait_ge(x2_lo, i + 1)
                for q in range(2):
                    pe.wait_ge(pg_lo, q + 1)
                    if i >= 2:
                        pe.wait_ge(gate_ready, 2 * (i - 2) + q + 1)
                    three_pass(b_gate[i % 2][q][:], (x2T_hi[i % 2], x2T_lo[i % 2]), (ple_hi[q], ple_lo[q]), range(KD),
                               lambda w, k: w[:, k, :], lambda m, k: m[:, k, :]).then_inc(gate_done, 1)
                    if q == 0 and i + 1 < NT:
                        x2_transpose(i + 1)


_INS = ["x", "p", "norm_mix", "w_in", "lam_q1", "lam_k1", "lam_q2", "lam_k2", "diff_subln", "w_out", "norm_ffn",
        "w_router_group", "b_router_group", "w_router_expert", "b_router_expert", "w_gate", "w_up", "w_down",
        "norm_ple", "w_ple_gate", "w_ple_proj", "norm_final"]
_LEADING = {"x": 1, "p": 2, "norm_final": 0}


def kernel(**inputs):
    import concourse.bacc as bacc
    from concourse.bass_utils import run_bass_kernel_spmd

    nc = bacc.Bacc("TRN2", target_bir_lowering=False, num_devices=1)
    arrays, args = {}, []
    for name in _INS:
        a = np.ascontiguousarray(inputs[name])
        a = a.reshape(a.shape[_LEADING.get(name, 1):])
        arrays[f"in_{name}"] = a
        args.append(nc.dram_tensor(f"in_{name}", a.shape, mybir.dt.from_np(a.dtype), kind="ExternalInput").ap())
    for name, a in zip(("decay", "bias", "small"), shape_constants()):
        arrays[f"const_{name}"] = a
        args.append(nc.dram_tensor(f"const_{name}", a.shape, F32, kind="ExternalInput").ap())
    args.append(nc.dram_tensor("out", (SEQ, D), F32, kind="ExternalOutput").ap())
    trunk(nc, *args)
    r = run_bass_kernel_spmd(nc, [arrays], core_ids=[0])
    return r.results[0]["out"].reshape(1, SEQ, D)
```

```python
from contextlib import ExitStack

import numpy as np

import concourse.bass as bass
from concourse import mybir

F32 = mybir.dt.float32
F32R = mybir.dt.float32r
I32 = mybir.dt.int32
U32 = mybir.dt.uint32
ALU = mybir.AluOpType
ACT = mybir.ActivationFunctionType
X = mybir.AxisListType.X

P = 128
SEQ, D = 512, 1024
NT = SEQ // P
KD = D // P
CHUNK = 64
HEADS = 4
DK = 128
EPS = 1e-6
LAM_INIT = 0.2
D_PLE = 256
N_GROUPS, PER_GROUP, N_EXPERTS, D_EXPERT = 4, 4, 16, 512
TOP_K = 2
NR = N_GROUPS + N_EXPERTS
BLK = 64
BPE = SEQ // BLK
MAX_BLOCKS = (TOP_K * SEQ - N_EXPERTS) // BLK + N_EXPERTS
ROW_BUFS = 3
GROUP = 6
TABLE = MAX_BLOCKS + ROW_BUFS
HALF = D // 2
N_PAIRS = TOP_K * SEQ
UC = 256
QKV = 512
PARTS = [3072, 2048, 2560, 0, 512, 1024, 1536]
DV, DQ, DKEY, RQ, RK, RV, RG = range(7)
IN_UNITS = 2 * len(PARTS)
OUT_UNITS = D // UC
UNITS = IN_UNITS + OUT_UNITS
NATURAL = (DV, RV, RG)
MASKED = -1e30
RING = 3
PROJ_BANKS = 3


def unit_outs(u):
    return NT if u >= IN_UNITS or u // 2 in NATURAL else 2


def outs_before(u):
    return sum(unit_outs(v) for v in range(u))


def schedule():
    steps = []

    def outs(u, *js, split=True):
        steps.extend(("out", u, j) for j in js)
        if split and js[-1] == unit_outs(u) - 1:
            steps.append(("split", u + 2))

    for u in range(5):
        outs(u, *range(unit_outs(u)))
    outs(5, 0)
    steps.append(("scores", 0, 0))
    outs(5, 1, split=False)
    steps.extend([("scores", 0, 1), ("split", 7)])
    outs(6, 0)
    steps.append(("weights", 0))
    outs(6, 1)
    steps.extend([("product", 0), ("scores", 1, 0)])
    outs(7, 0)
    steps.append(("scores", 1, 1))
    outs(7, 1)
    steps.append(("weights", 1))
    outs(8, 0)
    steps.extend([("product", 1), ("scores", 2, 0)])
    outs(8, 1, split=False)
    steps.extend([("scores", 2, 1), ("split", 10)])
    outs(9, 0)
    steps.append(("weights", 2))
    outs(9, 1)
    steps.extend([("product", 2), ("scores", 3, 0)])
    outs(10, 0, 1)
    steps.append(("scores", 3, 1))
    outs(10, 2, 3)
    steps.append(("weights", 3))
    outs(11, 0, 1)
    steps.extend([("product", 3), ("scores", 4), ("rms", 0)])
    outs(11, 2, 3)
    steps.append(("norm", 0))
    outs(12, 0)
    steps.extend([("norm", 1), ("scores", 5), ("product", 4), ("mixT", 0)])
    outs(12, 1)
    steps.extend([("norm", 2), ("mixT", 1)])
    outs(12, 2)
    steps.extend([("norm", 3), ("scores", 6), ("product", 5), ("mixT", 2)])
    outs(12, 3)
    outs(13, 0)
    steps.extend([("scores", 7), ("product", 6), ("mixT", 3)])
    outs(13, 1)
    steps.append(("product", 7))
    outs(13, 2)
    steps.extend([("rms", 4), ("norm", 4), ("norm", 5)])
    outs(13, 3, split=False)
    steps.extend([("norm", 6), ("norm", 7), ("mixT", 4), ("mixT", 5), ("opening", 0), ("opening", 1),
                  ("mixT", 6), ("mixT", 7), ("opening", 2), ("split", 15)])
    return steps


MIX_ROWS = [4, 5, 6, 7, 0, 1, 2, 3]


def over_blocks(engine, total, step, ahead=0):
    with engine.Fori(0, (MAX_BLOCKS - 1) // GROUP) as turn:
        def guarded(k):
            b = GROUP * turn + (1 + k)
            with engine.If(b + ahead < total):
                step(b, k, turn)
                if k + 1 < GROUP:
                    guarded(k + 1)

        guarded(0)


def shape_constants():
    s = np.arange(P)[:, None]
    t = np.arange(SEQ)[None, :]
    decay = np.zeros((P, HEADS, SEQ), np.float32)
    bias = np.zeros((P, HEADS, SEQ), np.float32)
    for h in range(HEADS):
        log_g = np.log1p(-np.exp2(-5.0 - h))
        decay[:, h] = np.where(t >= s, np.exp(log_g * np.maximum(t - s, 0)), 0.0) * DK ** -0.5
        key = t - (SEQ - P)
        slope = 2.0 ** (-8.0 * (h + 1) / HEADS)
        allowed = (key // CHUNK) <= (s // CHUNK)
        bias[:, h] = np.where(allowed, -slope * np.abs(s - key), MASKED)
    k, i, tok = np.arange(TOP_K)[None, :, None], np.arange(NT)[None, None, :], s[:, :, None]
    src = np.broadcast_to(2 * (P * i + tok), (P, TOP_K, NT))
    dst = np.broadcast_to(2 * (SEQ * k + P * i + tok - N_PAIRS), (P, TOP_K, NT))
    half = np.broadcast_to(s // BLK, (P, TABLE))
    small = np.concatenate([
        np.eye(P),
        (s < np.arange(P)[None, :]).astype(float),
        np.tile(np.arange(PER_GROUP), (P, 1)),
        np.tile(np.arange(BPE) * BLK, (P, 1)),
        np.tile(np.arange(TABLE), (P, 1)),
        np.tile((np.arange(TABLE) + 1) * BLK, (P, 1)),
        np.tile(np.arange(RING, N_EXPERTS, RING), (P, 1)),
        np.tile(np.arange(P) % BLK, (P, 1)),
        np.stack([src, dst], 3).reshape(P, -1),
        np.concatenate([half, half + 2 * N_PAIRS], 1),
    ], 1).astype(np.float32)
    return decay.reshape(P, -1), bias.reshape(P, -1), small


def trunk(nc, x, p, norm_mix, w_in, lam_q1, lam_k1, lam_q2, lam_k2, diff_subln, w_out, norm_ffn,
          w_rg, b_rg, w_re, b_re, w_gate, w_up, w_down, norm_ple, w_ple_gate, w_ple_proj,
          norm_final, decay_tab, bias_tab, small_tab, out):
    ctx = ExitStack()
    with ctx:
        K = 1024
        base = -(-nc.sbuf_base // 32) * 32

        def at(name, kb, shape, dt=F32):
            return nc.alloc_sbuf_tensor_at(name, shape, dt, offset=base + int(kb * K))

        w_raw = [at(f"w_raw{i}", 8 * i, [P, KD, UC]) for i in range(2)]
        w_hi = [at(f"w_hi{i}", 16 + 8 * i, [P, KD, UC], F32R) for i in range(2)]
        w_lo = [at(f"w_lo{i}", 32 + 8 * i, [P, KD, UC], F32R) for i in range(2)]
        h2 = at("h2", 0, [P, NT, D])
        hT_hi = at("hT_hi", 48, [P, KD, SEQ], F32R)
        hT_lo = at("hT_lo", 108, [P, KD, SEQ], F32R)
        dkT = at("dkT", 64, [P, HEADS, SEQ])
        dv = at("dv", 72, [P, NT, QKV])
        mix_r = [at(f"mix_r{i}", 48 + 8 * i, [P, HEADS, SEQ], F32R) for i in range(2)]
        mix_d = [at(f"mix_d{i}", 64 + 8 * i, [P, HEADS, SEQ], F32R) for i in range(2)]
        ple = at("ple", 48, [P, NT, D])
        ple_proj = at("ple_proj", 32, [P, D_PLE // P, D])
        pT = at("pT", 72, [P, D_PLE // P, SEQ])
        p_sb = at("p_sb", 16, [P, NT, D_PLE])
        rows = [at(f"rows{i}", kb, [P, D // 2]) for i, kb in enumerate((64, 66, 99.25))]
        rowsT = at("rowsT", 68, [P, 4, 2, BLK])
        silu_g = at("silu_g", 70, [P, UC])
        hid = at("hid", 71, [P, UC])
        hidT = at("hidT", 72, [P, 2, 2, BLK])
        y_blk = [at(f"y_blk{i}", kb, [P, D // 2]) for i, kb in enumerate((73, 76, 101.25))]
        out_sb = at("out_sb", 76, [P, D])
        xr = at("xr", 80, [P, NT, D])
        small = at("small", 96, [P, 553])
        widths = [P, P, PER_GROUP, BPE, TABLE, TABLE, (N_EXPERTS - 1) // RING, P, 4 * NT, 2 * TABLE]
        starts = [sum(widths[:n]) for n in range(len(widths))]
        assert sum(widths) == 553
        (ident, tri, iota4, iota64, iota_blk, edges, iota_ring, slot_of_row, pair_rows,
         row_offset) = [small[:, a:a + w] for a, w in zip(starts, widths)]
        subln_b = at("subln_b", 98.25, [P, P])
        ones = at("ones", 98.75, [P, P])
        gffn = at("gffn", 99.25, [P, D])
        w_r = at("w_r", 103.25, [P, KD, NR])
        cur = [104.0]

        def tiny(name, shape, dt=F32):
            n = int(np.prod(shape[1:])) * 4
            t = at(name, cur[0], shape, dt)
            cur[0] += -(-n // 32) * 32 / K
            assert cur[0] <= 107.75
            return t

        gffn_k = tiny("gffn_k", [P, KD])
        gple = tiny("gple", [P, KD])
        b_r = tiny("b_r", [P, NR])
        warm = tiny("warm", [P, 1])
        ssqh = tiny("ssqh", [P, 2 * HEADS, NT])
        rmsh = tiny("rmsh", [P, 2 * HEADS, NT])
        rstdh = tiny("rstdh", [P, 2 * HEADS, NT])
        eps = tiny("eps", [P, 1])
        lam_dot = tiny("lam_dot", [P, 2])
        lam_exp = tiny("lam_exp", [P, 2])
        neg_lam = tiny("neg_lam", [P, 1])
        ssq = tiny("ssq", [P, NT])
        rms = tiny("rms", [P, NT])
        rstd = tiny("rstd", [P, NT])
        row_max = [tiny(f"row_max{i}", [P, 2]) for i in range(2)]
        neg_max = [tiny(f"neg_max{i}", [P, 2]) for i in range(2)]
        z = [tiny(f"z{i}", [P, 2]) for i in range(2)]
        rz = [tiny(f"rz{i}", [P, 2]) for i in range(2)]
        rl = [tiny(f"rl{i}", [P, 1]) for i in range(2)]
        ssq2 = tiny("ssq2", [P, NT, OUT_UNITS])
        sum2 = tiny("sum2", [P, NT])
        rms2 = tiny("rms2", [P, NT])
        rstd2 = tiny("rstd2", [P, NT])
        ssq3 = tiny("ssq3", [P, NT])
        rms3 = tiny("rms3", [P, NT])
        rstd3 = tiny("rstd3", [P, NT])
        ssq4 = tiny("ssq4", [P, NT, 2])
        sum4 = tiny("sum4", [P, NT])
        rms4 = tiny("rms4", [P, NT])
        rstd4 = tiny("rstd4", [P, NT])
        w_top = [tiny(f"w_top{k}", [P, NT]) for k in range(2)]
        src_row = tiny("src_row", [P, TABLE], I32)
        dst_row = tiny("dst_row", [P, TABLE], I32)
        src_now = [tiny(f"src_now{i}", [P, 1], I32) for i in range(ROW_BUFS)]
        dst_now = [tiny(f"dst_now{i}", [P, 1], I32) for i in range(3)]
        cum_i = tiny("cum_i", [1, N_EXPERTS + 1], I32)
        blk_slot = tiny("blk_slot", [1, 32], I32)
        blk_loads = tiny("blk_loads", [1, 32], I32)
        dqT = at("dqT", 124, [P, HEADS, SEQ])
        rqT = at("rqT", 132, [P, HEADS, SEQ])
        rkT = at("rkT", 140, [P, HEADS, SEQ])
        rv = at("rv", 148, [P, NT, QKV])
        rg = at("rg", 156, [P, NT, QKV])
        dest = {DQ: dqT, DKEY: dkT, DV: dv, RQ: rqT, RK: rkT, RV: rv, RG: rg}
        decay = at("decay", 164, [P, HEADS, SEQ])
        bias = at("bias", 172, [P, HEADS, SEQ])
        xn = [at(f"xn{i}", 180 + 4 * i, [P, D]) for i in range(2)]
        gmix = at("gmix", 188, [P, D])
        junk = at("junk", 196, [P, D])
        A = [at(f"A{i}", 180 + 4 * i, [P, 2, SEQ]) for i in range(2)]
        W = [at(f"W{i}", 188 + 0.5 * (i * (i + 1) // 2), [P, P * (i + 1)]) for i in range(NT)]
        pT_off = [0, 512, 896, 1152]
        probsT = [at(f"probsT{i}", 193 + 5 * i, [P, 1280]) for i in range(2)]
        sq_head = at("sq_head", 203.75, [P, NT, P])
        sq_x1 = at("sq_x1", 205.75, [P, UC])
        lamv = at("lamv", 205.75, [P, 4, 64])
        lam_junk = at("lam_junk", 206.75, [P, 2, 64])
        gfin = at("gfin", 203.75, [P, D])
        RING_AT = [107.75, 155.75, 0]
        ring_gu = [at(f"ring_gu{i}", RING_AT[i], [P, KD, 2, D_EXPERT]) for i in range(RING)]
        ring_dn = [at(f"ring_dn{i}", RING_AT[i] + 32, [P, D_EXPERT // P, D]) for i in range(RING)]
        x1T = [at(f"x1T{i}", 203.75 + i, [P, 2, P]) for i in range(2)]
        r0 = [76.0]

        def routing(name, shape, dt=F32):
            t = at(name, r0[0], shape, dt)
            r0[0] += -(-int(np.prod(shape[1:])) * 4 // 32) * 32 / K
            assert r0[0] <= 80
            return t

        ple_gate_raw = at("ple_gate_raw", 155.75, [P, KD, D])
        ple_hi = [at(f"ple_hi{i}", 16 * i, [P, KD, D // 2], F32R) for i in range(2)]
        ple_lo = [at("ple_lo0", 32, [P, KD, D // 2], F32R), at("ple_lo1", 187.75, [P, KD, D // 2], F32R)]
        yg = [[at(f"yg{i}_{k}", 108 + 8 * i + 4 * k, [P, D]) for k in range(2)] for i in range(NT)]
        x2T_hi = [at(f"x2T_hi{i}", 140 + 8 * i, [P, KD, P], F32R) for i in range(2)]
        x2T_lo = [at(f"x2T_lo{i}", 144 + 8 * i, [P, KD, P], F32R) for i in range(2)]

        lg = routing("lg", [P, NT, NR])
        gmax = routing("gmax", [P, NT])
        eq = routing("eq", [P, NT, 4])
        cand = routing("cand", [P, NT, 4])
        cmin = routing("cmin", [P, NT])
        oh_g = routing("oh_g", [P, NT, 4])
        gsub = routing("gsub", [P, NT, 4])
        gexp = routing("gexp", [P, NT, 4])
        gsum = routing("gsum", [P, NT])
        g_w = routing("g_w", [P, NT])
        picked = routing("picked", [P, NT, 4, 4])
        les = routing("les", [P, NT, 4])
        les2 = routing("les2", [P, NT, 4])
        v_top = [routing(f"v_top{k}", [P, NT]) for k in range(2)]
        oh = [routing(f"oh{k}", [P, NT, 4]) for k in range(2)]
        vd = routing("vd", [P, NT])
        ve = routing("ve", [P, NT])
        vs = routing("vs", [P, NT])
        vr = routing("vr", [P, NT])
        E = at("E", 42, [P, 2, NT, 4, 4])
        member = at("member", 42.5, [P, NT, 16])
        prefix = at("prefix", 42.75, [P, 5, 16])
        counts = at("counts", 43.25, [P, 16])
        nb_gt = at("nb_gt", 43.5, [P, 16, BPE])
        nb = at("nb", 44, [P, 16])
        nb1 = at("nb1", 44.125, [P, 16])
        one16 = at("one16", 44.25, [P, 16])
        cum = at("cum", 44.375, [P, 16])
        first = at("first", 44.5, [P, 16])
        first64 = at("first64", 44.625, [P, 16])
        slots = at("slots", 44.75, [P, NT, 16])
        slot_e = at("slot_e", 45, [P, 2, NT, 16])
        slot_f = at("slot_f", 45.5, [P, 2, NT])
        past_edge = at("past_edge", 99.25, [P, 2 * NT, TABLE])
        blk_f = at("blk_f", 70.25, [P, 2 * NT])
        in_blk = at("in_blk", 70.5, [P, 2 * NT])
        blk_oh = at("blk_oh", 100.5, [P, 2 * NT, TABLE])
        blk_rows = at("blk_rows", 68, [P, 2 * NT, 2, TABLE])
        slot_oh = at("slot_oh", 203.75, [P, 2 * NT, P])
        rows_f = at("rows_f", 102, [P, 2 * TABLE])
        blk_ge = at("blk_ge", 46, [1, 32, 16])
        blk_e = at("blk_e", 45.75, [1, 32])
        blk_rge = at("blk_rge", 43.25, [1, 32, 5])
        blk_q = at("blk_q", 45.875, [1, 32])

        h2_rows = nc.dram_tensor("h2_rows", [2 * SEQ, HALF], F32, kind="Internal").ap()
        y_rows = nc.dram_tensor("y_rows", [2 * N_PAIRS + 2, HALF], F32, kind="Internal").ap()

        bank = [ctx.enter_context(nc.psum_tensor(f"bank{i}", [P, 512], F32)) for i in range(8)]
        b_proj = [bank[0], bank[1], bank[7]]
        b_score = bank[2:6]
        b_o = bank[6]
        b_rank = bank[5]
        b_ple = [bank[0], bank[1], bank[7], bank[4]]
        b_gu, b_dn, b_xT, b_hT = bank[0], bank[1], bank[2], bank[3]
        b_gate = [bank[0:2], bank[6:8]]

        def sem(name):
            return ctx.enter_context(nc.semaphore(name))

        s_x = [sem(f"x_loaded{i}") for i in range(NT)]
        s_const = sem("constants_loaded")
        s_late = sem("late_constants_loaded")
        s_tab = sem("tables_loaded")
        s_lam = sem("lambda_vectors_loaded")
        s_raw = [sem(f"unit_loaded{i}") for i in range(2)]
        s_h2 = sem("h2_stored")
        s_gu = [[sem(f"gate_up_loaded{i}_{half}") for half in range(2)] for i in range(RING)]
        s_dn = [sem(f"down_loaded{i}") for i in range(RING)]
        s_pple = sem("ple_inputs_loaded")
        s_plegate = sem("ple_gate_loaded")
        s_rows = [sem(f"block_rows_loaded{i}") for i in range(ROW_BUFS)]
        s_ystored = sem("block_out_stored")
        s_gather = [sem(f"expert_rows_gathered{i}") for i in range(NT)]
        s_out = sem("out_stored")

        dve_chain = sem("dve_chain")
        act_chain = sem("act_chain")
        memsets = sem("memsets_done")
        column_ready = sem("table_column_ready")
        gathers_begun = sem("gathers_begun")
        scatters_begun = sem("scatters_begun")
        x_ssq = sem("x_rms_ready")
        xn_ready = sem("xn_ready")
        xn_T = sem("xn_transposed")
        h_hi = sem("h_hi_ready")
        h_lo = sem("h_lo_ready")
        hi_done = sem("unit_hi_ready")
        lo_done = sem("unit_lo_ready")
        proj_done = sem("proj_done")
        proj_evac = sem("proj_evacuated")
        lam_ready = sem("lam_dots_ready")
        lam_exped = sem("lam_exp_ready")
        score_done = sem("scores_ready")
        score_evac = sem("scores_evacuated")
        max_ready = sem("row_max_ready")
        exp_done = sem("exp_ready")
        w_ready = sem("probs_ready")
        wT_done = sem("probs_transposed")
        wT_ready = sem("probsT_ready")
        ret_done = sem("ret_scores_ready")
        ret_ready = sem("ret_scoresT_ready")
        o_done = sem("head_out_ready")
        o_evac = sem("head_out_evacuated")
        orms_ready = sem("head_rms_ready")
        onorm_ready = sem("head_normed")
        mixT_done = sem("mix_transposed")
        mix_hi = sem("mix_hi_ready")
        mix_lo = sem("mix_lo_ready")
        x1_add = sem("x1_added")
        x1_sq = sem("x1_squares_ready")
        sum2_ready = sem("x1_sum_ready")
        rms2_ready = sem("x1_rms_ready")
        h2_ready = sem("h2_ready")
        x1_T = sem("x1_transposed")
        x1T_ready = sem("x1T_ready")
        wr_ready = sem("router_weights_scaled")
        lg_done = sem("logits_done")
        gsub_ready = sem("group_logits_shifted")
        gexp_ready = sem("group_exp_ready")
        vd_ready = sem("expert_logit_gap_ready")
        ve_ready = sem("expert_exp_ready")
        member_ready = sem("members_ready")
        rank_done = sem("ranks_ready")
        slot_oh_ready = sem("slot_one_hots_ready")
        rows_done = sem("slot_rows_summed")
        rows_ready = sem("slot_rows_ready")
        table_ready = sem("block_tables_ready")
        p_T = sem("p_transposed")
        pT_ready = sem("pT_ready")
        ple_done = sem("ple_product_ready")
        ple_ready = sem("ple_evacuated")
        xT_done = sem("rows_transposed")
        xT_ready = sem("rowsT_ready")
        gu_half_done = sem("gate_up_first_half_done")
        gu_done = sem("gate_up_done")
        sg_ready = sem("silu_ready")
        hid_ready = sem("hidden_ready")
        hT_done = sem("hidden_transposed")
        hidT_ready = sem("hiddenT_ready")
        dn_done = sem("down_done")
        y_ready = sem("block_out_ready")
        pg_hi = sem("ple_gate_hi_ready")
        pg_lo = sem("ple_gate_lo_ready")
        x2_ready = sem("x2_ready")
        rms3_ready = sem("x2_rms_ready")
        x2_T = sem("x2_transposed")
        rstd3_ready = sem("x2_rstd_ready")
        x3_sq = sem("x3_squares_ready")
        sum4_ready = sem("x3_sum_ready")
        x2_hi = sem("x2_hi_ready")
        x2_lo = sem("x2_lo_ready")
        gate_done = sem("ple_gate_logits_ready")
        gate_ready = sem("ple_gate_ready")
        x3_ready = sem("x3_ready")
        rms4_ready = sem("x3_rms_ready")
        res_ready = sem("result_ready")

        def mix_of(part, q):
            return (mix_d if q < HEADS else mix_r)[part][:, q % HEADS, :]

        def o_of(n):
            return (dqT if n < HEADS else rqT)[:, n % HEADS, :].rearrange("p (t c) -> p t c", t=NT)

        P1_OUTS = outs_before(IN_UNITS)
        block = ctx.enter_context(nc.Block())

        @block.sync
        def _(sp):
            w_in_v = w_in.rearrange("(k p) n -> p k n", p=P)
            w_out_v = w_out.rearrange("(k p) n -> p k n", p=P)

            def load_unit(u):
                if u >= 2:
                    sp.wait_ge(hi_done, u - 1)
                    sp.wait_ge(lo_done, u - 1)
                if u < IN_UNITS:
                    c = PARTS[u // 2] + UC * (u % 2)
                    src = w_in_v[:, :, c:c + UC]
                else:
                    c = UC * (u - IN_UNITS)
                    src = w_out_v[:, :, c:c + UC]
                sp.dma_start(w_raw[u % 2][:], src).then_inc(s_raw[u % 2], 16)

            for i in range(NT):
                sp.dma_start(xr[:, i, :], x[i * P:(i + 1) * P, :]).then_inc(s_x[i], 16)
            load_unit(0)
            load_unit(1)
            for n, v in enumerate((lam_q1, lam_k1, lam_q2, lam_k2)):
                sp.dma_start(lamv[:, n, :], v.rearrange("(o n) -> o n", o=1).to_broadcast([P, 64])).then_inc(s_lam, 16)
            sp.dma_start(subln_b[:], diff_subln.rearrange("(o n) -> o n", o=1).to_broadcast([P, P])).then_inc(s_late, 16)
            sp.dma_start(gple[:], norm_ple.rearrange("(k p) -> p k", p=P),
                         allow_slow_non_contiguous=True).then_inc(s_late, 16)
            sp.dma_start(gffn_k[:], norm_ffn.rearrange("(k p) -> p k", p=P),
                         allow_slow_non_contiguous=True).then_inc(s_late, 16)
            sp.dma_start(gffn[:], norm_ffn.rearrange("(o n) -> o n", o=1).to_broadcast([P, D])).then_inc(s_late, 16)
            sp.dma_start(w_r[:, :, 0:N_GROUPS], w_rg.rearrange("(k p) n -> p k n", p=P)).then_inc(s_late, 16)
            sp.dma_start(w_r[:, :, N_GROUPS:NR], w_re.rearrange("(k p) n -> p k n", p=P)).then_inc(s_late, 16)
            sp.dma_start(b_r[:, 0:N_GROUPS], b_rg.rearrange("(o n) -> o n", o=1).to_broadcast([P, N_GROUPS])).then_inc(s_late, 16)
            sp.dma_start(b_r[:, N_GROUPS:NR], b_re.rearrange("(o n) -> o n", o=1).to_broadcast([P, N_EXPERTS])).then_inc(s_late, 16)
            load_unit(2)
            load_unit(3)
            sp.dma_start(bias[:], bias_tab.rearrange("p (h t) -> p h t", h=HEADS)).then_inc(s_tab, 16)
            sp.dma_start(decay[:], decay_tab.rearrange("p (h t) -> p h t", h=HEADS)).then_inc(s_tab, 16)
            for u in range(4, UNITS):
                load_unit(u)
            sp.wait_ge(mix_lo, 2 * HEADS)
            sp.wait_ge(mix_hi, 2 * HEADS)

            def load_gu(e, slot, half):
                ks = slice(half * KD // 2, (half + 1) * KD // 2)
                for n, w in enumerate((w_gate, w_up)):
                    src = w[bass.ds(e, 1)].rearrange("o (k p) f -> p (o k) f", p=P)
                    sp.dma_start(ring_gu[slot][:, ks, n, :], src[:, ks, :]).then_inc(s_gu[slot][half], 16)

            def load_dn(e, slot):
                sp.dma_start(ring_dn[slot][:],
                             w_down[bass.ds(e, 1)].rearrange("o (k p) f -> p (o k) f", p=P)).then_inc(s_dn[slot], 16)

            for e in range(2):
                load_gu(e, e, 0)
                load_gu(e, e, 1)
                load_dn(e, e)
            sp.wait_ge(x1_add, NT * (OUT_UNITS - 1))
            sp.dma_start(p_sb[:], p.rearrange("(t p) c -> p t c", p=P)).then_inc(s_pple, 16)
            sp.dma_start(ple_proj[:], w_ple_proj.rearrange("(k p) n -> p k n", p=P)).then_inc(s_pple, 16)
            for i in range(NT):
                sp.wait_ge(h2_ready, i + 1)
                sp.dma_start(h2_rows[2 * P * i:2 * P * (i + 1)].rearrange("(p q) c -> p (q c)", q=2),
                             h2[:, i, :]).then_inc(s_h2, 16)
            sp.wait_ge(s_h2, 16 * NT)
            sp.wait_ge(p_T, D_PLE // P)
            load_gu(2, 2, 0)
            load_gu(2, 2, 1)
            sp.wait_ge(table_ready, 1)
            sp.wait_ge(ple_ready, 2 * NT)
            for buf in range(ROW_BUFS):
                sp.wait_ge(s_rows[buf], 16)
            load_dn(2, 2)
            sp.dma_start(gfin[:], norm_final.rearrange("(o n) -> o n", o=1).to_broadcast([P, D])).then_inc(s_plegate, 16)

            def blocks_through(e):
                return sp.value_load(cum_i[0:1, bass.ds(e, 1)], min_val=1, max_val=MAX_BLOCKS)

            def reload(e, slot):
                used = blocks_through(e - RING)
                sp.wait_ge(gu_half_done, used)
                load_gu(e, slot, 0)
                sp.wait_ge(gu_done, used)
                load_gu(e, slot, 1)
                sp.wait_ge(dn_done, used)
                load_dn(e, slot)

            with sp.Fori(0, N_EXPERTS // RING - 1) as turn:
                for slot in range(RING):
                    reload(RING * turn + (RING + slot), slot)
            reload(N_EXPERTS - 1, 0)
            sp.wait_ge(dn_done, blocks_through(N_EXPERTS - 3))
            sp.dma_start(ple_gate_raw[:], w_ple_gate.rearrange("(k p) n -> p k n", p=P)).then_inc(s_plegate, 16)
            sp.wait_ge(s_ystored, 16 * (blocks_through(N_EXPERTS - 1) + 1))
            for i in range(NT):
                for k in range(TOP_K):
                    r = 2 * (SEQ * k + P * i)
                    sp.dma_start(yg[i][k][:], y_rows[r:r + 2 * P].rearrange("(p q) c -> p (q c)", q=2)).then_inc(s_gather[i], 16)
            for i in range(NT):
                for q in range(2):
                    sp.wait_ge(res_ready, 2 * i + q + 1)
                    sp.dma_start(out[i * P:(i + 1) * P, q * HALF:(q + 1) * HALF],
                                 out_sb[:, q * HALF:(q + 1) * HALF]).then_inc(s_out, 16)
            sp.wait_ge(s_out, 32 * NT)

        @block.gpsimd
        def _(pool):
            pool.memset(ones[:], 1.0).then_inc(memsets, 1)
            pool.memset(eps[:], EPS).then_inc(memsets, 1)
            pool.wait_ge(memsets, 2)
            pool.dma_start(y_rows[2 * N_PAIRS:2 * N_PAIRS + 2].rearrange("r (a c) -> (r a) c", c=P),
                           ones[0:2 * HALF // P, :]).then_inc(s_ystored, 16)
            pool.wait_ge(rows_ready, 1)
            pool.wait_ge(s_h2, 16 * NT)
            total = pool.value_load(cum_i[0:1, N_EXPERTS - 1:N_EXPERTS], min_val=N_EXPERTS, max_val=MAX_BLOCKS)

            def column(now, table, b):
                c = slice(b, b + 1) if isinstance(b, int) else bass.ds(b, 1)
                pool.tensor_copy(now[:], table[:, c]).then_inc(column_ready, 1)
                return bass.IndirectOffsetOnAxis(ap=now[:].bitcast(U32), axis=0)

            def gather(b, buf, n_columns):
                rows_of = column(src_now[buf], src_row, b)
                pool.wait_ge(column_ready, n_columns)
                pool.sem_inc(gathers_begun, 1)
                pool.indirect_dma_start(out=rows[buf][:], out_offset=None, in_=h2_rows,
                                        in_offset=rows_of).then_inc(s_rows[buf], 16)

            def scatter(b, buf, n_columns):
                pool.wait_ge(y_ready, b + 2)
                pool.wait_ge(s_ystored, 16 * (b + 1))
                rows_of = column(dst_now[buf], dst_row, b)
                pool.wait_ge(column_ready, n_columns)
                pool.sem_inc(scatters_begun, 1)
                pool.indirect_dma_start(out=y_rows, out_offset=rows_of, in_=y_blk[buf][:],
                                        in_offset=None).then_inc(s_ystored, 16)

            for b in range(ROW_BUFS):
                gather(b, b, b + 1)
            pool.wait_ge(xT_done, 1)
            gather(ROW_BUFS, 0, ROW_BUFS + 1)

            def step(b, k, turn):
                pool.wait_ge(xT_done, b + 1)
                gather(b + ROW_BUFS, (1 + k) % ROW_BUFS, 2 * b + ROW_BUFS)
                scatter(b - 1, k % 2, 2 * b + (ROW_BUFS + 1))

            over_blocks(pool, total, step)
            scatter(total - 1, 2, 2 * total + ROW_BUFS)

        @block.scalar
        def _(act):
            chain = [0]

            def link(ins):
                chain[0] += 1
                ins.then_inc(act_chain, 1)
                act.wait_ge(act_chain, chain[0])

            act.dma_start(gmix[:], norm_mix.rearrange("(o n) -> o n", o=1).to_broadcast([P, D])).then_inc(s_const, 16)
            act.dma_start(small[:], small_tab).then_inc(s_const, 16)
            act.wait_ge(memsets, 2)
            link(nc.scalar.activation(warm[:], eps[:], ACT.Sqrt))

            def x_rms(i):
                act.wait_ge(s_x[i], 16)
                link(nc.scalar.activation(junk[:], xr[:, i, :], ACT.Square, accum_out=ssq[:, i:i + 1]))
                nc.scalar.activation(rms[:, i:i + 1], ssq[:, i:i + 1], ACT.Sqrt, bias=eps[:], scale=1.0 / D).then_inc(x_ssq, 1)

            def h_part(i):
                act.wait_ge(xn_T, i + 1)
                for q in range(2):
                    last = nc.scalar.activation(hT_hi[:, 4 * q:4 * q + 4, i * P:(i + 1) * P],
                                                b_score[2 * (i % 2) + q][:].rearrange("p (k t) -> p k t", k=4), ACT.Copy)
                last.then_inc(h_hi, 1)

            def split_hi(u):
                if u >= 2:
                    act.wait_ge(proj_done, outs_before(u - 1))
                act.wait_ge(s_raw[u % 2], 16 * (u // 2 + 1))
                nc.scalar.activation(w_hi[u % 2][:], w_raw[u % 2][:], ACT.Copy).then_inc(hi_done, 1)

            x_rms(0)
            x_rms(1)
            h_part(0)
            x_rms(2)
            h_part(1)
            split_hi(0)
            x_rms(3)
            h_part(2)
            h_part(3)
            split_hi(1)

            def evacuate(u, j):
                part, half = u // 2, u % 2
                n = outs_before(u) + j
                act.wait_ge(proj_done, n + 1)
                b = b_proj[n % PROJ_BANKS]
                if part in NATURAL:
                    o, i_ = dest[part][:, j, half * UC:(half + 1) * UC], b[:, 0:UC]
                else:
                    o, i_ = dest[part][:, 2 * half + j, :], b[:]
                if part == RG:
                    nc.scalar.activation(o, i_, ACT.Silu).then_inc(proj_evac, 1)
                else:
                    nc.scalar.activation(o, i_, ACT.Copy, scale=0.125 if part == DQ else 1.0).then_inc(proj_evac, 1)

            def exps(h, half):
                for i in (2 * half, 2 * half + 1):
                    s, L = NT * h + i, P * (i + 1)
                    act.wait_ge(max_ready, s + 1)
                    for c in range(2):
                        last = nc.scalar.activation(A[s % 2][:, c, 0:L], A[s % 2][:, c, 0:L], ACT.Exp,
                                                    bias=neg_max[s % 2][:, c:c + 1], accum_out=z[s % 2][:, c:c + 1])
                    last.then_inc(exp_done, 1)

            def probsT_evac(h):
                for j in range(NT):
                    act.wait_ge(wT_done, h + 1)
                    if h >= 2 and j == 0:
                        act.wait_ge(o_done, h - 1)
                    o = pT_off[j]
                    nc.scalar.activation(probsT[h % 2][:, o:o + SEQ - P * j], b_score[j][:, P * j:SEQ],
                                         ACT.Copy).then_inc(wT_ready, 1)

            def head_evac(n):
                act.wait_ge(o_done, n + 1)
                if n:
                    act.wait_ge(o_evac, n)
                ob = b_o[:].rearrange("p (t c) -> p t c", t=NT)
                for i in range(NT):
                    nc.scalar.activation(sq_head[:, i, :], ob[:, i, :], ACT.Square, accum_out=ssqh[:, n, i:i + 1])
                nc.scalar.activation(o_of(n), ob, ACT.Copy).then_inc(o_evac, 1)

            def head_rms(n):
                act.wait_ge(o_evac, n + HEADS)
                nc.scalar.activation(rmsh[:, n:n + HEADS, :], ssqh[:, n:n + HEADS, :], ACT.Sqrt, bias=eps[:],
                                     scale=1.0 / P).then_inc(orms_ready, 1)

            def mix_split_hi(q):
                act.wait_ge(mixT_done, q + 1)
                nc.scalar.activation(mix_of(0, q), b_score[q % 4][:], ACT.Copy).then_inc(mix_hi, 1)

            act.wait_ge(lam_ready, 1)
            nc.scalar.activation(lam_exp[:], lam_dot[:], ACT.Exp).then_inc(lam_exped, 1)
            for step, n, *j in schedule():
                if step == "out":
                    evacuate(n, *j)
                elif step == "scores" and n < HEADS:
                    exps(n, *j)
                elif step == "weights":
                    probsT_evac(n)
                elif step == "product":
                    head_evac(n)
                elif step == "rms":
                    head_rms(n)
                elif step == "mixT":
                    mix_split_hi(n)
                elif step == "split":
                    split_hi(n)

            def x1T_evac(m):
                act.wait_ge(x1_T, m + 1)
                if m >= 2:
                    act.wait_ge(lg_done, m - 1)
                nc.scalar.activation(x1T[m % 2][:], b_score[m % 4][:, 0:UC].rearrange("p (k t) -> p k t", k=2), ACT.Copy).then_inc(x1T_ready, 1)

            for u in range(OUT_UNITS):
                for i in range(NT):
                    m = NT * u + i
                    act.wait_ge(x1_add, m + 1)
                    if m:
                        act.wait_ge(x1_sq, m)
                    nc.scalar.activation(sq_x1[:], xr[:, i, u * UC:(u + 1) * UC], ACT.Square,
                                         accum_out=ssq2[:, i, u:u + 1]).then_inc(x1_sq, 1)
                    if u == OUT_UNITS - 1:
                        act.wait_ge(sum2_ready, i + 1)
                        nc.scalar.activation(rms2[:, i:i + 1], sum2[:, i:i + 1], ACT.Sqrt, bias=eps[:],
                                             scale=1.0 / D).then_inc(rms2_ready, 1)
                    if m:
                        x1T_evac(m - 1)
                if u < 2:
                    split_hi(IN_UNITS + 2 + u)
            x1T_evac(NT * OUT_UNITS - 1)
            for c in range(D_PLE // P):
                act.wait_ge(p_T, c + 1)
                nc.scalar.activation(pT[:, c, :], b_score[c][:], ACT.Copy).then_inc(pT_ready, 1)
            act.wait_ge(gsub_ready, 1)
            nc.scalar.activation(gexp[:], gsub[:], ACT.Exp).then_inc(gexp_ready, 1)
            act.wait_ge(vd_ready, 1)
            nc.scalar.activation(ve[:], vd[:], ACT.Exp).then_inc(ve_ready, 1)
            for n in range(2 * NT):
                act.wait_ge(ple_done, n + 1)
                nc.scalar.activation(ple[:, n // 2, (n % 2) * 512:(n % 2) * 512 + 512], b_ple[n % 4][:],
                                     ACT.Copy).then_inc(ple_ready, 1)

            act.wait_ge(table_ready, 1)
            total = act.value_load(cum_i[0:1, N_EXPERTS - 1:N_EXPERTS], min_val=N_EXPERTS, max_val=MAX_BLOCKS)

            def rowsT_evac(b):
                act.wait_ge(xT_done, b + 1)
                nc.scalar.activation(rowsT[:], b_xT[:].rearrange("p (j q t) -> p j q t", j=4, q=2),
                                     ACT.Copy).then_inc(xT_ready, 1)

            def silu(b):
                act.wait_ge(gu_done, b + 1)
                nc.scalar.activation(silu_g[:], b_gu[:, 0:UC], ACT.Silu).then_inc(sg_ready, 1)

            rowsT_evac(0)
            link(nc.scalar.activation(warm[:], eps[:], ACT.Silu))
            silu(0)
            rowsT_evac(1)

            def step(b, k, turn):
                act.wait_ge(hid_ready, b)
                silu(b)
                rowsT_evac(b + 1)

            over_blocks(act, total, step)

            act.wait_ge(s_plegate, 32)
            act.wait_ge(dn_done, act.value_load(cum_i[0:1, N_EXPERTS - 2:N_EXPERTS - 1], min_val=1, max_val=MAX_BLOCKS))
            for q in range(2):
                for k in range(KD):
                    nc.scalar.activation(ple_hi[q][:, k, :], ple_gate_raw[:, k, q * HALF:(q + 1) * HALF], ACT.Copy,
                                         scale=gple[:, k:k + 1]).then_inc(pg_hi, 1)

            def stage6_a(i):
                act.wait_ge(x2_T, i + 1)
                if i >= 2:
                    act.wait_ge(gate_done, 2 * (i - 1))
                for q in range(2):
                    last = nc.scalar.activation(x2T_hi[i % 2][:, 4 * q:4 * q + 4, :],
                                                b_score[2 * (i % 2) + q][:].rearrange("p (k t) -> p k t", k=4), ACT.Copy)
                last.then_inc(x2_hi, 1)
                link(nc.scalar.activation(yg[i][1][:], xr[:, i, :], ACT.Square, accum_out=ssq3[:, i:i + 1]))
                nc.scalar.activation(rms3[:, i:i + 1], ssq3[:, i:i + 1], ACT.Sqrt, bias=eps[:], scale=1.0 / D).then_inc(rms3_ready, 1)

            def stage6_b(i):
                act.wait_ge(rstd3_ready, i + 1)
                for q in range(2):
                    act.wait_ge(gate_done, 2 * i + q + 1)
                    nc.scalar.activation(yg[i][0][:, q * HALF:(q + 1) * HALF], b_gate[i % 2][q][:], ACT.Sigmoid,
                                         scale=rstd3[:, i:i + 1]).then_inc(gate_ready, 1)
                link(nc.scalar.activation(warm[:], eps[:], ACT.Sqrt))
                for q in range(2):
                    act.wait_ge(x3_ready, 2 * i + q + 1)
                    nc.scalar.activation(yg[i][1][:, q * HALF:(q + 1) * HALF], xr[:, i, q * HALF:(q + 1) * HALF], ACT.Square,
                                         accum_out=ssq4[:, i, q:q + 1]).then_inc(x3_sq, 1)
                act.wait_ge(sum4_ready, i + 1)
                nc.scalar.activation(rms4[:, i:i + 1], sum4[:, i:i + 1], ACT.Sqrt, bias=eps[:], scale=1.0 / D).then_inc(rms4_ready, 1)

            stage6_a(0)
            for i in range(NT):
                if i + 1 < NT:
                    stage6_a(i + 1)
                stage6_b(i)

        @block.vector
        def _(dve):
            chain = [0]
            V = nc.vector

            def link(ins):
                chain[0] += 1
                ins.then_inc(dve_chain, 1)
                dve.wait_ge(dve_chain, chain[0])

            def route():
                def wide(t, n):
                    return t.unsqueeze(len(t.shape)).to_broadcast(list(t.shape) + [n])

                def all_tiles(t):
                    return t.unsqueeze(1).to_broadcast([P, NT, t.shape[-1]])

                def first_max(values, best, one_hot):
                    link(V.tensor_reduce(best[:], values, X, ALU.max))
                    link(V.tensor_tensor(eq[:], values, wide(best[:], 4), ALU.is_equal))
                    link(V.scalar_tensor_tensor(cand[:], eq[:], -64.0, all_tiles(iota4), ALU.mult, ALU.add))
                    link(V.tensor_reduce(cmin[:], cand[:], X, ALU.min))
                    link(V.tensor_tensor(one_hot[:], cand[:], wide(cmin[:], 4), ALU.is_equal))

                dve.wait_ge(lg_done, NT * OUT_UNITS)
                link(V.tensor_tensor(lg[:], b_o[:, 0:NT * NR].rearrange("p (t c) -> p t c", t=NT), wide(rstd2[:], NR),
                                     ALU.mult))
                link(V.tensor_tensor(lg[:], lg[:], all_tiles(b_r[:]), ALU.add))
                first_max(lg[:, :, 0:N_GROUPS], gmax, oh_g)
                V.tensor_tensor(gsub[:], lg[:, :, 0:N_GROUPS], wide(gmax[:], 4), ALU.subtract).then_inc(gsub_ready, 1)
                link(V.tensor_tensor(picked[:], lg[:, :, N_GROUPS:NR].rearrange("p t (g j) -> p t g j", g=4),
                                     wide(oh_g[:], 4), ALU.mult))
                link(V.tensor_reduce(les[:], picked[:].rearrange("p t g j -> p t j g"), X, ALU.add))
                first_max(les[:], v_top[0], oh[0])
                link(V.scalar_tensor_tensor(les2[:], oh[0][:], MASKED, les[:], ALU.mult, ALU.add))
                first_max(les2[:], v_top[1], oh[1])
                V.tensor_tensor(vd[:], v_top[1][:], v_top[0][:], ALU.subtract).then_inc(vd_ready, 1)
                for k in range(TOP_K):
                    for g in range(N_GROUPS):
                        last = V.tensor_tensor(E[:, k, :, g, :], oh[k][:],
                                               oh_g[:, :, g:g + 1].to_broadcast([P, NT, 4]), ALU.mult)
                    link(last)
                Ef = E[:].rearrange("p k t g j -> p k t (g j)")
                link(V.tensor_tensor(member[:], Ef[:, 0], Ef[:, 1], ALU.add))
                link(V.memset(prefix[:, 0, :], 0.0))
                for i in range(NT):
                    link(V.tensor_tensor(prefix[:, i + 1, :], prefix[:, i, :], member[:, i, :], ALU.add))
                V.memset(one16[:], 1.0).then_inc(member_ready, 1)
                dve.wait_ge(rank_done, 1)
                link(V.tensor_copy(counts[:], b_rank[:, NT * 16:NT * 16 + 16]))
                link(V.tensor_tensor(nb_gt[:], wide(counts[:], BPE),
                                     iota64.unsqueeze(1).to_broadcast([P, 16, BPE]), ALU.is_gt))
                link(V.tensor_reduce(nb[:], nb_gt[:], X, ALU.add))
                link(V.tensor_scalar(nb1[:], nb[:], 1.0, None, ALU.max))
                link(V.tensor_tensor_scan(cum[:], one16[:], nb1[:], 0.0, ALU.mult, ALU.add))
                link(V.tensor_tensor(first[:], cum[:], nb1[:], ALU.subtract))
                link(V.tensor_scalar(first64[:], first[:], float(BLK), None, ALU.mult))
                link(V.tensor_tensor(slots[:], b_rank[:, 0:NT * 16].rearrange("p (t e) -> p t e", t=NT),
                                     first64[:].unsqueeze(1).to_broadcast([P, NT, 16]), ALU.add))
                for k in range(TOP_K):
                    link(V.tensor_tensor(slot_e[:, k], Ef[:, k], slots[:], ALU.mult))
                link(V.tensor_reduce(slot_f[:], slot_e[:], X, ALU.add))
                pairs = slot_f[:].rearrange("p k t -> p (k t)")

                def all_pairs(t):
                    return t.unsqueeze(1).to_broadcast([P, 2 * NT, t.shape[-1]])

                link(V.tensor_tensor(past_edge[:], wide(pairs, TABLE), all_pairs(edges), ALU.is_ge))
                link(V.tensor_reduce(blk_f[:], past_edge[:], X, ALU.add))
                V.scalar_tensor_tensor(in_blk[:], blk_f[:], -float(BLK), pairs, ALU.mult, ALU.add)
                link(V.tensor_tensor(blk_oh[:], wide(blk_f[:], TABLE), all_pairs(iota_blk), ALU.is_equal))
                V.tensor_tensor(slot_oh[:], wide(in_blk[:], P), all_pairs(slot_of_row), ALU.is_equal)
                V.tensor_tensor(blk_rows[:], blk_oh[:].unsqueeze(2).to_broadcast([P, 2 * NT, 2, TABLE]),
                                pair_rows.rearrange("p (n w) -> p n w", w=2).unsqueeze(3).to_broadcast([P, 2 * NT, 2, TABLE]),
                                ALU.mult).then_inc(slot_oh_ready, 1)
                V.tensor_copy(cum_i[:, 0:N_EXPERTS], cum[0:1, :])
                link(V.tensor_scalar(cum_i[:, N_EXPERTS:], cum[0:1, N_EXPERTS - 1:], -1.0, None, ALU.add))
                link(V.tensor_tensor(blk_ge[:], iota_blk[0:1, 0:32].unsqueeze(2).to_broadcast([1, 32, 16]),
                                     cum[0:1, :].unsqueeze(1).to_broadcast([1, 32, 16]), ALU.is_ge))
                link(V.tensor_reduce(blk_e[:], blk_ge[:], X, ALU.add))
                dve.wait_ge(rows_done, 1)
                link(V.tensor_tensor(rows_f[:], b_rank[:, P:P + 2 * TABLE], row_offset, ALU.add))
                V.tensor_copy(src_row[:], rows_f[:, 0:TABLE])
                V.tensor_copy(dst_row[:], rows_f[:, TABLE:2 * TABLE]).then_inc(rows_ready, 1)
                link(V.tensor_tensor(blk_rge[:], blk_e[:].unsqueeze(2).to_broadcast([1, 32, 5]),
                                     iota_ring[0:1].unsqueeze(1).to_broadcast([1, 32, 5]), ALU.is_ge))
                link(V.tensor_reduce(blk_q[:], blk_rge[:], X, ALU.add))
                V.scalar_tensor_tensor(blk_slot[:], blk_q[:], -float(RING), blk_e[:], ALU.mult, ALU.add)
                V.tensor_scalar(blk_loads[:], blk_q[:], 1.0, None, ALU.add).then_inc(table_ready, 1)
                dve.wait_ge(gexp_ready, 1)
                link(V.tensor_reduce(gsum[:], gexp[:], X, ALU.add))
                link(V.reciprocal(g_w[:], gsum[:]))
                dve.wait_ge(ve_ready, 1)
                link(V.tensor_scalar(vs[:], ve[:], 1.0, None, ALU.add))
                link(V.reciprocal(vr[:], vs[:]))
                link(V.tensor_tensor(w_top[0][:], vr[:], g_w[:], ALU.mult))
                link(V.tensor_tensor(w_top[1][:], w_top[0][:], ve[:], ALU.mult))

            def split_lo(u):
                if u >= 2:
                    dve.wait_ge(proj_done, outs_before(u - 1))
                dve.wait_ge(hi_done, u + 1)
                V.tensor_tensor(w_lo[u % 2][:], w_raw[u % 2][:], w_hi[u % 2][:].bitcast(F32),
                                ALU.subtract).then_inc(lo_done, 1)

            def normed(i):
                dve.wait_ge(x_ssq, i + 1)
                link(V.reciprocal(rstd[:, i:i + 1], rms[:, i:i + 1]))
                if i >= 2:
                    dve.wait_ge(xn_T, i - 1)
                V.scalar_tensor_tensor(xn[i % 2][:], xr[:, i, :], rstd[:, i:i + 1], gmix[:], ALU.mult,
                                       ALU.mult).then_inc(xn_ready, 1)

            def h_rest(i):
                dve.wait_ge(h_hi, i + 1)
                for q in range(2):
                    part = slice(4 * q, 4 * q + 4), slice(i * P, (i + 1) * P)
                    last = V.tensor_tensor(hT_lo[:, part[0], part[1]],
                                           b_score[2 * (i % 2) + q][:].rearrange("p (k t) -> p k t", k=4),
                                           hT_hi[:, part[0], part[1]].bitcast(F32), ALU.subtract)
                last.then_inc(h_lo, 1)

            dve.wait_ge(s_const, 16 * 2)
            normed(0)
            normed(1)
            h_rest(0)
            normed(2)
            h_rest(1)
            split_lo(0)
            normed(3)
            h_rest(2)
            h_rest(3)
            split_lo(1)
            dve.wait_ge(s_lam, 64)
            for c in range(2):
                last = V.tensor_tensor_reduce(out=lam_junk[:, c, :], in0=lamv[:, 2 * c, :], in1=lamv[:, 2 * c + 1, :],
                                              scale=1.0, scalar=0.0, op0=ALU.mult, op1=ALU.add,
                                              accum_out=lam_dot[:, c:c + 1])
            last.then_inc(lam_ready, 1)
            dve.wait_ge(lam_exped, 1)
            link(V.tensor_tensor(neg_lam[:], lam_exp[:, 1:2], lam_exp[:, 0:1], ALU.subtract))
            link(V.tensor_scalar(neg_lam[:], neg_lam[:], LAM_INIT, None, ALU.subtract))
            dve.wait_ge(s_late, 16 * 8)
            link(V.tensor_scalar(subln_b[:], subln_b[:], 1.0 - LAM_INIT, None, ALU.mult))
            V.tensor_tensor(w_r[:], w_r[:], gffn_k[:].unsqueeze(2).to_broadcast([P, KD, NR]), ALU.mult).then_inc(wr_ready, 1)
            dve.wait_ge(s_tab, 32)

            def scores(h, i):
                s, L = NT * h + i, P * (i + 1)
                dve.wait_ge(score_done, s + 1)
                for c in range(2):
                    last = V.tensor_tensor_reduce(
                        out=A[s % 2][:, c, 0:L], in0=b_score[2 * (i % 2) + c][:, 0:L],
                        in1=bias[:, h, SEQ - L:SEQ], scale=1.0, scalar=MASKED, op0=ALU.add, op1=ALU.max,
                        accum_out=row_max[s % 2][:, c:c + 1])
                last.then_inc(score_evac, 1)
                dve.wait_ge(score_evac, s + 1)
                V.tensor_scalar(neg_max[s % 2][:], row_max[s % 2][:], -1.0, None, ALU.mult).then_inc(max_ready, 1)

            def probs(h, i):
                s, L = NT * h + i, P * (i + 1)
                dve.wait_ge(exp_done, s + 1)
                link(V.reciprocal(rz[s % 2][:], z[s % 2][:]))
                link(V.tensor_tensor(rl[s % 2][:], rz[s % 2][:, 1:2], neg_lam[:], ALU.mult))
                link(V.tensor_scalar(A[s % 2][:, 1, 0:L], A[s % 2][:, 1, 0:L], rl[s % 2][:], None, ALU.mult))
                if h and i == 0:
                    dve.wait_ge(wT_done, h)
                V.scalar_tensor_tensor(W[i][:], A[s % 2][:, 0, 0:L], rz[s % 2][:, 0:1], A[s % 2][:, 1, 0:L],
                                       ALU.mult, ALU.add).then_inc(w_ready, 1)
                dve.wait_ge(w_ready, s + 1)

            def softmax(h, half):
                i = 2 * half
                scores(h, i)
                scores(h, i + 1)
                probs(h, i)
                probs(h, i + 1)

            def decayed(r):
                for j in range(NT):
                    dve.wait_ge(ret_done, NT * r + j + 1)
                    if j == 0:
                        dve.wait_ge(o_done, HEADS + r - 1)
                    o, L = pT_off[j], SEQ - P * j
                    V.tensor_tensor(probsT[r % 2][:, o:o + L], b_score[j][:, 0:L], decay[:, r, 0:L],
                                    ALU.mult).then_inc(ret_ready, 1)

            def head_rstd(n):
                dve.wait_ge(orms_ready, n // HEADS + 1)
                link(V.reciprocal(rstdh[:, n:n + HEADS, :], rmsh[:, n:n + HEADS, :]))

            def head_norm(n):
                h = n % HEADS
                if n >= HEADS:
                    dve.wait_ge(proj_evac, outs_before(2 * RG + 1 + h // 2))
                for i in range(NT):
                    gain = subln_b[:] if n < HEADS else rg[:, i, h * P:(h + 1) * P]
                    last = V.scalar_tensor_tensor(o_of(n)[:, i, :], o_of(n)[:, i, :], rstdh[:, n, i:i + 1], gain,
                                                  ALU.mult, ALU.mult)
                last.then_inc(onorm_ready, 1)

            def mix_split_lo(q):
                dve.wait_ge(mix_hi, q + 1)
                V.tensor_tensor(mix_of(1, q), b_score[q % 4][:], mix_of(0, q).bitcast(F32), ALU.subtract).then_inc(mix_lo, 1)

            for step, n, *j in schedule():
                if step == "split":
                    split_lo(n)
                elif step == "scores":
                    softmax(n, *j) if n < HEADS else decayed(n - HEADS)
                elif step == "rms":
                    head_rstd(n)
                elif step == "norm":
                    head_norm(n)
                elif step == "mixT":
                    mix_split_lo(n)

            for u in range(OUT_UNITS):
                for i in range(NT):
                    m = NT * u + i
                    dve.wait_ge(proj_done, P1_OUTS + m + 1)
                    part = xr[:, i, u * UC:(u + 1) * UC]
                    V.tensor_tensor(part, b_proj[(P1_OUTS + m) % PROJ_BANKS][:, 0:UC], part, ALU.add).then_inc(x1_add, 1)
                    if u == OUT_UNITS - 1:
                        dve.wait_ge(x1_sq, m + 1)
                        V.tensor_reduce(sum2[:, i:i + 1], ssq2[:, i, :], X, ALU.add).then_inc(sum2_ready, 1)
                        dve.wait_ge(rms2_ready, i + 1)
                        link(V.reciprocal(rstd2[:, i:i + 1], rms2[:, i:i + 1]))
                        V.scalar_tensor_tensor(h2[:, i, :], xr[:, i, :], rstd2[:, i:i + 1], gffn[:], ALU.mult,
                                               ALU.mult).then_inc(h2_ready, 1)
                if u < 2:
                    split_lo(IN_UNITS + 2 + u)
            route()

            total = dve.value_load(cum_i[0:1, N_EXPERTS - 1:N_EXPERTS], min_val=N_EXPERTS, max_val=MAX_BLOCKS)
            dve.sem_inc(y_ready, 1)

            def hidden(b):
                dve.wait_ge(sg_ready, b + 1)
                V.tensor_tensor(hid[:], silu_g[:], b_gu[:, UC:2 * UC], ALU.mult).then_inc(hid_ready, 1)

            def hiddenT(b):
                dve.wait_ge(hT_done, b + 1)
                V.tensor_copy(hidT[:], b_hT[:, 0:256].rearrange("p (j q t) -> p j q t", j=2, q=2)).then_inc(hidT_ready, 1)

            last_block = dve.value_load(cum_i[0:1, N_EXPERTS:], min_val=N_EXPERTS - 1, max_val=MAX_BLOCKS - 1)

            def evacuate_y(b, buf, fresh=False):
                dve.wait_ge(dn_done, b + 1)
                if not fresh:
                    dve.wait_ge(s_ystored, 16 * b)
                V.tensor_copy(y_blk[buf][:], b_dn[:]).then_inc(y_ready, 1)

            hidden(0)
            for b in range(2):
                hiddenT(b)
                hidden(b + 1)
                evacuate_y(b, b, fresh=True)

            def step(b, k, turn):
                hiddenT(b + 1)
                hidden(b + 2)
                evacuate_y(b + 1, k % 2)

            over_blocks(dve, total, step, ahead=2)

            def split_gate(pieces):
                for n in pieces:
                    q, k = n // KD, n % KD
                    dve.wait_ge(pg_hi, n + 1)
                    V.scalar_tensor_tensor(ple_lo[q][:, k, :], ple_gate_raw[:, k, q * HALF:(q + 1) * HALF],
                                           gple[:, k:k + 1], ple_hi[q][:, k, :].bitcast(F32), ALU.mult,
                                           ALU.subtract).then_inc(pg_lo, 1)

            hiddenT(last_block)
            split_gate(range(6))
            evacuate_y(last_block, 2, fresh=True)
            split_gate(range(6, 2 * KD))

            def stage6_a(i):
                dve.wait_ge(s_gather[i], 16 * TOP_K)
                link(V.scalar_tensor_tensor(xr[:, i, :], yg[i][0][:], w_top[0][:, i:i + 1], xr[:, i, :], ALU.mult, ALU.add))
                V.scalar_tensor_tensor(xr[:, i, :], yg[i][1][:], w_top[1][:, i:i + 1], xr[:, i, :], ALU.mult,
                                       ALU.add).then_inc(x2_ready, 1)

            def stage6_split(i):
                dve.wait_ge(x2_hi, i + 1)
                for q in range(2):
                    last = V.tensor_tensor(x2T_lo[i % 2][:, 4 * q:4 * q + 4, :],
                                           b_score[2 * (i % 2) + q][:].rearrange("p (k t) -> p k t", k=4),
                                           x2T_hi[i % 2][:, 4 * q:4 * q + 4, :].bitcast(F32), ALU.subtract)
                last.then_inc(x2_lo, 1)
                dve.wait_ge(rms3_ready, i + 1)
                V.reciprocal(rstd3[:, i:i + 1], rms3[:, i:i + 1]).then_inc(rstd3_ready, 1)

            def stage6_b(i):
                for q in range(2):
                    half = slice(q * HALF, (q + 1) * HALF)
                    dve.wait_ge(gate_ready, 2 * i + q + 1)
                    link(V.tensor_tensor(yg[i][0][:, half], yg[i][0][:, half], ple[:, i, half], ALU.mult))
                    V.tensor_tensor(xr[:, i, half], xr[:, i, half], yg[i][0][:, half], ALU.add).then_inc(x3_ready, 1)
                dve.wait_ge(x3_sq, 2 * i + 2)
                V.tensor_tensor(sum4[:, i:i + 1], ssq4[:, i, 0:1], ssq4[:, i, 1:2], ALU.add).then_inc(sum4_ready, 1)
                dve.wait_ge(rms4_ready, i + 1)
                link(V.reciprocal(rstd4[:, i:i + 1], rms4[:, i:i + 1]))
                if i:
                    dve.wait_ge(s_out, 32 * i)
                for q in range(2):
                    half = slice(q * HALF, (q + 1) * HALF)
                    V.scalar_tensor_tensor(out_sb[:, half], xr[:, i, half], rstd4[:, i:i + 1], gfin[:, half], ALU.mult,
                                           ALU.mult).then_inc(res_ready, 1)

            for buf in range(ROW_BUFS):
                dve.wait_ge(s_rows[buf], 16 * ((total + (2 * ROW_BUFS - 1 - buf)) // ROW_BUFS))
            stage6_a(0)
            stage6_split(0)
            stage6_a(1)
            for i in range(NT):
                if i + 1 < NT:
                    stage6_split(i + 1)
                if i + 2 < NT:
                    stage6_a(i + 2)
                stage6_b(i)

        @block.tensor
        def _(pe):
            T = nc.tensor

            def three_pass(o, w, m, chunks, w_of, m_of):
                for k in chunks:
                    T.matmul(o, w_of(w[0], k), m_of(m[0], k), start=(k == 0), stop=False)
                    T.matmul(o, w_of(w[0], k), m_of(m[1], k), start=False, stop=False)
                    last = T.matmul(o, w_of(w[1], k), m_of(m[0], k), start=False, stop=(k == KD - 1))
                return last

            pe.wait_ge(s_const, 16 * 2)
            for i in range(NT):
                pe.wait_ge(xn_ready, i + 1)
                if i >= 2:
                    pe.wait_ge(h_lo, i - 1)
                for k in range(KD):
                    last = T.transpose(b_score[2 * (i % 2) + k // 4][:, (k % 4) * P:(k % 4 + 1) * P],
                                       xn[i % 2][:, k * P:(k + 1) * P], ident)
                last.then_inc(xn_T, 1)
            def unit_part(u, j):
                n = outs_before(u) + j
                pe.wait_ge(hi_done, u + 1)
                pe.wait_ge(lo_done, u + 1)
                if n >= PROJ_BANKS:
                    pe.wait_ge(proj_evac, n - PROJ_BANKS + 1)
                if n < NT:
                    pe.wait_ge(h_hi, n + 1)
                    pe.wait_ge(h_lo, n + 1)
                b = b_proj[n % PROJ_BANKS]
                whl, hhl = (w_hi[u % 2], w_lo[u % 2]), (hT_hi, hT_lo)
                if u // 2 in NATURAL:
                    last = three_pass(b[:, 0:UC], hhl, whl, range(KD),
                                      lambda w, k: w[:, k, j * P:(j + 1) * P], lambda m, k: m[:, k, :])
                else:
                    last = three_pass(b[:], whl, hhl, range(KD),
                                      lambda w, k: w[:, k, j * P:(j + 1) * P], lambda m, k: m[:, k, :])
                last.then_inc(proj_done, 1)

            def scores(h, half):
                pe.wait_ge(proj_evac, outs_before(2 * DKEY + 1 + h // 2))
                for i in (2 * half, 2 * half + 1):
                    s, L = NT * h + i, P * (i + 1)
                    if h and i == 0:
                        pe.wait_ge(wT_ready, NT * h)
                    if s >= 2:
                        pe.wait_ge(score_evac, s - 1)
                    for c in range(2):
                        last = T.matmul(b_score[2 * (i % 2) + c][:, 0:L], dqT[64 * c:64 * c + 64, h, i * P:(i + 1) * P],
                                        dkT[64 * c:64 * c + 64, h, 0:L], start=True, stop=True)
                    last.then_inc(score_done, 1)

            def probs_transpose(h):
                pe.wait_ge(score_evac, NT * (h + 1))
                for i in range(NT):
                    pe.wait_ge(w_ready, NT * h + i + 1)
                    for j in range(i + 1):
                        last = T.transpose(b_score[j][:, i * P:(i + 1) * P], W[i][:, j * P:(j + 1) * P], ident)
                last.then_inc(wT_done, 1)

            def head_product(n):
                if n:
                    pe.wait_ge(o_evac, n)
                h, v = n % HEADS, dv if n < HEADS else rv
                if n < HEADS:
                    pe.wait_ge(wT_ready, NT * (h + 1))
                else:
                    pe.wait_ge(ret_ready, NT * (h + 1))
                    pe.wait_ge(proj_evac, outs_before(2 * RV + 2))
                for i in range(NT):
                    for j in range(i + 1):
                        o = pT_off[j] + (i - j) * P
                        last = T.matmul(b_o[:, i * P:(i + 1) * P], probsT[n % 2][:, o:o + P],
                                        v[:, j, h * P:(h + 1) * P], start=(j == 0), stop=(j == i))
                last.then_inc(o_done, 1)

            def ret_scores(r, n_mix):
                if n_mix:
                    pe.wait_ge(mix_lo, n_mix)
                if r == 0:
                    pe.wait_ge(proj_evac, outs_before(2 * RK + 2))
                    pe.wait_ge(wT_ready, NT * HEADS)
                for j in range(NT):
                    if r:
                        pe.wait_ge(ret_ready, NT * (r - 1) + j + 1)
                    T.matmul(b_score[j][:, 0:SEQ - j * P], rkT[:, r, j * P:(j + 1) * P],
                             rqT[:, r, j * P:SEQ], start=True, stop=True).then_inc(ret_done, 1)

            def mix_transpose(q, n_ret):
                pe.wait_ge(onorm_ready, q + 1)
                pe.wait_ge(ret_ready, NT * n_ret)
                if q >= 4:
                    pe.wait_ge(mix_lo, q - 3)
                for i in range(NT):
                    last = T.transpose(b_score[q % 4][:, i * P:(i + 1) * P], o_of(q)[:, i, :], ident)
                last.then_inc(mixT_done, 1)

            def out_part(m, chunks):
                u, i = IN_UNITS + m // NT, m % NT
                return three_pass(b_proj[(P1_OUTS + m) % PROJ_BANKS][:, 0:UC], (0, 1), (w_hi[u % 2], w_lo[u % 2]), chunks,
                                  lambda part, q: mix_of(part, q)[:, i * P:(i + 1) * P],
                                  lambda t, q: t[:, MIX_ROWS[q], :])

            def opening(m):
                if m == 0:
                    pe.wait_ge(hi_done, IN_UNITS + 1)
                    pe.wait_ge(lo_done, IN_UNITS + 1)
                    pe.wait_ge(mix_lo, HEADS)
                pe.wait_ge(proj_evac, P1_OUTS - PROJ_BANKS + m + 1)
                out_part(m, range(HEADS))

            n_ret = n_mix = 0
            for step, n, *j in schedule():
                if step == "out":
                    unit_part(n, *j)
                elif step == "scores" and n < HEADS:
                    scores(n, *j)
                elif step == "scores":
                    ret_scores(n - HEADS, n_mix)
                    n_ret += 1
                elif step == "weights":
                    probs_transpose(n)
                elif step == "product":
                    head_product(n)
                elif step == "mixT":
                    mix_transpose(n, n_ret)
                    n_mix += 1
                elif step == "opening":
                    opening(n)

            def x1_transpose(m):
                u, i = m // NT, m % NT
                pe.wait_ge(x1_add, m + 1)
                if m >= 4:
                    pe.wait_ge(x1T_ready, m - 3)
                for c in range(2):
                    k = 2 * u + c
                    last = T.transpose(b_score[m % 4][:, c * P:(c + 1) * P], xr[:, i, k * P:(k + 1) * P], ident)
                last.then_inc(x1_T, 1)

            def logits(m):
                u, i = m // NT, m % NT
                if m == 0:
                    pe.wait_ge(wr_ready, 1)
                    pe.wait_ge(o_evac, 2 * HEADS)
                pe.wait_ge(x1T_ready, m + 1)
                for c in range(2):
                    last = T.matmul(b_o[:, i * NR:(i + 1) * NR], x1T[m % 2][:, c, :], w_r[:, 2 * u + c, :],
                                    start=(m == 0 and c == 0), stop=(m == NT * OUT_UNITS - 1 and c == 1))
                last.then_inc(lg_done, 1)

            for m in range(NT * OUT_UNITS):
                u = IN_UNITS + m // NT
                pe.wait_ge(hi_done, u + 1)
                pe.wait_ge(lo_done, u + 1)
                if m == 0:
                    pe.wait_ge(mix_lo, 2 * HEADS)
                if m < PROJ_BANKS:
                    out_part(m, range(HEADS, KD)).then_inc(proj_done, 1)
                else:
                    pe.wait_ge(x1_add, m - PROJ_BANKS + 1)
                    out_part(m, range(KD)).then_inc(proj_done, 1)
                if m >= 1:
                    x1_transpose(m - 1)
                if m >= 2:
                    logits(m - 2)
            x1_transpose(NT * OUT_UNITS - 1)
            logits(NT * OUT_UNITS - 2)
            logits(NT * OUT_UNITS - 1)
            pe.wait_ge(s_pple, 32)
            for c in range(D_PLE // P):
                for t in range(NT):
                    last = T.transpose(b_score[c][:, t * P:(t + 1) * P], p_sb[:, t, c * P:(c + 1) * P], ident)
                last.then_inc(p_T, 1)

            def ple_product(n):
                t, q = n // 2, n % 2
                if n >= 4:
                    pe.wait_ge(ple_ready, n - 3)
                else:
                    pe.wait_ge(x1_add, NT * OUT_UNITS)
                    pe.wait_ge(x1T_ready, NT * OUT_UNITS)
                for c in range(D_PLE // P):
                    last = T.matmul(b_ple[n % 4][:], pT[:, c, t * P:(t + 1) * P], ple_proj[:, c, q * 512:(q + 1) * 512],
                                    start=(c == 0), stop=(c == D_PLE // P - 1))
                last.then_inc(ple_done, 1)

            pe.wait_ge(pT_ready, 2)
            for n in range(3):
                ple_product(n)
            pe.wait_ge(member_ready, 1)
            T.matmul(b_rank[:, 0:80], ones[:], prefix[:].rearrange("p i e -> p (i e)"), start=True, stop=False)
            T.matmul(b_rank[:, 0:64], tri, member[:].rearrange("p i e -> p (i e)"), start=False, stop=True).then_inc(rank_done, 1)
            for n in range(3, 7):
                ple_product(n)
            pe.wait_ge(slot_oh_ready, 1)
            for n in range(2 * NT):
                last = T.matmul(b_rank[:, P:P + 2 * TABLE], slot_oh[:, n, :], blk_rows[:, n].rearrange("p w b -> p (w b)"),
                                start=(n == 0), stop=(n == 2 * NT - 1))
            last.then_inc(rows_done, 1)
            ple_product(7)

            pe.wait_ge(table_ready, 1)
            total = pe.value_load(cum_i[0:1, N_EXPERTS - 1:N_EXPERTS], min_val=N_EXPERTS, max_val=MAX_BLOCKS)

            def in_slot(b, products):
                loads = pe.value_load(blk_loads[0:1, bass.ds(b, 1)], min_val=1, max_val=6)
                slot = pe.value_load(blk_slot[0:1, bass.ds(b, 1)], min_val=0, max_val=RING - 1)
                with pe.If(slot < 1):
                    products(0, loads)
                with pe.Else():
                    with pe.If(slot < 2):
                        products(1, loads)
                    with pe.Else():
                        products(2, loads)

            def rows_transpose(b, buf, loads):
                pe.wait_ge(s_rows[buf], 16 * loads)
                for j in range(4):
                    last = T.transpose(b_xT[:, j * P:(j + 1) * P], rows[buf][:, j * P:(j + 1) * P], ident)
                last.then_inc(xT_done, 1)

            def gate_up(b):
                def products(s, loads):
                    pe.wait_ge(xT_ready, b + 1)
                    for k in range(KD):
                        if k % (KD // 2) == 0:
                            pe.wait_ge(s_gu[s][k // (KD // 2)], 32 * loads)
                        for q in range(2):
                            last = T.matmul(b_gu[q * BLK:(q + 1) * BLK, :], rowsT[:, k % 4, k // 4, :],
                                            ring_gu[s][:, k, :, q * UC:(q + 1) * UC],
                                            start=(k == 0), stop=(k == KD - 1))
                        if k == KD // 2 - 1:
                            last.then_inc(gu_half_done, 1)
                    last.then_inc(gu_done, 1)

                in_slot(b, products)

            def hidden_transpose(b):
                pe.wait_ge(hid_ready, b + 1)
                for j in range(2):
                    last = T.transpose(b_hT[:, j * P:(j + 1) * P], hid[:, j * P:(j + 1) * P], ident)
                last.then_inc(hT_done, 1)

            def down(b):
                def products(s, loads):
                    pe.wait_ge(hidT_ready, b + 1)
                    pe.wait_ge(y_ready, b + 1)
                    pe.wait_ge(s_dn[s], 16 * loads)
                    for kf in range(D_EXPERT // P):
                        for q in range(2):
                            last = T.matmul(b_dn[q * BLK:(q + 1) * BLK, :], hidT[:, kf % 2, kf // 2, :],
                                            ring_dn[s][:, kf, q * (D // 2):(q + 1) * (D // 2)],
                                            start=(kf == 0), stop=(kf == D_EXPERT // P - 1))
                    last.then_inc(dn_done, 1)

                in_slot(b, products)

            rows_transpose(0, 0, 1)
            pe.wait_ge(ple_ready, 2 * NT)
            gate_up(0)
            rows_transpose(1, 1, 1)

            def step(b, k, turn):
                hidden_transpose(b - 1)
                gate_up(b)
                rows_transpose(b + 1, (2 + k) % ROW_BUFS, GROUP // ROW_BUFS * turn + ((2 + k) // ROW_BUFS + 1))
                down(b - 1)

            over_blocks(pe, total, step)
            hidden_transpose(total - 1)
            down(total - 1)

            def x2_transpose(i):
                pe.wait_ge(x2_ready, i + 1)
                if i >= 2:
                    pe.wait_ge(x2_lo, i - 1)
                for k in range(KD):
                    last = T.transpose(b_score[2 * (i % 2) + k // 4][:, (k % 4) * P:(k % 4 + 1) * P],
                                       xr[:, i, k * P:(k + 1) * P], ident)
                last.then_inc(x2_T, 1)

            x2_transpose(0)
            for i in range(NT):
                pe.wait_ge(x2_hi, i + 1)
                pe.wait_ge(x2_lo, i + 1)
                for q in range(2):
                    pe.wait_ge(pg_lo, KD * (q + 1))
                    if i >= 2:
                        pe.wait_ge(gate_ready, 2 * (i - 2) + q + 1)
                    three_pass(b_gate[i % 2][q][:], (x2T_hi[i % 2], x2T_lo[i % 2]), (ple_hi[q], ple_lo[q]), range(KD),
                               lambda w, k: w[:, k, :], lambda m, k: m[:, k, :]).then_inc(gate_done, 1)
                    if q == 0 and i + 1 < NT:
                        x2_transpose(i + 1)


_INS = ["x", "p", "norm_mix", "w_in", "lam_q1", "lam_k1", "lam_q2", "lam_k2", "diff_subln", "w_out", "norm_ffn",
        "w_router_group", "b_router_group", "w_router_expert", "b_router_expert", "w_gate", "w_up", "w_down",
        "norm_ple", "w_ple_gate", "w_ple_proj", "norm_final"]
_LEADING = {"x": 1, "p": 2, "norm_final": 0}


def kernel(**inputs):
    import concourse.bacc as bacc
    from concourse.bass_utils import run_bass_kernel_spmd

    nc = bacc.Bacc("TRN2", target_bir_lowering=False, num_devices=1)
    arrays, args = {}, []
    for name in _INS:
        a = np.ascontiguousarray(inputs[name])
        a = a.reshape(a.shape[_LEADING.get(name, 1):])
        arrays[f"in_{name}"] = a
        args.append(nc.dram_tensor(f"in_{name}", a.shape, mybir.dt.from_np(a.dtype), kind="ExternalInput").ap())
    for name, a in zip(("decay", "bias", "small"), shape_constants()):
        arrays[f"const_{name}"] = a
        args.append(nc.dram_tensor(f"const_{name}", a.shape, F32, kind="ExternalInput").ap())
    args.append(nc.dram_tensor("out", (SEQ, D), F32, kind="ExternalOutput").ap())
    trunk(nc, *args)
    r = run_bass_kernel_spmd(nc, [arrays], core_ids=[0])
    return r.results[0]["out"].reshape(1, SEQ, D)
```
